# Optimizing a Trainium2 kernel written in Bass

```python
import jax, jax.numpy as jnp
from jax import lax
import numpy as np

D_MODEL = 1024
BATCH = 1
SEQ = 256
DEPTH = 4

CTX_LEN = 256
GRID_W = 64
N_MIXERS = 3
EPS = 1e-6

NA_HEADS = 16
NA_HEAD_DIM = D_MODEL // NA_HEADS
NA_KH = 8
NA_KW = 16
NA_SCALE = NA_HEAD_DIM ** -0.5

RET_HEADS = 4
RET_QK_DIM = D_MODEL // RET_HEADS
RET_V_DIM = 2 * D_MODEL // RET_HEADS
RET_CHUNK = 128
ROPE_BASE = 10000.0

CONV_WIDTH = 31

FFN_HIDDEN = 2816
FFN_CONV_WIDTH = 3

N_NA_LAYERS = (DEPTH + 2) // 3
N_RET_LAYERS = (DEPTH + 1) // 3
N_CONV_LAYERS = DEPTH // 3

kernel_name = 'hybrid_na_retnet_conformer_dit'

F32 = jnp.float32

def rms_norm(x, gain):
    x32 = x.astype(F32)
    y = x32 * lax.rsqrt(jnp.mean(x32 * x32, axis=-1, keepdims=True) + EPS)
    return (y * gain.astype(F32)).astype(x.dtype)

def modulate_norm(x, gain, shift, scale):
    return rms_norm(x, gain) * (1 + scale) + shift

def layer_norm(x, gain, bias):
    x32 = x.astype(F32)
    mu = jnp.mean(x32, axis=-1, keepdims=True)
    xc = x32 - mu
    var = jnp.mean(xc * xc, axis=-1, keepdims=True)
    return (xc * lax.rsqrt(var + EPS) * gain.astype(F32) + bias.astype(F32)).astype(x.dtype)

def split_heads(x, n_heads):
    b, n, _ = x.shape
    return x.reshape(b, n, n_heads, -1).transpose(0, 2, 1, 3)

def merge_heads(x):
    b, h, n, d = x.shape
    return x.transpose(0, 2, 1, 3).reshape(b, n, h * d)

def depthwise_conv(x, w, b):
    y = lax.conv_general_dilated(x, w[:, None, :], window_strides=(1,), padding='SAME',
                                 dimension_numbers=('NWC', 'WIO', 'NWC'),
                                 feature_group_count=x.shape[-1])
    return y + b

def axial_rope_tables(n, dim):
    t = jnp.arange(n)
    row = (t // GRID_W).astype(F32)
    col = (t % GRID_W).astype(F32)
    n_freq = dim // 4
    inv_freq = jnp.power(ROPE_BASE, -jnp.arange(n_freq, dtype=F32) / n_freq)
    ang = jnp.concatenate([row[:, None] * inv_freq, col[:, None] * inv_freq], axis=-1)
    return jnp.cos(ang), jnp.sin(ang)

def apply_rope(x, cos, sin):
    half = x.shape[-1] // 2
    x1 = x[..., :half].astype(F32)
    x2 = x[..., half:].astype(F32)
    return jnp.concatenate([x1 * cos - x2 * sin, x1 * sin + x2 * cos], axis=-1).astype(x.dtype)

def head_rms_norm(x, gain):
    x32 = x.astype(F32)
    y = x32 * lax.rsqrt(jnp.mean(x32 * x32, axis=-1, keepdims=True) + EPS)
    return (y * gain.astype(F32)).astype(x.dtype)

def na_mixer(hx, hc, w_qkv, w_o, q_gain, k_gain, rpb, need_ctx):
    b, n, _ = hx.shape
    rows = n // GRID_W
    kh = min(NA_KH, rows)
    nb = kh * NA_KW

    def qkv(h):
        q, k, v = jnp.split(h @ w_qkv, 3, axis=-1)
        q = head_rms_norm(split_heads(q, NA_HEADS), q_gain)
        k = head_rms_norm(split_heads(k, NA_HEADS), k_gain)
        return q, k, split_heads(v, NA_HEADS)

    qx, kx, vx = qkv(hx)
    qc, kc, vc = qkv(hc)

    r = jnp.arange(rows)
    col = jnp.arange(GRID_W)
    row_start = jnp.clip(r - kh // 2, 0, rows - kh)
    col_start = jnp.clip(col - NA_KW // 2, 0, GRID_W - NA_KW)
    key_r = row_start[:, None] + jnp.arange(kh)
    key_c = col_start[:, None] + jnp.arange(NA_KW)
    nb_idx = (key_r[:, None, :, None] * GRID_W + key_c[None, :, None, :]).reshape(rows, GRID_W, nb)
    rel_r = key_r - r[:, None] + (NA_KH - 1)
    rel_c = key_c - col[:, None] + (NA_KW - 1)
    bias = rpb[:, rel_r[:, None, :, None], rel_c[None, :, None, :]]
    bias = jnp.moveaxis(bias.reshape(NA_HEADS, rows, GRID_W, nb), 0, 1)
    q_rows = jnp.moveaxis(qx.reshape(b, NA_HEADS, rows, GRID_W, NA_HEAD_DIM), 2, 0)

    def row_block(args):
        q_r, idx_r, bias_r = args
        k_nb = jnp.take(kx, idx_r, axis=2)
        v_nb = jnp.take(vx, idx_r, axis=2)
        s_nb = jnp.einsum('bhqd,bhqkd->bhqk', q_r, k_nb) * NA_SCALE + bias_r
        s_ctx = jnp.einsum('bhqd,bhkd->bhqk', q_r, kc) * NA_SCALE
        p = jax.nn.softmax(jnp.concatenate([s_nb, s_ctx], axis=-1).astype(F32), axis=-1).astype(v_nb.dtype)
        return (jnp.einsum('bhqk,bhqkd->bhqd', p[..., :nb], v_nb)
                + jnp.einsum('bhqk,bhkd->bhqd', p[..., nb:], vc))

    o = lax.map(row_block, (q_rows, nb_idx, bias))
    o = jnp.moveaxis(o, 0, 2).reshape(b, NA_HEADS, n, NA_HEAD_DIM)
    yx = merge_heads(o) @ w_o
    if not need_ctx:
        return yx, None
    s = jnp.einsum('bhqd,bhkd->bhqk', qc, kc) * NA_SCALE
    p = jax.nn.softmax(s.astype(F32), axis=-1).astype(vc.dtype)
    yc = merge_heads(jnp.einsum('bhqk,bhkd->bhqd', p, vc)) @ w_o
    return yx, yc

def retention_scan(q, k, v, log_gamma, state):
    b, h, n, _ = q.shape
    dv = v.shape[-1]
    nc = n // RET_CHUNK

    def chunks(t):
        return jnp.moveaxis(t.reshape(b, h, nc, RET_CHUNK, t.shape[-1]), 2, 0)

    pos = jnp.arange(RET_CHUNK, dtype=F32)
    lg = log_gamma.astype(F32)[:, None, None]
    diff = pos[:, None] - pos[None, :]
    intra = jnp.where(diff >= 0, jnp.exp(jnp.maximum(diff, 0.0)[None] * lg), 0.0)
    q_decay = jnp.exp((pos + 1.0)[None, :, None] * lg)
    k_decay = jnp.exp((RET_CHUNK - 1.0 - pos)[None, :, None] * lg)
    chunk_decay = jnp.exp(RET_CHUNK * lg)

    def step(s, inp):
        qc, kc, vc = inp
        v32 = vc.astype(F32)
        scores = jnp.einsum('bhid,bhjd->bhij', qc, kc).astype(F32) * intra
        out = (jnp.einsum('bhij,bhjv->bhiv', scores, v32)
               + jnp.einsum('bhid,bhdv->bhiv', qc.astype(F32) * q_decay, s))
        s = s * chunk_decay + jnp.einsum('bhjd,bhjv->bhdv', kc.astype(F32) * k_decay, v32)
        return s, out

    state, out = lax.scan(step, state, (chunks(q), chunks(k), chunks(v)))
    return jnp.moveaxis(out, 0, 2).reshape(b, h, n, dv), state

def retention_mixer(hx, hc, w_q, w_k, w_v, w_g, w_o, gn_gain, decay_logit, cos, sin, need_ctx):
    b = hx.shape[0]
    k_scale = RET_QK_DIM ** -0.5
    qx = apply_rope(split_heads(hx @ w_q, RET_HEADS), cos, sin)
    kx = apply_rope(split_heads(hx @ w_k, RET_HEADS), cos, sin) * k_scale
    vx = split_heads(hx @ w_v, RET_HEADS)
    qc = split_heads(hc @ w_q, RET_HEADS)
    kc = split_heads(hc @ w_k, RET_HEADS) * k_scale
    vc = split_heads(hc @ w_v, RET_HEADS)
    log_gamma = jax.nn.log_sigmoid(decay_logit.astype(F32))
    zero = jnp.zeros((b, RET_HEADS, RET_QK_DIM, RET_V_DIM), F32)

    def flip(t):
        return jnp.flip(t, axis=2)

    oc_f, sc_f = retention_scan(qc, kc, vc, log_gamma[0], zero)
    ox_f, _ = retention_scan(qx, kx, vx, log_gamma[0], sc_f)
    oc_b, sc_b = retention_scan(flip(qc), flip(kc), flip(vc), log_gamma[1], zero)
    ox_b, _ = retention_scan(flip(qx), flip(kx), flip(vx), log_gamma[1], sc_b)

    def finish(h, o):
        mu = jnp.mean(o, axis=-1, keepdims=True)
        oc_ = o - mu
        o = oc_ * lax.rsqrt(jnp.mean(oc_ * oc_, axis=-1, keepdims=True) + EPS)
        o = (merge_heads(o) * gn_gain.astype(F32)).astype(h.dtype)
        return (jax.nn.silu(h @ w_g) * o) @ w_o

    yx = finish(hx, ox_f + flip(ox_b))
    if not need_ctx:
        return yx, None
    return yx, finish(hc, oc_f + flip(oc_b))

def conv_mixer(hx, hc, w_pw1, b_pw1, w_dw, b_dw, ln_g, ln_b, w_pw2, b_pw2, need_ctx):
    def one(h):
        a, g = jnp.split(h @ w_pw1 + b_pw1, 2, axis=-1)
        u = a * jax.nn.sigmoid(g)
        u = depthwise_conv(u, w_dw, b_dw)
        u = jax.nn.silu(layer_norm(u, ln_g, ln_b))
        return u @ w_pw2 + b_pw2
    yx = one(hx)
    if not need_ctx:
        return yx, None
    return yx, one(hc)

def conv_ffn(h, w_up, w_dw, b_dw, w_down):
    u, v = jnp.split(h @ w_up, 2, axis=-1)
    u = jax.nn.gelu(depthwise_conv(u, w_dw, b_dw))
    return (u * v) @ w_down

def setup_inputs(seed: int = 0) -> dict:
    key = jax.random.key(seed)
    ks = iter(jax.random.split(key, 48))
    D = D_MODEL

    def nrm(shape, scale):
        return jax.random.normal(next(ks), shape, F32) * scale

    base_logit = jnp.log(jnp.power(2.0, 5.0 + jnp.arange(RET_HEADS, dtype=F32)) - 1.0)
    return {
        'x': nrm((BATCH, SEQ, D), 1.0),
        'c': nrm((BATCH, D), 1.0),
        'ctx': nrm((BATCH, CTX_LEN, D), 1.0),
        'c_ctx': nrm((D,), 1.0),
        'ada_w': nrm((DEPTH, D, 6 * D), D ** -0.5),
        'ada_b': nrm((DEPTH, 6 * D), 0.02),
        'norm_mix': 1.0 + nrm((DEPTH, D), 0.1),
        'norm_ffn': 1.0 + nrm((DEPTH, D), 0.1),
        'na_w_qkv': nrm((N_NA_LAYERS, D, 3 * D), D ** -0.5),
        'na_w_o': nrm((N_NA_LAYERS, D, D), D ** -0.5),
        'na_q_gain': 1.0 + nrm((N_NA_LAYERS, NA_HEAD_DIM), 0.1),
        'na_k_gain': 1.0 + nrm((N_NA_LAYERS, NA_HEAD_DIM), 0.1),
        'na_rpb': nrm((N_NA_LAYERS, NA_HEADS, 2 * NA_KH - 1, 2 * NA_KW - 1), 0.1),
        'ret_w_q': nrm((N_RET_LAYERS, D, RET_HEADS * RET_QK_DIM), D ** -0.5),
        'ret_w_k': nrm((N_RET_LAYERS, D, RET_HEADS * RET_QK_DIM), D ** -0.5),
        'ret_w_v': nrm((N_RET_LAYERS, D, RET_HEADS * RET_V_DIM), D ** -0.5),
        'ret_w_g': nrm((N_RET_LAYERS, D, RET_HEADS * RET_V_DIM), D ** -0.5),
        'ret_w_o': nrm((N_RET_LAYERS, RET_HEADS * RET_V_DIM, D), (RET_HEADS * RET_V_DIM) ** -0.5),
        'ret_gn_gain': 1.0 + nrm((N_RET_LAYERS, RET_HEADS * RET_V_DIM), 0.1),
        'ret_decay_logit': base_logit + nrm((N_RET_LAYERS, 2, RET_HEADS), 0.1),
        'cv_w_pw1': nrm((N_CONV_LAYERS, D, 2 * D), D ** -0.5),
        'cv_b_pw1': nrm((N_CONV_LAYERS, 2 * D), 0.02),
        'cv_w_dw': nrm((N_CONV_LAYERS, CONV_WIDTH, D), CONV_WIDTH ** -0.5),
        'cv_b_dw': nrm((N_CONV_LAYERS, D), 0.02),
        'cv_ln_g': 1.0 + nrm((N_CONV_LAYERS, D), 0.1),
        'cv_ln_b': nrm((N_CONV_LAYERS, D), 0.02),
        'cv_w_pw2': nrm((N_CONV_LAYERS, D, D), D ** -0.5),
        'cv_b_pw2': nrm((N_CONV_LAYERS, D), 0.02),
        'ffn_w_up': nrm((DEPTH, D, 2 * FFN_HIDDEN), D ** -0.5),
        'ffn_w_dw': nrm((DEPTH, FFN_CONV_WIDTH, FFN_HIDDEN), FFN_CONV_WIDTH ** -0.5),
        'ffn_b_dw': nrm((DEPTH, FFN_HIDDEN), 0.02),
        'ffn_w_down': nrm((DEPTH, FFN_HIDDEN, D), FFN_HIDDEN ** -0.5),
    }

def reference(x, c, ctx, c_ctx, ada_w, ada_b, norm_mix, norm_ffn,
              na_w_qkv, na_w_o, na_q_gain, na_k_gain, na_rpb,
              ret_w_q, ret_w_k, ret_w_v, ret_w_g, ret_w_o, ret_gn_gain, ret_decay_logit,
              cv_w_pw1, cv_b_pw1, cv_w_dw, cv_b_dw, cv_ln_g, cv_ln_b, cv_w_pw2, cv_b_pw2,
              ffn_w_up, ffn_w_dw, ffn_b_dw, ffn_w_down):
    n = x.shape[1]
    cos, sin = axial_rope_tables(n, RET_QK_DIM)
    silu_c = jax.nn.silu(c)
    silu_cc = jax.nn.silu(c_ctx)[None, :]
    xs, cs = x, ctx
    for i in range(DEPTH):
        need_ctx = i < DEPTH - 1
        mx = jnp.split((silu_c @ ada_w[i] + ada_b[i])[:, None, :], 6, axis=-1)
        mc = jnp.split((silu_cc @ ada_w[i] + ada_b[i])[:, None, :], 6, axis=-1)
        hx = modulate_norm(xs, norm_mix[i], mx[0], mx[1])
        hc = modulate_norm(cs, norm_mix[i], mc[0], mc[1])
        kind, j = i % N_MIXERS, i // N_MIXERS
        if kind == 0:
            yx, yc = na_mixer(hx, hc, na_w_qkv[j], na_w_o[j], na_q_gain[j], na_k_gain[j], na_rpb[j], need_ctx)
        elif kind == 1:
            yx, yc = retention_mixer(hx, hc, ret_w_q[j], ret_w_k[j], ret_w_v[j], ret_w_g[j], ret_w_o[j],
                                     ret_gn_gain[j], ret_decay_logit[j], cos, sin, need_ctx)
        else:
            yx, yc = conv_mixer(hx, hc, cv_w_pw1[j], cv_b_pw1[j], cv_w_dw[j], cv_b_dw[j],
                                cv_ln_g[j], cv_ln_b[j], cv_w_pw2[j], cv_b_pw2[j], need_ctx)
        xs = xs + mx[2] * yx
        hx = modulate_norm(xs, norm_ffn[i], mx[3], mx[4])
        xs = xs + mx[5] * conv_ffn(hx, ffn_w_up[i], ffn_w_dw[i], ffn_b_dw[i], ffn_w_down[i])
        if need_ctx:
            cs = cs + mc[2] * yc
            hc = modulate_norm(cs, norm_ffn[i], mc[3], mc[4])
            cs = cs + mc[5] * conv_ffn(hc, ffn_w_up[i], ffn_w_dw[i], ffn_b_dw[i], ffn_w_down[i])
    return xs


_drawn_inputs = setup_inputs


def setup_inputs(seed=0):
    import zlib

    import numpy as np

    out = dict(_drawn_inputs(seed))
    spreads = {}
    factors = {'na_q_gain': 4.091,
     'na_k_gain': 4.361,
     'na_rpb': 8.0,
     'cv_b_pw1': 8.0,
     'cv_b_dw': 8.0,
     'cv_ln_b': 8.0,
     'cv_b_pw2': 6.909,
     'ffn_b_dw': 3.375}
    for name, (base, spread) in spreads.items():
        noise = np.random.default_rng([zlib.crc32(name.encode()), seed]).standard_normal(out[name].shape)
        drawn = base * np.exp(spread * noise) if base else spread * noise
        out[name] = __import__('jax').numpy.asarray(drawn.astype(out[name].dtype))
    for name, factor in factors.items():
        out[name] = (out[name] * factor).astype(out[name].dtype)
    return out
```

```python
from contextlib import ExitStack

import numpy as np

import concourse.bass as bass
from concourse import mybir

F32 = mybir.dt.float32
F32R = mybir.dt.float32r
ALU = mybir.AluOpType
ACT = mybir.ActivationFunctionType
AX = mybir.AxisListType.X

P = 128
D = 1024
C = D // P
CTX = 256
SEQ = 256
T = CTX + SEQ
TB = T // P
DEPTH = 4
GRID_W = 64
EPS = 1e-6
ALL = slice(0, T)
CT = slice(0, CTX)
XT = slice(CTX, T)

NA_HEADS = 16
NA_HD = D // NA_HEADS
NA_KH = 8
NA_KW = 16
RPB_H = 2 * NA_KH - 1
RPB_W = 2 * NA_KW - 1
ROWS = SEQ // GRID_W

RET_HEADS = 4
RET_QK = D // RET_HEADS
RET_V = 2 * D // RET_HEADS
RET_VC = 2 * D // P
DIST_W = 5 * P

CONV_W = 31
FFN_H = 2816
FC = FFN_H // P
DOWN = (8, 8, 6)

SLOTS = 4
LEAD = 3
GROUP = 8 * P
ADA_SLICES = 6 * D // 512
FAR = 1e30


class Step:

    def __init__(self, first, per=0, i=0):
        self.first, self.per, self.i = first, per, i
        self.slot = first % SLOTS
        self.n = first + per * i
        self.lap = first // SLOTS + (per // SLOTS) * i

    def ahead(self, k):
        return Step(self.first + k, self.per, self.i)


def plan():
    group, tile, ready = 4 * 4, 0, 0
    layers = []
    for layer in range(DEPTH):
        p = {"mix": group, "mix_tile": tile, "mix_ready": ready}
        ready += C
        if layer % 3 == 0:
            p["qk_per"] = 12 if layer == 0 else 4
            p["v"] = group + 4 * p["qk_per"]
            p["o"] = p["v"] + 8
            p["o_ready"] = ready
            ready += C
            group, tile = p["o"] + 8, tile + 32
        elif layer % 3 == 1:
            p["v"] = group + 16
            p["g"] = p["v"] + 16
            p["o"] = p["g"] + 16
            group, tile = p["o"] + 16, tile + 56
        else:
            p["o"] = group + 16
            p["o_ready"] = ready
            ready += C
            group, tile = p["o"] + 8, tile + 24
        p["ffn_ready"] = ready
        ready += C
        p["ada"] = group if layer < DEPTH - 1 else None
        p["up"] = group + (4 if layer < DEPTH - 1 else 0)
        p["up_per"] = 8 if layer < DEPTH - 1 else 4
        p["up_tile"] = tile
        p["down"] = p["up"] + FC // 2 * p["up_per"]
        p["down_tile"] = tile + 2 * FC
        group, tile = p["down"] + C * len(DOWN), tile + 2 * FC + C
        layers.append(p)
    return layers, group


def bodies(engine, count, unroll=False):
    if unroll:
        yield from range(count)
    else:
        with engine.Fori(0, count) as i:
            yield i


def build(nc, x, weights, ada_in, ada_bias, gain, na_gain, rpb, na_mask, rope, decay, dist, gn_gain,
          cv_bias, cv_filter, ffn_filter, ones, head_ones, identity, pick, out):
    layers, n_groups = plan()
    ctx = ExitStack()
    with ctx:
        def sb(name, shape, dt=F32):
            return ctx.enter_context(nc.sbuf_tensor(name, shape, dt))

        def sem(name):
            return ctx.enter_context(nc.semaphore(name))

        X = sb("X", [P, C, T])
        Hhi = sb("Hhi", [P, C, T], F32R)
        Hlo = sb("Hlo", [P, C, T], F32R)
        Whi = sb("Whi", [P, SLOTS, GROUP], F32R)
        with nc.sbuf_tensor("raw", [P, SLOTS, GROUP], F32) as raw:
            pass
        Wlo = sb("Wlo", [P, SLOTS, GROUP], F32R)
        hb = sb("hb", [P, 2, T])
        total = sb("total", [P, T])
        square = sb("square", [P, 2, T])
        root = sb("root", [P, T])
        rstd = sb("rstd", [P, T])
        rows = sb("rows", [4, 512])
        mod = sb("mod", [P, 2, 6 * C, 2])
        scale = sb("scale", [P, 2, C, 2])
        cfull = sb("cfull", [P, C, 2])
        csilu = sb("csilu", [P, C, 2])
        cparts = sb("cparts", [P, C, 4], F32R)
        bias_ada = sb("bias_ada", [P, DEPTH, 6 * C])
        gains = sb("gains", [P, DEPTH, 2, C])
        qk_gain = sb("qk_gain", [P, 2, 2])
        mask = sb("mask", [P, GRID_W])
        cos_sin = sb("cos_sin", [P, 2, SEQ])
        logit = sb("logit", [P, 2 * RET_HEADS])
        small = sb("small", [P, 3, 2 * RET_HEADS])
        log_gamma = sb("log_gamma", [P, 2 * RET_HEADS])
        gn = sb("gn", [P, RET_VC])
        cvb = sb("cvb", [P, 6, C])
        cvf = sb("cvf", [P, C, CONV_W])
        fff = sb("fff", [P, DEPTH, FC, 4])
        one = sb("one", [P, P])
        one_head = sb("one_head", [P, P])
        ident = sb("ident", [P, P])
        picker = sb("picker", [4, 2])
        eps = sb("eps", [P, 1])
        peak = sb("peak", [P, 4])
        psum_p = sb("psum_p", [P, 4])
        rinv = sb("rinv", [P, 4])
        stats = sb("stats", [P, TB, 6])
        mv = sb("mv", [P, TB, 2])
        sd4 = sb("sd4", [P, TB])

        def region(*tensors):
            with ExitStack() as stack:
                return [stack.enter_context(nc.sbuf_tensor(n, s, dt)) for n, s, dt in tensors]

        Ghi, Glo, cv = region(("Ghi", [P, FC, T], F32R), ("Glo", [P, FC, T], F32R), ("cv", [P, 2, T], F32))
        QK, V, O, rel, prob, probT, Qz = region(
            ("QK", [P, 2 * C, T], F32), ("V", [P, TB, D], F32), ("O", [P, TB, D], F32),
            ("rel", [P, NA_HEADS, 6, GRID_W], F32), ("prob", [P, 2, T], F32), ("probT", [P, 2, T], F32),
            ("Qz", [P, 2, T], F32))
        _, rel_in = region(("na_qk", [P, 2 * C * T], F32), ("rel_in", [P, NA_HEADS * 6, GRID_W], F32))
        _, na_sq, na_root = region(("na_skip", [P, 2 * C * T + 2 * TB * D + NA_HEADS * 6 * GRID_W], F32),
                                   ("na_sq", [P, 2, T], F32), ("na_root", [P, 4, T], F32))
        QKr, Vr, On, decay_t = region(
            ("QKr", [P, 2 * C, T], F32), ("Vr", [P, TB, 2 * D], F32), ("On", [P, TB, 2 * D], F32),
            ("decay_t", [P, 2, DIST_W], F32))
        OT, Yhi, Ylo = region(("OT", [P, RET_VC, T], F32), ("Yhi", [P, RET_VC, T], F32R),
                              ("Ylo", [P, RET_VC, T], F32R))
        _, rope_t = region(("ret_skip", [P, 2 * C * T + 2 * TB * 2 * D], F32), ("rope_t", [P, 4, SEQ], F32))
        A = [hb[:, 0, :], square[:, 0, :], square[:, 1, :]]
        gated = [hb[:, 0, :], hb[:, 1, :], square[:, 0, :], square[:, 1, :]]
        U, conv2, Wc, glu_s = region(("U", [P, 2, T], F32), ("conv2", [P, 2, T], F32),
                                     ("Wc", [P, C, T], F32), ("glu_s", [P, 2, T], F32))
        bank = [ctx.enter_context(nc.psum_tensor(f"bank{b}", [P, 512], F32)) for b in range(8)]

        raw_loaded = [sem(f"raw_loaded{s}") for s in range(SLOTS)]
        const_loaded = sem("const_loaded")
        x_loaded = sem("x_loaded")
        hi_split = sem("hi_split")
        lo_split = sem("lo_split")
        weights_used = sem("weights_used")
        tile_free = sem("tile_free")
        c_ready = sem("c_ready")
        lg_step = sem("lg_step")
        rows_copied = sem("rows_copied")
        cols_made = sem("cols_made")
        mod_ready = sem("mod_ready")
        sum_step = sem("sum_step")
        norm_summed = sem("norm_summed")
        norm_root = sem("norm_root")
        norm_rstd = sem("norm_rstd")
        norm_scaled = sem("norm_scaled")
        norm_x = sem("norm_x")
        norm_ctx = sem("norm_ctx")
        h_hi = sem("h_hi")
        h_ready = sem("h_ready")
        qk_squared = sem("qk_squared")
        qk_summed = sem("qk_summed")
        qk_root = sem("qk_root")
        qk_rstd = sem("qk_rstd")
        rel_loaded = sem("rel_loaded")
        rel_ready = sem("rel_ready")
        qz_cleared = sem("qz_cleared")
        q_staged = sem("q_staged")
        scored = sem("scored")
        biased = sem("biased")
        peaked = sem("peaked")
        exped = sem("exped")
        p_turned = sem("p_turned")
        p_copied = sem("p_copied")
        attended = sem("attended")
        inverted = sem("inverted")
        o_stored = sem("o_stored")
        o_turned = sem("o_turned")
        rope_step = sem("rope_step")
        dist_loaded = sem("dist_loaded")
        decayed = sem("decayed")
        mask_made = sem("mask_made")
        ret_scored = sem("ret_scored")
        weighted = sem("weighted")
        ret_out = sem("ret_out")
        gn_stat = sem("gn_stat")
        gn_root = sem("gn_root")
        gn_rstd = sem("gn_rstd")
        gn_done = sem("gn_done")
        gn_turned = sem("gn_turned")
        ot_copied = sem("ot_copied")
        gate_silu = sem("gate_silu")
        y_made = sem("y_made")
        y_hi = sem("y_hi")
        glu_sigmoid = sem("glu_sigmoid")
        glu_made = sem("glu_made")
        tap_done = sem("tap_done")
        ln_sum = sem("ln_sum")
        ln_stat = sem("ln_stat")
        ln_mean = sem("ln_mean")
        ln_centred = sem("ln_centred")
        ln_square = sem("ln_square")
        ln_scaled = sem("ln_scaled")
        ln_silu = sem("ln_silu")
        cv_y = sem("cv_y")
        ffn_tap = sem("ffn_tap")
        gelu_done = sem("gelu_done")
        g_hi = sem("g_hi")
        g_ready = sem("g_ready")
        out_stored = sem("out_stored")

        FREE0 = 4

        def norm_tokens(layer, part):
            return XT if layer == DEPTH - 1 and part == 1 else ALL

        def halves(tok):
            return ((1, XT),) if tok == XT else ((0, CT), (1, XT))

        CONSTS = [(ada_in, cfull), (ada_bias, bias_ada), (gain, gains), (na_gain, qk_gain), (na_mask, mask),
                  (rope, cos_sin), (decay, logit), (gn_gain, gn), (cv_bias, cvb), (cv_filter, cvf),
                  (ffn_filter, fff), (ones, one), (head_ones, one_head), (identity, ident), (pick, picker)]
        CONSTS_IN = 16 * len(CONSTS)

        block = ctx.enter_context(nc.Block())

        @block.sync
        def _(sp):
            for s in range(SLOTS):
                sp.dma_start(raw[:, s, :], weights[s, :, :]).then_inc(raw_loaded[s], 16)
            with sp.Fori(1, n_groups // SLOTS) as lap:
                for s in range(SLOTS):
                    sp.wait_ge(weights_used, SLOTS * lap + (s - SLOTS + 1))
                    sp.dma_start(raw[:, s, :], weights[SLOTS * lap + s, :, :]).then_inc(raw_loaded[s], 16)
            last = layers[-1]
            sp.wait_ge(tile_free, FREE0 + last["down_tile"] + C)
            sp.dma_start(out, X[:, :, XT]).then_inc(out_stored, 16)
            sp.wait_ge(out_stored, 16)

        @block.gpsimd
        def _(pool):
            g = nc.gpsimd

            def clear_total(r, tok):
                if r:
                    pool.wait_ge(norm_summed, r)
                g.memset(total[:, tok], 0.0).then_inc(sum_step, 1)

            def add_square(r, c, c_static, tok):
                first = r * (1 + 2 * C) + 1
                g.tensor_tensor(square[:, c_static % 2, tok], X[:, c, tok], X[:, c, tok], ALU.mult)\
                    .then_inc(sum_step, 1)
                pool.wait_ge(sum_step, first + 2 * c + 1)
                g.tensor_tensor(total[:, tok], total[:, tok], square[:, c_static % 2, tok], ALU.add)\
                    .then_inc(sum_step, 1)

            def after_residual(r, tile0, tok):
                clear_total(r, tok)
                for i in bodies(pool, 2):
                    for m in range(4):
                        pool.wait_ge(tile_free, FREE0 + tile0 + 1 + m + 4 * i)
                        add_square(r, 4 * i + m, m, tok)

            def pairs_staged(layer):
                j = layer // 3
                r = 2 * layer
                pool.wait_ge(norm_summed, r + 1)
                for par in range(2):
                    for a in range(6):
                        src = bass.AP(rpb.tensor, j * NA_HEADS * RPB_H * RPB_W + (a + 5 - par) * RPB_W - 48,
                                      [[1, GRID_W], [RPB_H * RPB_W, NA_HEADS], [1, GRID_W]])
                        dst = rel_in[:, :, :].rearrange("p (h a) k -> p h a k", a=6)
                        g.dma_start(dst[64 * par:64 * par + 64, :, a, :], src).then_inc(rel_loaded, 16)
                pool.wait_ge(rel_loaded, 16 * 12 * (j + 1))
                pool.wait_ge(const_loaded, CONSTS_IN)
                g.tensor_tensor(rel[:, :, :, :].rearrange("p h a k -> p (h a) k"),
                                rel_in[:, :, ::-1],
                                mask[:, None, :].to_broadcast([P, NA_HEADS * 6, GRID_W]), ALU.add)\
                    .then_inc(rel_ready, 1)
                pool.wait_ge(tile_free, FREE0 + layers[layer]["mix_tile"] + 24)
                g.memset(Qz[64:128, 0, :], 0.0).then_inc(qz_cleared, 1)
                g.memset(Qz[0:64, 1, :], 0.0).then_inc(qz_cleared, 1)
                tok, n_units, u0 = (XT, 4, 8 * C) if layer == DEPTH - 1 else (ALL, 8, 0)
                for i in bodies(pool, C):
                    pool.wait_ge(scored, 1 + u0 + n_units * i)
                    for par in range(2):
                        half = slice(64 * par, 64 * par + 64)
                        g.tensor_copy(Qz[half, par, tok], QK[half, i, tok]).then_inc(q_staged, 1)
                pool.wait_ge(q_staged, 2 * C * (j + 1))

            g.memset(eps[:, :], EPS).then_inc(c_ready, 1)
            pool.wait_ge(x_loaded, 16)
            clear_total(0, ALL)
            for c in range(C):
                add_square(0, c, c, ALL)

            for layer, p in enumerate(layers):
                r = 2 * layer
                if layer % 3 == 0:
                    pairs_staged(layer)
                    out_tile = p["mix_tile"] + 24
                elif layer % 3 == 1:
                    def add(dst, a0, b0):
                        return g.tensor_tensor(dst, decay_t[:, 0, a0:a0 + CTX], decay_t[:, 1, b0:b0 + CTX], ALU.add)

                    for h in range(RET_HEADS):
                        if h:
                            pool.wait_ge(mask_made, 6 * h)
                        else:
                            pool.wait_ge(rope_step, 17)
                        g.dma_start(decay_t[:, :, :], dist).then_inc(dist_loaded, 16)
                        pool.wait_ge(decayed, 2 * h + 2)
                        if h:
                            pool.wait_ge(ret_out, h)
                        add(A[0][:, CT], P, 3 * P).then_inc(mask_made, 1)
                        add(A[0][:, XT], 3 * P, P).then_inc(mask_made, 1)
                        add(A[1][:, CT], 0, 2 * P).then_inc(mask_made, 1)
                        add(A[1][:, XT], 2 * P, 0).then_inc(mask_made, 1)
                        add(A[2][:, 0:CTX], P, 3 * P).then_inc(mask_made, 1)
                        add(A[2][:, CTX:T], 0, 2 * P).then_inc(mask_made, 1)
                    out_tile = p["mix_tile"] + 48
                else:
                    pool.wait_ge(norm_summed, r + 1)
                    g.memset(total[:, :], 0.0).then_inc(ln_sum, 1)
                    for i in bodies(pool, 4):
                        for k in range(2):
                            pool.wait_ge(tap_done, (CONV_W + 1) * (2 * i + k + 1))
                            pool.wait_ge(ln_sum, 2 * i + k + 1)
                            g.tensor_tensor(total[:, :], total[:, :], Wc[:, 2 * i + k, :], ALU.add)\
                                .then_inc(ln_sum, 1)
                    pool.wait_ge(ln_stat, 1)
                    g.memset(total[:, :], 0.0).then_inc(ln_sum, 1)
                    for c in range(C):
                        pool.wait_ge(ln_square, c + 1)
                        pool.wait_ge(ln_sum, 10 + c)
                        g.tensor_tensor(total[:, :], total[:, :], square[:, c % 2, :], ALU.add)\
                            .then_inc(ln_sum, 1)
                    pool.wait_ge(ln_stat, 2)
                    out_tile = p["mix_tile"] + 16
                after_residual(r + 1, out_tile, norm_tokens(layer, 1))
                if layer < DEPTH - 1:
                    after_residual(r + 2, p["down_tile"], ALL)

        @block.tensor
        def _(pe):
            t = nc.tensor

            def three(dst, st, w, hi, lo, start, stop):
                t.matmul(dst, Whi[:, st.slot, w], hi, start=start, stop=False)
                t.matmul(dst, Whi[:, st.slot, w], lo, start=False, stop=False)
                return t.matmul(dst, Wlo[:, st.slot, w], hi, start=False, stop=stop)

            def three_moving(dst, st, w, hi, lo, start, stop):
                t.matmul(dst, hi, Whi[:, st.slot, w], start=start, stop=False)
                t.matmul(dst, lo, Whi[:, st.slot, w], start=False, stop=False)
                return t.matmul(dst, hi, Wlo[:, st.slot, w], start=False, stop=stop)

            def tile(index, static, groups, hi, lo, tok, ready=None):
                pe.wait_ge(tile_free, index + 1)
                dst, k, count = bank[static % 4], 0, sum(n for _, n in groups)
                for st, n in groups:
                    pe.wait_ge(lo_split, st.n + 1)
                    for q in range(n):
                        if ready:
                            pe.wait_ge(ready[0], ready[1] + k + 1)
                        last = three(dst[:, tok], st, slice(P * q, P * q + P), hi[:, k, tok], lo[:, k, tok],
                                     k == 0, k == count - 1)
                        k += 1
                    last.then_inc(weights_used, 1)

            def ada(st, quarter):
                pe.wait_ge(lo_split, st.n + 1)
                for q in range(2):
                    k = 2 * quarter + q
                    w = slice(512 * q, 512 * q + 512)
                    t.matmul(bank[6][0:4, :], cparts[:, k, :], Whi[:, st.slot, w], start=k == 0, stop=False)
                    last = t.matmul(bank[6][0:4, :], cparts[:, k, :], Wlo[:, st.slot, w], start=False, stop=k == C - 1)
                last.then_inc(weights_used, 1)

            def ada_cols(index):
                pe.wait_ge(rows_copied, index + 1)
                for q in range(4):
                    last = t.matmul(bank[7][:, 2 * q:2 * q + 2], rows[:, P * q:P * q + P], picker[:, :],
                                    start=True, stop=True)
                last.then_inc(cols_made, 1)

            def norm_sum(r, tok):
                pe.wait_ge(sum_step, (r + 1) * (1 + 2 * C))
                t.matmul(bank[4][:, tok], one[:, :], total[:, tok], start=True, stop=True).then_inc(norm_summed, 1)

            def tokens_major(first, per, count, tile0, V_slices):
                for i in bodies(pe, count):
                    for b in range(TB):
                        pe.wait_ge(tile_free, tile0 + b + 1 + TB * i)
                    for quarter in range(4):
                        st = Step(first + quarter, per, i)
                        pe.wait_ge(lo_split, st.n + 1)
                        for q in range(2):
                            k = 2 * quarter + q
                            for b in range(TB):
                                tk = slice(P * b, P * b + P)
                                last = three_moving(bank[b][:, :], st, slice(512 * q, 512 * q + 512),
                                                    Hhi[:, k, tk], Hlo[:, k, tk], k == 0, k == C - 1)
                        last.then_inc(weights_used, 1)

            def na(layer, p):
                j = layer // 3
                last_layer = layer == DEPTH - 1
                per = p["qk_per"]
                qk0 = 2 * C * j
                a0 = 4

                def head_sum(k_static, k, tok):
                    pe.wait_ge(qk_squared, qk0 + k + 1)
                    t.matmul(bank[4 + k_static % 2][:, tok], one_head[:, :], na_sq[:, k_static % 2, tok],
                             start=True, stop=True).then_inc(qk_summed, 1)

                for part, tok in ((0, XT if last_layer else ALL), (1, ALL)):
                    for i in bodies(pe, 2):
                        stride = per // 4
                        for m in range(4):
                            k = 8 * part + m + 4 * i
                            tile(p["mix_tile"] + k, m, [(Step(p["mix"] + 2 * per * part + stride * m, per, i), C)],
                                 Hhi, Hlo, tok, (h_ready, p["mix_ready"]) if m == 0 else None)
                            if layer == 0 and m == 2:
                                ada_cols(a0 + 4 * part + 2 * i)
                            if layer == 0:
                                for q in range(2):
                                    ada(Step(p["mix"] + 2 * per * part + stride * m + 1 + q, per, i), 2 * (m % 2) + q)
                            if m:
                                head_sum(m - 1, k - 1, tok)
                        head_sum(3, 8 * part + 3 + 4 * i, tok)
                        if layer == 0:
                            ada_cols(a0 + 4 * part + 1 + 2 * i)
                tokens_major(p["v"], 4, 2, p["mix_tile"] + 16, None)

                n_units = 4 if last_layer else 8
                u0 = 0 if layer == 0 else 8 * C
                blocks = (2, 3) if last_layer else (0, 1, 2, 3)
                units = [(par, b) for par in range(2) for b in blocks]
                pe.wait_ge(tile_free, FREE0 + p["mix_tile"] + 24)
                if layer == 0:
                    pe.wait_ge(mod_ready, 12)
                for i in bodies(pe, C):
                    pe.wait_ge(q_staged, 2 * C * j + 2 + 2 * i)
                    for s in range(n_units + 3):
                        if s < n_units:
                            par, b = units[s]
                            keys = CT if b < 2 else ALL
                            pe.wait_ge(exped, u0 + s + 1 + n_units * i)
                            last = t.matmul(bank[s % 4][:, keys], Qz[:, par, P * b:P * b + P], QK[:, 8 + i, keys],
                                            start=True, stop=True)
                            last.then_inc(scored, 1)
                        if 2 <= s < n_units + 2:
                            u = s - 2
                            par, b = units[u]
                            pe.wait_ge(exped, u0 + 4 + u + 1 + n_units * i)
                            pe.wait_ge(p_copied, u0 + u + 1 + n_units * i)
                            n_keys = 2 if b < 2 else 4
                            for kb in range(n_keys):
                                last = t.transpose(bank[4 + u % 2][:, P * kb:P * kb + P], prob[:, u % 2, P * kb:P * kb + P],
                                                   ident[:, :])
                            last.then_inc(p_turned, 1)
                        if s >= 3:
                            u = s - 3
                            par, b = units[u]
                            pe.wait_ge(p_copied, u0 + 2 + u + 1 + n_units * i)
                            pe.wait_ge(o_stored, u0 + 2 + u + 1 + n_units * i)
                            n_keys = 2 if b < 2 else 4
                            for kb in range(n_keys):
                                last = t.matmul(bank[6 + u % 2][:, 0:NA_HD], probT[:, u % 2, P * kb:P * kb + P],
                                                V[:, kb, bass.ts(2 * i + par, NA_HD)], start=kb == 0,
                                                stop=kb == n_keys - 1)
                            last.then_inc(attended, 1)
                out_blocks = blocks
                pe.wait_ge(o_stored, u0 + 4 + n_units * C)
                for c in range(C):
                    if c >= 4:
                        pe.wait_ge(h_ready, p["o_ready"] + c - 3)
                    for b in out_blocks:
                        last = t.transpose(bank[c % 4][:, P * b:P * b + P], O[:, b, P * c:P * c + P], ident[:, :])
                    last.then_inc(o_turned, 1)
                tok = XT if last_layer else ALL
                for i in bodies(pe, 2):
                    for m in range(4):
                        if m == 0:
                            pe.wait_ge(h_ready, p["o_ready"] + C)
                        tile(p["mix_tile"] + 24 + m + 4 * i, m, [(Step(p["o"] + m, 4, i), C)], Hhi, Hlo, tok)

            def retention(p):
                for i in bodies(pe, 4):
                    for m in range(4):
                        tile(p["mix_tile"] + m + 4 * i, m, [(Step(p["mix"] + m, 4, i), C)], Hhi, Hlo, ALL,
                             (h_ready, p["mix_ready"]) if m == 0 else None)
                tokens_major(p["v"], 4, 4, p["mix_tile"] + 16, None)
                pe.wait_ge(tile_free, FREE0 + p["mix_tile"] + 32)
                pe.wait_ge(rope_step, 17)

                def scores(h):
                    if h:
                        pe.wait_ge(weighted, 3 * h)
                    for kb in range(TB):
                        dst = bank[kb][:, :] if kb < 2 else bank[2][:, CTX * (kb - 2):CTX * (kb - 1)]
                        for d in range(2):
                            last = t.matmul(dst, QKr[:, C + 2 * h + d, P * kb:P * kb + P],
                                            QKr[:, 2 * h + d, ALL if kb < 2 else XT], start=d == 0, stop=d == 1)
                    last.then_inc(ret_scored, 1)

                def mix_values(h):
                    pe.wait_ge(weighted, 3 * h + 3)
                    if h:
                        pe.wait_ge(gn_done, TB * h)
                    for b in range(TB):
                        n_keys = 2 if b < 2 else 4
                        for kb in range(n_keys):
                            a = A[kb][:, P * b:P * b + P] if kb < 2 else \
                                A[2][:, CTX * (kb - 2) + P * (b - 2):CTX * (kb - 2) + P * (b - 1)]
                            last = t.matmul(bank[4 + b][:, :], a, Vr[:, kb, RET_V * h:RET_V * (h + 1)],
                                            start=kb == 0, stop=kb == n_keys - 1)
                    last.then_inc(ret_out, 1)

                scores(0)
                for h in range(RET_HEADS):
                    if h + 1 < RET_HEADS:
                        scores(h + 1)
                    mix_values(h)
                pe.wait_ge(gn_done, TB * RET_HEADS)
                for c in range(RET_VC):
                    if c >= 4:
                        pe.wait_ge(ot_copied, c - 3)
                    for b in range(TB):
                        last = t.transpose(bank[c % 4][:, P * b:P * b + P], On[:, b, P * c:P * c + P], ident[:, :])
                    last.then_inc(gn_turned, 1)
                pe.wait_ge(ot_copied, RET_VC)
                for i in bodies(pe, 4):
                    for m in range(4):
                        tile(p["mix_tile"] + 32 + m + 4 * i, m, [(Step(p["g"] + m, 4, i), C)], Hhi, Hlo, ALL)
                pe.wait_ge(tile_free, FREE0 + p["mix_tile"] + 48)
                for i in bodies(pe, 2):
                    for m in range(4):
                        tile(p["mix_tile"] + 48 + m + 4 * i, m,
                             [(Step(p["o"] + 2 * m, 8, i), 8), (Step(p["o"] + 2 * m + 1, 8, i), 8)], Yhi, Ylo, ALL)

            def conv(p):
                for i in bodies(pe, 4):
                    for m in range(4):
                        tile(p["mix_tile"] + m + 4 * i, m, [(Step(p["mix"] + m, 4, i), C)], Hhi, Hlo, ALL,
                             (h_ready, p["mix_ready"]) if m == 0 else None)
                for k, done in enumerate((C + 1, 2 * C + 2)):
                    pe.wait_ge(ln_sum, done)
                    if k:
                        pe.wait_ge(ln_mean, 1)
                    t.matmul(bank[4][:, :], one[:, :], total[:, :], start=True, stop=True).then_inc(ln_stat, 1)
                for i in bodies(pe, 2):
                    for m in range(4):
                        tile(p["mix_tile"] + 16 + m + 4 * i, m, [(Step(p["o"] + m, 4, i), C)], Hhi, Hlo, ALL,
                             (h_ready, p["o_ready"]) if m == 0 else None)

            def ffn(layer, p):
                last_layer = layer == DEPTH - 1
                tok = XT if last_layer else ALL
                per = p["up_per"]
                if not last_layer:
                    for quarter in range(4):
                        ada(Step(p["ada"] + quarter), quarter)
                    ada_cols(ADA_SLICES * (layer + 1))
                for i in bodies(pe, FC // 2):
                    for m in range(4):
                        s = p["up"] + (2 * m if per == 8 else m)
                        if per == 8:
                            ada(Step(s, per, i), m)
                            s += 1
                        tile(p["up_tile"] + m + 4 * i, m, [(Step(s, per, i), C)], Hhi, Hlo, tok,
                             (h_ready, p["ffn_ready"]) if m == 0 else None)
                    if per == 8:
                        ada_cols(ADA_SLICES * (layer + 1) + 1 + i)
                per = 4 * len(DOWN)
                for i in bodies(pe, 2, last_layer):
                    for m in range(4):
                        tile(p["down_tile"] + m + 4 * i, m,
                             [(Step(p["down"] + 3 * m + q, per, i), DOWN[q]) for q in range(3)], Ghi, Glo, tok,
                             (g_ready, 2 + FC * layer) if m == 0 else None)

            pe.wait_ge(const_loaded, CONSTS_IN)
            pe.wait_ge(c_ready, 4)
            for i in bodies(pe, 4):
                for quarter in range(4):
                    ada(Step(quarter, 4, i), quarter)
                ada_cols(i)
            for layer, p in enumerate(layers):
                norm_sum(2 * layer, ALL)
                if layer % 3 == 0:
                    na(layer, p)
                elif layer % 3 == 1:
                    retention(p)
                else:
                    conv(p)
                norm_sum(2 * layer + 1, norm_tokens(layer, 1))
                ffn(layer, p)

        @block.scalar
        def _(act):
            a = nc.scalar

            def split(st):
                st = st.ahead(LEAD)
                if isinstance(st.n, int) and st.n >= n_groups:
                    return
                act.wait_ge(raw_loaded[st.slot], 16 * (st.lap + 1))
                a.activation(Whi[:, st.slot, :], raw[:, st.slot, :], ACT.Copy).then_inc(hi_split, 1)

            def norm_apply(layer, part, between=()):
                tok = norm_tokens(layer, part)
                r = 2 * layer + part
                act.wait_ge(norm_summed, r + 1)
                a.activation(root[:, tok], bank[4][:, tok], ACT.Sqrt, bias=eps[:, :], scale=1.0 / D)\
                    .then_inc(norm_root, 1)
                ready = layers[layer]["ffn_ready" if part else "mix_ready"]
                k0 = C * r
                for c in range(C):
                    act.wait_ge(norm_scaled, k0 + c + 1)
                    if tok == ALL:
                        a.activation(hb[:, c % 2, CT], hb[:, c % 2, CT], ACT.Identity,
                                     bias=mod[:, layer % 2, 3 * C * part + c, 0:1],
                                     scale=scale[:, part, c, 0:1]).then_inc(norm_ctx, 1)
                        act.wait_ge(norm_ctx, k0 + c + 1)
                    act.wait_ge(norm_x, k0 + c + 1)
                    a.activation(Hhi[:, c, tok], hb[:, c % 2, tok], ACT.Copy).then_inc(h_hi, 1)
                    if c < len(between):
                        split(between[c])

            def na(layer, p):
                j = layer // 3
                last_layer = layer == DEPTH - 1
                per = p["qk_per"]
                qk0 = 2 * C * j

                def root_of(k_static, k, tok):
                    act.wait_ge(qk_summed, qk0 + k + 1)
                    a.activation(na_root[:, k_static % 4, tok], bank[4 + k_static % 2][:, tok], ACT.Sqrt,
                                 bias=eps[:, :], scale=1.0 / NA_HD).then_inc(qk_root, 1)

                for part, tok in ((0, XT if last_layer else ALL), (1, ALL)):
                    for i in bodies(act, 2):
                        stride = per // 4
                        for m in range(4):
                            k = 8 * part + m + 4 * i
                            st = Step(p["mix"] + 2 * per * part + stride * m, per, i)
                            act.wait_ge(weights_used, st.n + 1)
                            a.activation(na_sq[:, m % 2, tok], bank[m][:, tok], ACT.Square).then_inc(qk_squared, 1)
                            for q in range(stride):
                                split(st.ahead(q))
                            if m:
                                root_of(m - 1, k - 1, tok)
                        root_of(3, 8 * part + 3 + 4 * i, tok)
                for i in bodies(act, 2):
                    for quarter in range(4):
                        split(Step(p["v"] + quarter, 4, i))

                n_units = 4 if last_layer else 8
                u0 = 0 if layer == 0 else 8 * C
                blocks = (2, 3) if last_layer else (0, 1, 2, 3)
                units = [(par, b) for par in range(2) for b in blocks]
                for i in bodies(act, C):
                    for s in range(n_units + 2):
                        if s >= 2:
                            u = s - 2
                            par, b = units[u]
                            keys = CT if b < 2 else ALL
                            act.wait_ge(p_turned, u0 + 2 + u + 1 + n_units * i)
                            act.wait_ge(attended, u0 + u + 1 + n_units * i)
                            a.activation(probT[:, u % 2, keys], bank[4 + u % 2][:, keys], ACT.Copy)\
                                .then_inc(p_copied, 1)
                        if s < n_units:
                            u = s
                            par, b = units[u]
                            keys = CT if b < 2 else ALL
                            act.wait_ge(peaked, u0 + u + 1 + n_units * i)
                            act.wait_ge(p_turned, u0 + u + 1 + n_units * i)
                            act.wait_ge(o_stored, u0 + u + 1 + n_units * i)
                            a.activation(prob[:, u % 2, keys], bank[u % 4][:, keys], ACT.Exp, bias=peak[:, u % 4:u % 4 + 1],
                                         accum_out=psum_p[:, u % 4:u % 4 + 1]).then_inc(exped, 1)
                tok = XT if last_layer else ALL
                for c in range(C):
                    act.wait_ge(o_turned, C * j + c + 1)
                    a.activation(Hhi[:, c, tok], bank[c % 4][:, tok], ACT.Copy).then_inc(h_hi, 1)
                for i in bodies(act, 2):
                    for m in range(4):
                        split(Step(p["o"] + m, 4, i))

            def retention(p):
                for i in bodies(act, 4):
                    for m in range(4):
                        split(Step(p["mix"] + m, 4, i))
                for i in bodies(act, 4):
                    for m in range(4):
                        split(Step(p["v"] + m, 4, i))
                act.wait_ge(lg_step, 6)

                def decays(h):
                    act.wait_ge(dist_loaded, 16 * (h + 1))
                    for way in range(2):
                        lg = log_gamma[:, RET_HEADS * way + h:RET_HEADS * way + h + 1]
                        a.activation(decay_t[:, way, :], decay_t[:, way, :], ACT.Exp, scale=lg).then_inc(decayed, 1)

                decays(0)
                for h in range(RET_HEADS):
                    if h + 1 < RET_HEADS:
                        decays(h + 1)
                    act.wait_ge(gn_stat, 2 * TB * (h + 1))
                    a.activation(sd4[:, :], mv[:, :, 1], ACT.Sqrt, bias=eps[:, :]).then_inc(gn_root, 1)
                for c in range(RET_VC):
                    act.wait_ge(gn_turned, c + 1)
                    a.activation(OT[:, c, :], bank[c % 4][:, :], ACT.Copy).then_inc(ot_copied, 1)
                for i in bodies(act, 4):
                    for m in range(4):
                        st = Step(p["g"] + m, 4, i)
                        act.wait_ge(weights_used, st.n + 1)
                        a.activation(gated[m], bank[m][:, :], ACT.Silu).then_inc(gate_silu, 1)
                        split(st)
                        act.wait_ge(y_made, m + 1 + 4 * i)
                        a.activation(Yhi[:, m + 4 * i, :], gated[m], ACT.Copy).then_inc(y_hi, 1)
                for i in bodies(act, 2):
                    for m in range(8):
                        split(Step(p["o"] + m, 8, i))

            def conv(p):
                for i in bodies(act, 4):
                    for k in range(2):
                        split(Step(p["mix"] + 2 * k, 4, i))
                        st = Step(p["mix"] + 2 * k + 1, 4, i)
                        act.wait_ge(weights_used, st.n + 1)
                        a.activation(glu_s[:, k, :], bank[2 * k + 1][:, :], ACT.Sigmoid,
                                     bias=cvb[:, 1, bass.ds(2 * i + k, 1)]).then_inc(glu_sigmoid, 1)
                        split(st)
                for c in range(C):
                    act.wait_ge(ln_centred, c + 1)
                    if c >= 2:
                        act.wait_ge(ln_sum, 10 + c - 1)
                    a.activation(square[:, c % 2, :], Wc[:, c, :], ACT.Square).then_inc(ln_square, 1)
                act.wait_ge(ln_stat, 2)
                a.activation(root[:, :], bank[4][:, :], ACT.Sqrt, bias=eps[:, :], scale=1.0 / D).then_inc(ln_mean, 1)
                for c in range(C):
                    act.wait_ge(ln_scaled, c + 1)
                    a.activation(hb[:, c % 2, :], hb[:, c % 2, :], ACT.Silu, bias=cvb[:, 4, c:c + 1],
                                 scale=cvb[:, 3, c:c + 1]).then_inc(ln_silu, 1)
                    act.wait_ge(ln_silu, c + 1)
                    a.activation(Hhi[:, c, :], hb[:, c % 2, :], ACT.Copy).then_inc(h_hi, 1)
                for i in bodies(act, 2):
                    for m in range(4):
                        split(Step(p["o"] + m, 4, i))

            def ffn(layer, p):
                last_layer = layer == DEPTH - 1
                tok = XT if last_layer else ALL
                per = p["up_per"]
                for i in bodies(act, FC // 2):
                    for m in range(4):
                        s = p["up"] + (2 * m if per == 8 else m)
                        if per == 8:
                            split(Step(s, per, i))
                            s += 1
                        split(Step(s, per, i))
                        k = m // 2
                        act.wait_ge(tile_free, FREE0 + p["up_tile"] + m + 1 + 4 * i)
                        if m % 2 == 0:
                            a.activation(cv[:, k, tok], cv[:, k, tok], ACT.Gelu_apprx_tanh).then_inc(gelu_done, 1)
                        else:
                            a.activation(Ghi[:, k + 2 * i, tok], cv[:, k, tok], ACT.Copy).then_inc(g_hi, 1)
                per = 4 * len(DOWN)
                for i in bodies(act, 2, last_layer):
                    for m in range(per):
                        split(Step(p["down"] + m, per, i))

            act.dma_start(X[:, :, :], x).then_inc(x_loaded, 16)
            for src, dst in CONSTS:
                full = dst[tuple(slice(None) for _ in dst.shape)]
                act.dma_start(full, src).then_inc(const_loaded, 16)
            act.wait_ge(const_loaded, CONSTS_IN)
            a.activation(csilu[:, :, :], cfull[:, :, :], ACT.Silu).then_inc(c_ready, 1)
            act.wait_ge(c_ready, 2)
            a.activation(cparts[:, :, 0:2], csilu[:, :, :], ACT.Copy).then_inc(c_ready, 1)
            act.wait_ge(lg_step, 2)
            a.activation(small[:, 1, :], small[:, 0, :], ACT.Exp, scale=-1.0).then_inc(lg_step, 1)
            act.wait_ge(lg_step, 3)
            a.activation(small[:, 2, :], small[:, 1, :], ACT.Ln, bias=1.0).then_inc(lg_step, 1)
            for n in range(LEAD):
                split(Step(n - LEAD))
            for i in bodies(act, 4):
                for quarter in range(4):
                    split(Step(quarter, 4, i))
            for layer, p in enumerate(layers):
                norm_apply(layer, 0)
                if layer % 3 == 0:
                    na(layer, p)
                elif layer % 3 == 1:
                    retention(p)
                else:
                    conv(p)
                if layer < DEPTH - 1:
                    split(Step(p["ada"]))
                    norm_apply(layer, 1, [Step(p["ada"] + q) for q in (1, 2, 3)])
                else:
                    norm_apply(layer, 1)
                ffn(layer, p)

        @block.vector
        def _(dve):
            v = nc.vector

            def split(st):
                st = st.ahead(LEAD)
                if isinstance(st.n, int) and st.n >= n_groups:
                    return
                dve.wait_ge(hi_split, st.n + 1)
                v.tensor_tensor(Wlo[:, st.slot, :], raw[:, st.slot, :], Whi[:, st.slot, :].bitcast(F32), ALU.subtract)\
                    .then_inc(lo_split, 1)

            def ada_rows(index, st):
                dve.wait_ge(weights_used, st.n + 1)
                v.tensor_copy(rows[:, :], bank[6][0:4, :]).then_inc(rows_copied, 1)

            def ada_store(index, layer, s):
                dve.wait_ge(cols_made, index + 1)
                v.tensor_tensor(mod[:, layer % 2, bass.ts(s, 4), :],
                                bank[7][:, 0:8].rearrange("p (q s) -> p q s", s=2),
                                bias_ada[:, layer, bass.ts(s, 4)].unsqueeze(2).to_broadcast([P, 4, 2]), ALU.add)\
                    .then_inc(mod_ready, 1)

            def norm_apply(layer, part, between=()):
                tok = norm_tokens(layer, part)
                r = 2 * layer + part
                if layer == 0:
                    dve.wait_ge(mod_ready, 12 if part else 4)
                else:
                    dve.wait_ge(mod_ready, ADA_SLICES * (layer + 1))
                v.scalar_tensor_tensor(scale[:, part, :, :], mod[:, layer % 2, C * (3 * part + 1):C * (3 * part + 2), :],
                                       1.0, gains[:, layer, part, :].unsqueeze(2).to_broadcast([P, C, 2]),
                                       ALU.add, ALU.mult)
                dve.wait_ge(norm_root, r + 1)
                v.reciprocal(rstd[:, tok], root[:, tok]).then_inc(norm_rstd, 1)
                dve.wait_ge(norm_rstd, r + 1)
                k0 = C * r
                ready = layers[layer]["ffn_ready" if part else "mix_ready"]

                def low(c):
                    dve.wait_ge(h_hi, ready + c + 1)
                    v.tensor_tensor(Hlo[:, c, tok], hb[:, c % 2, tok], Hhi[:, c, tok].bitcast(F32), ALU.subtract)\
                        .then_inc(h_ready, 1)

                for c in range(C):
                    if c >= 2:
                        dve.wait_ge(h_ready, ready + c - 1)
                    v.tensor_tensor(hb[:, c % 2, tok], X[:, c, tok], rstd[:, tok], ALU.mult).then_inc(norm_scaled, 1)
                    dve.wait_ge(norm_scaled, k0 + c + 1)
                    v.tensor_scalar(hb[:, c % 2, XT], hb[:, c % 2, XT], scale[:, part, c, 1:2],
                                    mod[:, layer % 2, 3 * C * part + c, 1:2], ALU.mult, ALU.add).then_inc(norm_x, 1)
                    if c:
                        low(c - 1)
                    if c < len(between):
                        between[c]()
                low(C - 1)

            def residual(layer, part, src, m, tok, bias=None):
                for half, hs in halves(tok):
                    gate = mod[:, layer % 2, bass.ds(C * (3 * part + 2) + m, 1), half]
                    last = v.scalar_tensor_tensor(X[:, m, hs], src[:, hs], gate, X[:, m, hs], ALU.mult, ALU.add)
                last.then_inc(tile_free, 1)

            def projected(layer, first, stride, per, tok, unroll=False):
                part = 1 if stride == 3 else 0
                for i in bodies(dve, 2, unroll):
                    for m in range(4):
                        st = Step(first + stride * m, per, i)
                        for q in range(stride - 1):
                            split(st.ahead(q))
                        dve.wait_ge(weights_used, st.ahead(stride - 1).n + 1)
                        residual(layer, part, bank[m], m + 4 * i, tok)
                        split(st.ahead(stride - 1))

            def tokens_major(first, count, dst):
                for i in bodies(dve, count):
                    for quarter in range(3):
                        split(Step(first + quarter, 4, i))
                    st = Step(first + 3, 4, i)
                    dve.wait_ge(weights_used, st.n + 1)
                    for b in range(TB):
                        v.tensor_copy(dst[:, b, bass.ts(i, 512)], bank[b][:, :]).then_inc(tile_free, 1)
                    split(st)

            def na(layer, p):
                j = layer // 3
                last_layer = layer == DEPTH - 1
                per = p["qk_per"]
                qk0 = 2 * C * j
                for part, tok in ((0, XT if last_layer else ALL), (1, ALL)):
                    def normed(m, k, tok):
                        dve.wait_ge(qk_root, qk0 + k + 1)
                        v.reciprocal(na_root[:, m, tok], na_root[:, m, tok]).then_inc(qk_rstd, 1)
                        dve.wait_ge(qk_rstd, qk0 + k + 1)
                        v.scalar_tensor_tensor(QK[:, k, tok], bank[m][:, tok], qk_gain[:, j, part:part + 1],
                                               na_root[:, m, tok], ALU.mult, ALU.mult).then_inc(tile_free, 1)

                    for i in bodies(dve, 2):
                        stride = per // 4
                        for m in range(4):
                            k = 8 * part + m + 4 * i
                            st = Step(p["mix"] + 2 * per * part + stride * m, per, i)
                            for q in range(stride):
                                split(st.ahead(q))
                            if m:
                                normed(m - 1, k - 1, tok)
                            s = 4 + 4 * part + 2 * i
                            if layer == 0 and m % 2:
                                ada_rows(s, st.ahead(2))
                            if layer == 0 and m == 2:
                                ada_store(s, 0, s)
                        normed(3, 8 * part + 3 + 4 * i, tok)
                        if layer == 0:
                            ada_store(s + 1, 0, s + 1)
                dve.wait_ge(rel_ready, j + 1)
                tokens_major(p["v"], 2, V)

                n_units = 4 if last_layer else 8
                u0 = 0 if layer == 0 else 8 * C
                blocks = (2, 3) if last_layer else (0, 1, 2, 3)
                units = [(par, b) for par in range(2) for b in blocks]
                x_units = sum(b >= 2 for _, b in units)
                b0 = 0 if layer == 0 else 4 * C
                for i in bodies(dve, C):
                    n_biased = 0
                    for s in range(n_units + 3):
                        if s < n_units:
                            u = s
                            par, b = units[u]
                            keys = CT if b < 2 else ALL
                            dve.wait_ge(scored, u0 + 1 + u + 1 + n_units * i)
                            if b >= 2:
                                n_biased += 1
                                a0 = 2 if b == 2 else 0
                                sx = bank[u % 4][:, XT].rearrange("p (r k) -> p r k", k=GRID_W)
                                v.tensor_tensor(sx, sx, rel[:, 2 * i + par, a0:a0 + 4, :], ALU.add).then_inc(biased, 1)
                                dve.wait_ge(biased, b0 + n_biased + x_units * i)
                            v.tensor_reduce(peak[:, u % 4:u % 4 + 1], bank[u % 4][:, keys], axis=AX, op=ALU.max,
                                            negate=True).then_inc(peaked, 1)
                        if s >= 3:
                            u = s - 3
                            par, b = units[u]
                            dve.wait_ge(attended, u0 + 2 + u + 1 + n_units * i)
                            v.reciprocal(rinv[:, u % 4:u % 4 + 1], psum_p[:, u % 4:u % 4 + 1]).then_inc(inverted, 1)
                            dve.wait_ge(inverted, u0 + u + 1 + n_units * i)
                            v.tensor_scalar(O[:, b, bass.ts(2 * i + par, NA_HD)], bank[6 + u % 2][:, 0:NA_HD],
                                            rinv[:, u % 4:u % 4 + 1], None, ALU.mult).then_inc(o_stored, 1)
                tok = XT if last_layer else ALL
                for c in range(C):
                    dve.wait_ge(h_hi, p["o_ready"] + c + 1)
                    v.tensor_tensor(Hlo[:, c, tok], bank[c % 4][:, tok], Hhi[:, c, tok].bitcast(F32), ALU.subtract)\
                        .then_inc(h_ready, 1)
                projected(layer, p["o"], 1, 4, tok)

            def retention(p):
                cos, sin = cos_sin[:, 0, :], cos_sin[:, 1, :]
                for i in bodies(dve, 4):
                    for k in range(2):
                        split(Step(p["mix"] + 2 * k, 4, i))
                        st = Step(p["mix"] + 2 * k + 1, 4, i)
                        dve.wait_ge(weights_used, st.n + 1)
                        first, second = bank[2 * k], bank[2 * k + 1]
                        j = 2 * k + 4 * i
                        dve.wait_ge(rope_step, 2 * k + 1 + 4 * i)
                        v.tensor_tensor(rope_t[:, 0, :], first[:, XT], cos, ALU.mult)
                        v.tensor_tensor(rope_t[:, 1, :], first[:, XT], sin, ALU.mult)
                        v.tensor_copy(QKr[:, j, CT], first[:, CT]).then_inc(tile_free, 1)
                        v.tensor_tensor(rope_t[:, 2, :], second[:, XT], sin, ALU.mult)
                        v.tensor_tensor(rope_t[:, 3, :], second[:, XT], cos, ALU.mult)
                        v.tensor_copy(QKr[:, j + 1, CT], second[:, CT]).then_inc(tile_free, 1)
                        dve.wait_ge(tile_free, FREE0 + p["mix_tile"] + 2 * k + 2 + 4 * i)
                        v.tensor_tensor(QKr[:, j, XT], rope_t[:, 0, :], rope_t[:, 2, :], ALU.subtract)\
                            .then_inc(rope_step, 1)
                        v.tensor_tensor(QKr[:, j + 1, XT], rope_t[:, 1, :], rope_t[:, 3, :], ALU.add)\
                            .then_inc(rope_step, 1)
                        split(st)
                tokens_major(p["v"], 4, Vr)
                for h in range(RET_HEADS):
                    dve.wait_ge(ret_scored, h + 1)
                    dve.wait_ge(mask_made, 6 * (h + 1))
                    for b in range(3):
                        v.scalar_tensor_tensor(A[b], bank[b][:, :], RET_QK ** -0.5, A[b],
                                               ALU.mult, ALU.mult).then_inc(weighted, 1)
                    dve.wait_ge(ret_out, h + 1)
                    for b in range(TB):
                        v.bn_stats(stats[:, b, :], bank[4 + b][:, :]).then_inc(gn_stat, 1)
                    dve.wait_ge(gn_stat, 2 * TB * h + TB)
                    for b in range(TB):
                        v.bn_aggr(mv[:, b, :], stats[:, b, :]).then_inc(gn_stat, 1)
                    dve.wait_ge(gn_root, h + 1)
                    v.reciprocal(sd4[:, :], sd4[:, :]).then_inc(gn_rstd, 1)
                    dve.wait_ge(gn_rstd, h + 1)
                    for b in range(TB):
                        v.tensor_scalar(On[:, b, RET_V * h:RET_V * (h + 1)], bank[4 + b][:, :], mv[:, b, 0:1],
                                        sd4[:, b:b + 1], ALU.subtract, ALU.mult).then_inc(gn_done, 1)
                for i in bodies(dve, 4):
                    for m in range(4):
                        dve.wait_ge(gate_silu, m + 1 + 4 * i)
                        v.scalar_tensor_tensor(gated[m], OT[:, m + 4 * i, :], gn[:, bass.ds(m + 4 * i, 1)],
                                               gated[m], ALU.mult, ALU.mult).then_inc(y_made, 1)
                        dve.wait_ge(y_made, m + 1 + 4 * i)
                        split(Step(p["g"] + m, 4, i))
                        dve.wait_ge(y_hi, m + 1 + 4 * i)
                        v.tensor_tensor(Ylo[:, m + 4 * i, :], gated[m], Yhi[:, m + 4 * i, :].bitcast(F32),
                                        ALU.subtract).then_inc(tile_free, 1)
                projected(1, p["o"], 2, 8, ALL)

            def conv(p):
                mid = CONV_W // 2
                taps = [mid, mid - 1] + [k for k in range(CONV_W) if k not in (mid, mid - 1)]
                u3 = U[:, :, :].rearrange("p k (s n) -> p k s n", s=2)
                w4 = Wc[:, :, :].rearrange("p c (s n) -> p c s n", s=2)
                z4 = conv2[:, :, :].rearrange("p k (s n) -> p k s n", s=2)
                for i in bodies(dve, 4):
                    for k in range(2):
                        split(Step(p["mix"] + 2 * k, 4, i))
                        st = Step(p["mix"] + 2 * k + 1, 4, i)
                        c = 2 * i + k
                        dve.wait_ge(glu_sigmoid, c + 1)
                        v.scalar_tensor_tensor(U[:, k, :], bank[2 * k][:, :], cvb[:, 0, bass.ds(c, 1)], glu_s[:, k, :],
                                               ALU.add, ALU.mult).then_inc(tile_free, 1)
                        dve.wait_ge(tile_free, FREE0 + p["mix_tile"] + 2 * k + 1 + 4 * i)
                        dve.sem_inc(tile_free, 1)
                        split(st)
                        done = (CONV_W + 1) * c
                        for n, tap in enumerate(taps):
                            w = cvf[:, bass.ds(c, 1), tap]
                            shift = tap - mid
                            lo, hi = max(0, -shift), min(CTX, CTX - shift)
                            acc = w4[:, c, :, :] if n % 2 == 0 else z4[:, k, :, :]
                            if n == 0:
                                v.tensor_scalar(acc, u3[:, k, :, :], w, cvb[:, 2, bass.ds(c, 1)], ALU.mult, ALU.add)\
                                    .then_inc(tap_done, 1)
                            elif n == 1:
                                v.memset(z4[:, k, :, 0:1], 0.0)
                                v.tensor_scalar(acc[:, :, lo:hi], u3[:, k, :, lo + shift:hi + shift], w, None, ALU.mult)\
                                    .then_inc(tap_done, 1)
                            else:
                                dve.wait_ge(tap_done, done + n - 1)
                                v.scalar_tensor_tensor(acc[:, :, lo:hi], u3[:, k, :, lo + shift:hi + shift], w,
                                                       acc[:, :, lo:hi], ALU.mult, ALU.add).then_inc(tap_done, 1)
                        dve.wait_ge(tap_done, done + CONV_W)
                        v.tensor_tensor(Wc[:, c, :], Wc[:, c, :], conv2[:, k, :], ALU.add).then_inc(tap_done, 1)
                dve.wait_ge(ln_stat, 1)
                v.tensor_scalar(rstd[:, :], bank[4][:, :], 1.0 / D, None, ALU.mult).then_inc(ln_mean, 1)
                dve.wait_ge(ln_mean, 1)
                for c in range(C):
                    v.tensor_tensor(Wc[:, c, :], Wc[:, c, :], rstd[:, :], ALU.subtract).then_inc(ln_centred, 1)
                dve.wait_ge(ln_centred, C)
                dve.wait_ge(ln_mean, 2)
                v.reciprocal(rstd[:, :], root[:, :]).then_inc(ln_mean, 1)
                dve.wait_ge(ln_mean, 3)

                def low(c):
                    dve.wait_ge(h_hi, p["o_ready"] + c + 1)
                    v.tensor_tensor(Hlo[:, c, :], hb[:, c % 2, :], Hhi[:, c, :].bitcast(F32), ALU.subtract)\
                        .then_inc(h_ready, 1)

                for c in range(C):
                    if c >= 2:
                        dve.wait_ge(h_ready, p["o_ready"] + c - 1)
                    v.tensor_tensor(hb[:, c % 2, :], Wc[:, c, :], rstd[:, :], ALU.mult).then_inc(ln_scaled, 1)
                    if c:
                        low(c - 1)
                low(C - 1)
                for i in bodies(dve, 2):
                    for m in range(4):
                        st = Step(p["o"] + m, 4, i)
                        c = m + 4 * i
                        dve.wait_ge(weights_used, st.n + 1)
                        dve.wait_ge(tile_free, FREE0 + p["mix_tile"] + 16 + c - 1)
                        v.tensor_scalar(glu_s[:, m % 2, :], bank[m][:, :], cvb[:, 5, bass.ds(c, 1)], None, ALU.add)\
                            .then_inc(cv_y, 1)
                        dve.wait_ge(cv_y, c + 1)
                        residual(2, 0, glu_s[:, m % 2, :], c, ALL)
                        split(st)

            def ffn(layer, p):
                last_layer = layer == DEPTH - 1
                tok = XT if last_layer else ALL
                s0 = 1 if last_layer else 0
                per = p["up_per"]
                for i in bodies(dve, FC // 2):
                    for m in range(4):
                        s = p["up"] + (2 * m if per == 8 else m)
                        if per == 8:
                            split(Step(s, per, i))
                            s += 1
                        st = Step(s, per, i)
                        k, j = m // 2, m // 2 + 2 * i
                        dve.wait_ge(weights_used, st.n + 1)
                        if m % 2 == 0:
                            u3 = bank[m][:, :].rearrange("p (s n) -> p s n", s=2)[:, s0:2, :]
                            c3 = cv[:, k, :].rearrange("p (s n) -> p s n", s=2)[:, s0:2, :]
                            f = fff[:, layer, bass.ds(j, 1), :]
                            dve.wait_ge(g_ready, FC * layer + k + 1 + 2 * i)
                            v.tensor_scalar(c3, u3, f[:, 0, 1:2], f[:, 0, 3:4], ALU.mult, ALU.add).then_inc(ffn_tap, 1)
                            dve.wait_ge(ffn_tap, 2 * FC * layer + 2 * k + 1 + 4 * i)
                            v.scalar_tensor_tensor(c3[:, :, 1:], u3[:, :, :-1], f[:, 0, 0:1], c3[:, :, 1:],
                                                   ALU.mult, ALU.add).then_inc(ffn_tap, 1)
                            dve.wait_ge(ffn_tap, 2 * FC * layer + 2 * k + 2 + 4 * i)
                            v.scalar_tensor_tensor(c3[:, :, :-1], u3[:, :, 1:], f[:, 0, 2:3], c3[:, :, :-1],
                                                   ALU.mult, ALU.add).then_inc(tile_free, 1)
                            split(st)
                        else:
                            dve.wait_ge(gelu_done, FC * layer + k + 1 + 2 * i)
                            v.tensor_tensor(cv[:, k, tok], cv[:, k, tok], bank[m][:, tok], ALU.mult)\
                                .then_inc(tile_free, 1)
                            split(st)
                            dve.wait_ge(g_hi, FC * layer + k + 1 + 2 * i)
                            v.tensor_tensor(Glo[:, j, tok], cv[:, k, tok], Ghi[:, j, tok].bitcast(F32), ALU.subtract)\
                                .then_inc(g_ready, 1)
                    if per == 8:
                        ada_rows(0, Step(p["up"] + 6, per, i))
                        ada_store(ADA_SLICES * (layer + 1) + 1 + i, layer + 1, 1 + i)
                projected(layer, p["down"], 3, 12, tok, last_layer)

            dve.sem_inc(tile_free, FREE0)
            for s, n in ((g_ready, 2), (rope_step, 1), (scored, 1), (exped, 4), (p_copied, 2), (o_stored, 4), (p_turned, 2), (attended, 2)):
                dve.sem_inc(s, n)
            dve.wait_ge(const_loaded, CONSTS_IN)
            dve.wait_ge(c_ready, 3)
            v.tensor_tensor(cparts[:, :, 2:4], csilu[:, :, :], cparts[:, :, 0:2].bitcast(F32), ALU.subtract)\
                .then_inc(c_ready, 1)
            v.tensor_scalar(small[:, 1, :], logit[:, :], -1.0, None, ALU.mult).then_inc(lg_step, 1)
            dve.wait_ge(lg_step, 1)
            v.tensor_tensor(small[:, 0, :], small[:, 1, :], logit[:, :], ALU.max).then_inc(lg_step, 1)
            v.tensor_scalar(qk_gain[:, :, 0:1], qk_gain[:, :, 0:1], NA_HD ** -0.5, None, ALU.mult)
            dve.wait_ge(lg_step, 4)
            v.scalar_tensor_tensor(log_gamma[:, :], logit[:, :], 0.0, small[:, 2, :], ALU.min, ALU.subtract)\
                .then_inc(lg_step, 1)
            dve.wait_ge(lg_step, 5)
            v.tensor_scalar(log_gamma[:, :], log_gamma[:, :], -1e-25, None, ALU.min).then_inc(lg_step, 1)
            for n in range(LEAD):
                split(Step(n - LEAD))
            for i in bodies(dve, 4):
                for quarter in range(4):
                    split(Step(quarter, 4, i))
                ada_rows(i, Step(3, 4, i))
                ada_store(i, 0, i)
            for layer, p in enumerate(layers):
                norm_apply(layer, 0)
                if layer % 3 == 0:
                    na(layer, p)
                elif layer % 3 == 1:
                    retention(p)
                else:
                    conv(p)
                if layer < DEPTH - 1:
                    first = p["ada"]
                    split(Step(first))
                    norm_apply(layer, 1, [
                        lambda: split(Step(first + 1)), lambda: split(Step(first + 2)),
                        lambda: split(Step(first + 3)), lambda: ada_rows(0, Step(first + 3)),
                        lambda: ada_store(ADA_SLICES * (layer + 1), layer + 1, 0)])
                else:
                    norm_apply(layer, 1)
                ffn(layer, p)


def _tile_groups(w, order=None):
    k, n = w.shape[0] // P, w.shape[1] // P
    tiles = w.reshape(k, P, n, P).transpose(2, 1, 0, 3)
    return tiles[order] if order is not None else tiles


def _whole(w, order=None):
    return _tile_groups(w, order).reshape(-1, P, GROUP)


def _slices(w):
    n = w.shape[1] // 512
    return w.reshape(4, 2, P, n, 512).transpose(3, 0, 2, 1, 4).reshape(n, 4, P, GROUP)


def _stream(a):
    ada = [_slices(a["ada_w"][layer]) for layer in range(DEPTH)]
    parts = [ada[0][0:4].reshape(-1, P, GROUP)]
    for layer in range(DEPTH):
        j = layer // 3
        if layer % 3 == 0:
            qkv = a["na_w_qkv"][j]
            qk = _whole(qkv[:, :2 * D])
            if layer == 0:
                rest = ada[0][4:].reshape(2 * C, 2, P, GROUP)
                qk = np.concatenate([qk[:, None], rest], axis=1).reshape(-1, P, GROUP)
            parts += [qk, _slices(qkv[:, 2 * D:]).reshape(-1, P, GROUP), _whole(a["na_w_o"][j])]
        elif layer % 3 == 1:
            o = a["ret_w_o"][j].reshape(2, D, D)
            o = np.stack([_whole(o[0]), _whole(o[1])], axis=1).reshape(-1, P, GROUP)
            parts += [_whole(a["ret_w_q"][j]), _whole(a["ret_w_k"][j]),
                      _slices(a["ret_w_v"][j]).reshape(-1, P, GROUP), _whole(a["ret_w_g"][j]), o]
        else:
            pw = _whole(a["cv_w_pw1"][j]).reshape(2, C, P, GROUP).transpose(1, 0, 2, 3)
            parts += [pw.reshape(-1, P, GROUP), _whole(a["cv_w_pw2"][j])]
        up = _whole(a["ffn_w_up"][layer]).reshape(2, FC, P, GROUP).transpose(1, 0, 2, 3).reshape(-1, P, GROUP)
        if layer < DEPTH - 1:
            parts.append(ada[layer + 1][0])
            rest = ada[layer + 1][1:].reshape(-1, P, GROUP)
            up = np.stack([rest, up], axis=1).reshape(-1, P, GROUP)
        parts.append(up)
        down = _tile_groups(a["ffn_w_down"][layer])
        down = np.pad(down, ((0, 0), (0, 0), (0, 24 - FC), (0, 0)))
        parts.append(down.reshape(C, P, 3, GROUP).transpose(0, 2, 1, 3).reshape(-1, P, GROUP))
    return np.concatenate(parts)


def _per_feature(v):
    v = v.reshape(v.shape[:-1] + (-1, P))
    return np.moveaxis(v, -1, 0)


def _constants():
    col = np.arange(GRID_W)
    start = np.clip(col - NA_KW // 2, 0, GRID_W - NA_KW)
    inside = (col[None, :] >= start[:, None]) & (col[None, :] < start[:, None] + NA_KW)
    na_mask = np.tile(np.where(inside, 0.0, -FAR), (2, 1)).astype(np.float32)

    t = np.arange(SEQ)
    n_freq = RET_QK // 4
    inv = np.power(np.float32(10000.0), -np.arange(n_freq, dtype=np.float32) / np.float32(n_freq)).astype(np.float32)
    ang = np.concatenate([(t // GRID_W).astype(np.float32)[None, :] * inv[:, None],
                          (t % GRID_W).astype(np.float32)[None, :] * inv[:, None]])
    rope = np.stack([np.cos(ang), np.sin(ang)], axis=1).astype(np.float32)

    p, u = np.arange(P)[:, None], np.arange(DIST_W)[None, :]
    ahead, back = u - P - p, p + 3 * P - u
    dist = np.stack([np.where(ahead >= 0, ahead, FAR), np.where(back >= 0, back, FAR)], axis=1).astype(np.float32)

    head = np.arange(P) // NA_HD
    return {
        "na_mask": na_mask, "rope": rope, "dist": dist,
        "ones": np.ones((P, P), np.float32),
        "head_ones": (head[:, None] == head[None, :]).astype(np.float32),
        "identity": np.eye(P, dtype=np.float32),
        "pick": np.tile(np.eye(2, dtype=np.float32), (2, 1)),
    }


def kernel(**inputs):
    import concourse.bacc as bacc
    from concourse.bass_utils import run_bass_kernel_spmd

    a = {k: np.asarray(v) for k, v in inputs.items()}
    tokens = np.concatenate([a["ctx"][0], a["x"][0]])
    arrays = {
        "x": _per_feature(tokens).transpose(0, 2, 1),
        "weights": _stream(a),
        "ada_in": _per_feature(np.stack([a["c_ctx"], a["c"][0]])).transpose(0, 2, 1),
        "ada_bias": _per_feature(a["ada_b"]),
        "gain": _per_feature(np.stack([a["norm_mix"], a["norm_ffn"]], axis=1)),
        "na_gain": np.tile(np.stack([a["na_q_gain"], a["na_k_gain"]], axis=1), (1, 1, 2)).transpose(2, 0, 1),
        "rpb": a["na_rpb"][..., ::-1],
        "decay": np.broadcast_to(a["ret_decay_logit"][0].reshape(1, -1), (P, 2 * RET_HEADS)),
        "gn_gain": _per_feature(a["ret_gn_gain"][0]),
        "cv_bias": _per_feature(np.stack([a["cv_b_pw1"][0, :D], a["cv_b_pw1"][0, D:], a["cv_b_dw"][0],
                                          a["cv_ln_g"][0], a["cv_ln_b"][0], a["cv_b_pw2"][0]])),
        "cv_filter": _per_feature(a["cv_w_dw"][0]).transpose(0, 2, 1),
        "ffn_filter": _per_feature(np.concatenate([a["ffn_w_dw"], a["ffn_b_dw"][:, None]], axis=1))
        .transpose(0, 1, 3, 2),
        **_constants(),
    }
    arrays = {k: np.ascontiguousarray(v) for k, v in arrays.items()}
    nc = bacc.Bacc("TRN2", target_bir_lowering=False, num_devices=1)
    aps = {k: nc.dram_tensor(f"in_{k}", v.shape, mybir.dt.from_np(v.dtype), kind="ExternalInput").ap()
           for k, v in arrays.items()}
    out = nc.dram_tensor("out_y", (P, C, SEQ), F32, kind="ExternalOutput").ap()
    build(nc, out=out, **aps)
    run = run_bass_kernel_spmd(nc, [{f"in_{k}": v for k, v in arrays.items()}], core_ids=[0])
    y = run.results[0]["out_y"]
    return np.ascontiguousarray(y.transpose(2, 1, 0)).reshape(1, SEQ, D)
```

```python
from contextlib import ExitStack

import numpy as np

import concourse.bass as bass
from concourse import mybir

F32 = mybir.dt.float32
F32R = mybir.dt.float32r
ALU = mybir.AluOpType
ACT = mybir.ActivationFunctionType
AX = mybir.AxisListType.X

P = 128
D = 1024
C = D // P
CTX = 256
SEQ = 256
T = CTX + SEQ
TB = T // P
DEPTH = 4
GRID_W = 64
EPS = 1e-6
ALL = slice(0, T)
CT = slice(0, CTX)
XT = slice(CTX, T)

NA_HEADS = 16
NA_HD = D // NA_HEADS
NA_KH = 8
NA_KW = 16
RPB_H = 2 * NA_KH - 1
RPB_W = 2 * NA_KW - 1
ROWS = SEQ // GRID_W

RET_HEADS = 4
RET_QK = D // RET_HEADS
RET_V = 2 * D // RET_HEADS
RET_VC = 2 * D // P
DIST_W = 5 * P

CONV_W = 31
POOL_TAPS = 14
FFN_H = 2816
FC = FFN_H // P
DOWN = (8, 8, 6)

SLOTS = 4
LEAD = 3
GROUP = 8 * P
ADA_SLICES = 6 * D // 512
FAR = 1e30


class Step:

    def __init__(self, first, per=0, i=0):
        self.first, self.per, self.i = first, per, i
        self.slot = first % SLOTS
        self.n = first + per * i
        self.lap = first // SLOTS + (per // SLOTS) * i

    def ahead(self, k):
        return Step(self.first + k, self.per, self.i)


def plan():
    group, tile, ready = 0, 0, 0
    layers = []
    for layer in range(DEPTH):
        p = {"mix": group, "mix_tile": tile, "mix_ready": ready}
        ready += C
        if layer % 3 == 0:
            p["qk_per"], p["o_per"] = (8, 12) if layer == 0 else (4, 4)
            p["v"] = group + 4 * p["qk_per"]
            p["o"] = p["v"] + 8
            p["o_ready"] = ready
            ready += C
            group, tile = p["o"] + 2 * p["o_per"], tile + 32
        elif layer % 3 == 1:
            p["v"] = group + 16
            p["g"] = p["v"] + 16
            p["o"] = p["g"] + 16
            group, tile = p["o"] + 16, tile + 56
        else:
            p["o"] = group + 16
            p["o_ready"] = ready
            ready += C
            group, tile = p["o"] + 8, tile + 24
        p["ffn_ready"] = ready
        ready += C
        p["ada"] = group if layer < DEPTH - 1 else None
        p["up"] = group + (4 if layer < DEPTH - 1 else 0)
        p["up_per"] = 8 if layer < DEPTH - 1 else 4
        p["up_tile"] = tile
        p["down"] = p["up"] + FC // 2 * p["up_per"]
        p["down_tile"] = tile + 2 * FC
        group, tile = p["down"] + C * len(DOWN), tile + 2 * FC + C
        layers.append(p)
    return layers, group


def bodies(engine, count, unroll=False):
    if unroll:
        yield from range(count)
    else:
        with engine.Fori(0, count) as i:
            yield i


def build(nc, x, ada_first, weights, ada_in, ada_bias, gain, na_gain, rpb, na_mask, rope, decay, dist, gn_gain,
          cv_bias, cv_filter, ffn_filter, ones, head_ones, identity, pick, out):
    layers, n_groups = plan()
    ctx = ExitStack()
    with ctx:
        def sb(name, shape, dt=F32):
            return ctx.enter_context(nc.sbuf_tensor(name, shape, dt))

        def sem(name):
            return ctx.enter_context(nc.semaphore(name))

        X = sb("X", [P, C, T])
        Hhi = sb("Hhi", [P, C, T], F32R)
        Hlo = sb("Hlo", [P, C, T], F32R)
        Whi = sb("Whi", [P, SLOTS, GROUP], F32R)
        with nc.sbuf_tensor("raw", [P, SLOTS, GROUP], F32) as raw:
            pass
        Wlo = sb("Wlo", [P, SLOTS, GROUP], F32R)
        hb = sb("hb", [P, 2, T])
        total = sb("total", [P, T])
        square = sb("square", [P, 2, T])
        root = sb("root", [P, T])
        rstd = sb("rstd", [P, T])
        rows = sb("rows", [4, 512])
        mod = sb("mod", [P, 2, 6 * C, 2])
        scale = sb("scale", [P, 2, C, 2])
        cfull = sb("cfull", [P, C, 2])
        csilu = sb("csilu", [P, C, 2])
        cparts = sb("cparts", [P, C, 4], F32R)
        bias_ada = sb("bias_ada", [P, DEPTH, 6 * C])
        gains = sb("gains", [P, DEPTH, 2, C])
        qk_gain = sb("qk_gain", [P, 2, 2])
        mask = sb("mask", [P, GRID_W])
        cos_sin = sb("cos_sin", [P, 2, SEQ])
        logit = sb("logit", [P, 2 * RET_HEADS])
        small = sb("small", [P, 3, 2 * RET_HEADS])
        log_gamma = sb("log_gamma", [P, 2 * RET_HEADS])
        gn = sb("gn", [P, RET_VC])
        cvb = sb("cvb", [P, 6, C])
        cvf = sb("cvf", [P, C, CONV_W])
        fff = sb("fff", [P, DEPTH, FC, 4])
        one = sb("one", [P, P])
        one_head = sb("one_head", [P, P])
        ident = sb("ident", [P, P])
        picker = sb("picker", [4, 2])
        eps = sb("eps", [P, 1])
        peak = sb("peak", [P, 4])
        psum_p = sb("psum_p", [P, 4])
        rinv = sb("rinv", [P, 4])
        stats = sb("stats", [P, TB, 6])
        mv = sb("mv", [P, TB, 2])
        sd4 = sb("sd4", [P, TB])

        def region(*tensors):
            with ExitStack() as stack:
                return [stack.enter_context(nc.sbuf_tensor(n, s, dt)) for n, s, dt in tensors]

        ada_raw, = region(("ada_raw", [P, 16, GROUP], F32))
        Ghi, Glo, cv = region(("Ghi", [P, FC, T], F32R), ("Glo", [P, FC, T], F32R), ("cv", [P, 2, T], F32))
        QK, V, O, rel, prob, probT, Qz = region(
            ("QK", [P, 2 * C, T], F32), ("V", [P, TB, D], F32), ("O", [P, TB, D], F32),
            ("rel", [P, NA_HEADS, 6, GRID_W], F32), ("prob", [P, 2, T], F32), ("probT", [P, 2, T], F32),
            ("Qz", [P, 2, T], F32))
        _, rel_in = region(("na_qk", [P, 2 * C * T], F32), ("rel_in", [P, NA_HEADS * 6, GRID_W], F32))
        _, na_sq, na_root = region(("na_skip", [P, 2 * C * T + 2 * TB * D + NA_HEADS * 6 * GRID_W], F32),
                                   ("na_sq", [P, 2, T], F32), ("na_root", [P, 4, T], F32))
        QKr, Vr, On, decay_t = region(
            ("QKr", [P, 2 * C, T], F32), ("Vr", [P, TB, 2 * D], F32), ("On", [P, TB, 2 * D], F32),
            ("decay_t", [P, 2, DIST_W], F32))
        OT, Yhi, Ylo = region(("OT", [P, RET_VC, T], F32), ("Yhi", [P, RET_VC, T], F32R),
                              ("Ylo", [P, RET_VC, T], F32R))
        _, rope_t = region(("ret_skip", [P, 2 * C * T + 2 * TB * 2 * D], F32), ("rope_t", [P, 4, SEQ], F32))
        A = [hb[:, 0, :], square[:, 0, :], square[:, 1, :]]
        gated = [hb[:, 0, :], hb[:, 1, :], square[:, 0, :], square[:, 1, :]]
        U, odd, pooled, prods, Wc, glu_s, zeros = region(
            ("U", [P, 2, T], F32), ("odd", [P, 2, T], F32), ("pooled", [P, 2, T], F32), ("prods", [P, 4, T], F32),
            ("Wc", [P, C, T], F32), ("glu_s", [P, 2, T], F32), ("zeros", [P, T], F32))
        bank = [ctx.enter_context(nc.psum_tensor(f"bank{b}", [P, 512], F32)) for b in range(8)]

        ada_loaded = [sem(f"ada_loaded{s}") for s in range(4)]
        raw_loaded = [sem(f"raw_loaded{s}") for s in range(SLOTS)]
        const_loaded = sem("const_loaded")
        x_loaded = sem("x_loaded")
        hi_split = sem("hi_split")
        lo_split = sem("lo_split")
        weights_used = sem("weights_used")
        tile_free = sem("tile_free")
        c_loaded = sem("c_loaded")
        c_ready = sem("c_ready")
        lg_step = sem("lg_step")
        ada_rows_made = sem("ada_rows_made")
        rows_copied = sem("rows_copied")
        cols_made = sem("cols_made")
        mod_ready = sem("mod_ready")
        sum_step = sem("sum_step")
        norm_summed = sem("norm_summed")
        norm_root = sem("norm_root")
        norm_rstd = sem("norm_rstd")
        norm_scaled = sem("norm_scaled")
        h_hi = sem("h_hi")
        h_ready = sem("h_ready")
        qk_squared = sem("qk_squared")
        qk_summed = sem("qk_summed")
        qk_root = sem("qk_root")
        qk_rstd = sem("qk_rstd")
        rel_loaded = sem("rel_loaded")
        rel_ready = sem("rel_ready")
        qz_cleared = sem("qz_cleared")
        q_staged = sem("q_staged")
        scored = sem("scored")
        biased = sem("biased")
        peaked = sem("peaked")
        exped = sem("exped")
        p_turned = sem("p_turned")
        p_copied = sem("p_copied")
        attended = sem("attended")
        inverted = sem("inverted")
        o_stored = sem("o_stored")
        o_turned = sem("o_turned")
        rope_step = sem("rope_step")
        dist_loaded = sem("dist_loaded")
        decayed = sem("decayed")
        mask_made = sem("mask_made")
        ret_scored = sem("ret_scored")
        weighted = sem("weighted")
        ret_out = sem("ret_out")
        gn_stat = sem("gn_stat")
        gn_root = sem("gn_root")
        gn_rstd = sem("gn_rstd")
        gn_done = sem("gn_done")
        gn_turned = sem("gn_turned")
        ot_copied = sem("ot_copied")
        gate_silu = sem("gate_silu")
        y_made = sem("y_made")
        y_hi = sem("y_hi")
        glu_sigmoid = sem("glu_sigmoid")
        glu_made = sem("glu_made")
        tap_done = sem("tap_done")
        tap_made = sem("tap_made")
        tap_cleared = sem("tap_cleared")
        tap_pooled = sem("tap_pooled")
        ln_used = sem("ln_used")
        ln_stat = sem("ln_stat")
        ln_mean = sem("ln_mean")
        ln_centred = sem("ln_centred")
        ln_square = sem("ln_square")
        ln_scaled = sem("ln_scaled")
        ln_silu = sem("ln_silu")
        cv_y = sem("cv_y")
        ffn_tap = sem("ffn_tap")
        gelu_done = sem("gelu_done")
        g_hi = sem("g_hi")
        g_ready = sem("g_ready")
        out_stored = sem("out_stored")

        FREE0 = 4
        SCORED0 = 8
        mid = CONV_W // 2
        order = [mid] + [k for k in range(CONV_W) if k != mid]
        taps, pool_taps = order[:CONV_W - POOL_TAPS], order[CONV_W - POOL_TAPS:]
        TAP_STEPS = len(taps) + 2
        TAP_FREE = TAP_STEPS + 1

        def norm_tokens(layer, part):
            return XT if layer == DEPTH - 1 and part == 1 else ALL

        def halves(tok):
            return ((1, XT),) if tok == XT else ((0, CT), (1, XT))

        CONSTS = [(ada_bias, bias_ada), (gain, gains), (na_gain, qk_gain), (na_mask, mask),
                  (rope, cos_sin), (decay, logit), (gn_gain, gn), (cv_bias, cvb), (cv_filter, cvf),
                  (ffn_filter, fff), (ones, one), (head_ones, one_head), (identity, ident), (pick, picker)]
        CONSTS_IN = 16 * len(CONSTS)

        block = ctx.enter_context(nc.Block())

        @block.sync
        def _(sp):
            for s in range(4):
                for q in range(4):
                    sp.dma_start(ada_raw[:, 4 * s + q, :], ada_first[4 * s + q, :, :]).then_inc(ada_loaded[s], 16)
            for s in range(SLOTS):
                sp.dma_start(raw[:, s, :], weights[s, :, :]).then_inc(raw_loaded[s], 16)
            with sp.Fori(1, n_groups // SLOTS) as lap:
                for s in range(SLOTS):
                    sp.wait_ge(weights_used, SLOTS * lap + (s - SLOTS + 1))
                    sp.dma_start(raw[:, s, :], weights[SLOTS * lap + s, :, :]).then_inc(raw_loaded[s], 16)
            last = layers[-1]
            sp.wait_ge(tile_free, FREE0 + last["down_tile"] + C)
            sp.dma_start(out, X[:, :, XT]).then_inc(out_stored, 16)
            sp.wait_ge(out_stored, 16)

        @block.gpsimd
        def _(pool):
            g = nc.gpsimd

            def clear_total(r, tok):
                if r:
                    pool.wait_ge(norm_summed, r)
                g.memset(total[:, tok], 0.0).then_inc(sum_step, 1)

            def add_square(r, c, c_static, tok):
                first = r * (1 + 2 * C) + 1
                g.tensor_tensor(square[:, c_static % 2, tok], X[:, c, tok], X[:, c, tok], ALU.mult)\
                    .then_inc(sum_step, 1)
                pool.wait_ge(sum_step, first + 2 * c + 1)
                g.tensor_tensor(total[:, tok], total[:, tok], square[:, c_static % 2, tok], ALU.add)\
                    .then_inc(sum_step, 1)

            def after_residual(r, tile0, tok):
                clear_total(r, tok)
                for i in bodies(pool, 2):
                    for m in range(4):
                        pool.wait_ge(tile_free, FREE0 + tile0 + 1 + m + 4 * i)
                        add_square(r, 4 * i + m, m, tok)

            def pairs_staged(layer):
                j = layer // 3
                r = 2 * layer
                pool.wait_ge(norm_summed, r + 1)
                for par in range(2):
                    for a in range(6):
                        src = bass.AP(rpb.tensor, j * NA_HEADS * RPB_H * RPB_W + (a + 5 - par) * RPB_W - 48,
                                      [[1, GRID_W], [RPB_H * RPB_W, NA_HEADS], [1, GRID_W]])
                        dst = rel_in[:, :, :].rearrange("p (h a) k -> p h a k", a=6)
                        g.dma_start(dst[64 * par:64 * par + 64, :, a, :], src).then_inc(rel_loaded, 16)
                pool.wait_ge(rel_loaded, 16 * 12 * (j + 1))
                pool.wait_ge(const_loaded, CONSTS_IN)
                g.tensor_tensor(rel[:, :, :, :].rearrange("p h a k -> p (h a) k"),
                                rel_in[:, :, ::-1],
                                mask[:, None, :].to_broadcast([P, NA_HEADS * 6, GRID_W]), ALU.add)\
                    .then_inc(rel_ready, 1)
                pool.wait_ge(tile_free, FREE0 + layers[layer]["mix_tile"] + 24)
                g.memset(Qz[64:128, 0, :], 0.0).then_inc(qz_cleared, 1)
                g.memset(Qz[0:64, 1, :], 0.0).then_inc(qz_cleared, 1)
                tok, n_units, u0 = (XT, 4, 8 * C) if layer == DEPTH - 1 else (ALL, 8, 0)
                for i in bodies(pool, C):
                    for par in range(2):
                        pool.wait_ge(scored, SCORED0 + u0 - n_units + n_units // 2 * (par + 1) + n_units * i)
                        half = slice(64 * par, 64 * par + 64)
                        g.tensor_copy(Qz[half, par, tok], QK[half, i, tok]).then_inc(q_staged, 1)
                pool.wait_ge(q_staged, 2 * C * (j + 1))

            g.memset(eps[:, :], EPS).then_inc(c_ready, 1)
            pool.wait_ge(x_loaded, 16)
            clear_total(0, ALL)
            for c in range(C):
                add_square(0, c, c, ALL)

            for layer, p in enumerate(layers):
                r = 2 * layer
                if layer % 3 == 0:
                    pairs_staged(layer)
                    out_tile = p["mix_tile"] + 24
                elif layer % 3 == 1:
                    def add(dst, a0, b0):
                        return g.tensor_tensor(dst, decay_t[:, 0, a0:a0 + CTX], decay_t[:, 1, b0:b0 + CTX], ALU.add)

                    for h in range(RET_HEADS):
                        if h:
                            pool.wait_ge(mask_made, 6 * h)
                        else:
                            pool.wait_ge(rope_step, 17)
                        g.dma_start(decay_t[:, :, :], dist).then_inc(dist_loaded, 16)
                        pool.wait_ge(decayed, 2 * h + 2)
                        if h:
                            pool.wait_ge(ret_out, h)
                        add(A[0][:, CT], P, 3 * P).then_inc(mask_made, 1)
                        add(A[0][:, XT], 3 * P, P).then_inc(mask_made, 1)
                        add(A[1][:, CT], 0, 2 * P).then_inc(mask_made, 1)
                        add(A[1][:, XT], 2 * P, 0).then_inc(mask_made, 1)
                        add(A[2][:, 0:CTX], P, 3 * P).then_inc(mask_made, 1)
                        add(A[2][:, CTX:T], 0, 2 * P).then_inc(mask_made, 1)
                    out_tile = p["mix_tile"] + 48
                else:
                    g.memset(zeros[:, :], 0.0).then_inc(tap_cleared, 1)
                    pool.wait_ge(tap_cleared, 1)
                    for i in bodies(pool, 4):
                        for k in range(2):
                            c = 2 * i + k
                            pool.wait_ge(tap_done, TAP_STEPS * (c - 1) + TAP_FREE)
                            g.tensor_tensor(pooled[:, k, :], zeros[:, :], zeros[:, :], ALU.add).then_inc(tap_cleared, 1)
                            pool.wait_ge(tap_cleared, c + 2)
                            for n, tap in enumerate(pool_taps):
                                shift = tap - mid
                                lo, hi = max(0, -shift), min(CTX, CTX - shift)
                                ring = (POOL_TAPS * k + n) % 4
                                acc = pooled[:, k, :].rearrange("p (s n) -> p s n", s=2)[:, :, lo:hi]
                                made = prods[:, ring, :].rearrange("p (s n) -> p s n", s=2)[:, :, lo:hi]
                                pool.wait_ge(tap_made, POOL_TAPS * c + n + 1)
                                pool.wait_ge(tap_pooled, 4 + POOL_TAPS * c + n)
                                g.tensor_tensor(acc, acc, made, ALU.add).then_inc(tap_pooled, 1)
                    out_tile = p["mix_tile"] + 16
                after_residual(r + 1, out_tile, norm_tokens(layer, 1))
                if layer < DEPTH - 1:
                    after_residual(r + 2, p["down_tile"], ALL)

        @block.tensor
        def _(pe):
            t = nc.tensor

            def three(dst, st, w, hi, lo, start, stop):
                t.matmul(dst, Whi[:, st.slot, w], hi, start=start, stop=False)
                t.matmul(dst, Whi[:, st.slot, w], lo, start=False, stop=False)
                return t.matmul(dst, Wlo[:, st.slot, w], hi, start=False, stop=stop)

            def three_moving(dst, st, w, hi, lo, start, stop):
                t.matmul(dst, hi, Whi[:, st.slot, w], start=start, stop=False)
                t.matmul(dst, lo, Whi[:, st.slot, w], start=False, stop=False)
                return t.matmul(dst, hi, Wlo[:, st.slot, w], start=False, stop=stop)

            def tile(index, static, groups, hi, lo, tok, ready=None):
                pe.wait_ge(tile_free, index + 1)
                dst, k, count = bank[static % 4], 0, sum(n for _, n in groups)
                for st, n in groups:
                    pe.wait_ge(lo_split, st.n + 1)
                    for q in range(n):
                        if ready:
                            pe.wait_ge(ready[0], ready[1] + k + 1)
                        last = three(dst[:, tok], st, slice(P * q, P * q + P), hi[:, k, tok], lo[:, k, tok],
                                     k == 0, k == count - 1)
                        k += 1
                    last.then_inc(weights_used, 1)

            def ada(st, quarter):
                pe.wait_ge(lo_split, st.n + 1)
                for q in range(2):
                    k = 2 * quarter + q
                    w = slice(512 * q, 512 * q + 512)
                    t.matmul(bank[6][0:4, :], cparts[:, k, :], Whi[:, st.slot, w], start=k == 0, stop=False)
                    last = t.matmul(bank[6][0:4, :], cparts[:, k, :], Wlo[:, st.slot, w], start=False, stop=k == C - 1)
                last.then_inc(weights_used, 1)

            def ada_cols(index, n_rows=4):
                pe.wait_ge(rows_copied, index + 1)
                for q in range(4):
                    last = t.matmul(bank[7][:, 2 * q:2 * q + 2], rows[0:n_rows, P * q:P * q + P],
                                    picker[0:n_rows, :], start=True, stop=True)
                last.then_inc(cols_made, 1)

            def norm_sum(r, tok):
                pe.wait_ge(sum_step, (r + 1) * (1 + 2 * C))
                t.matmul(bank[4][:, tok], one[:, :], total[:, tok], start=True, stop=True).then_inc(norm_summed, 1)

            def tokens_major(first, per, count, tile0, V_slices):
                for i in bodies(pe, count):
                    for b in range(TB):
                        pe.wait_ge(tile_free, tile0 + b + 1 + TB * i)
                    for quarter in range(4):
                        st = Step(first + quarter, per, i)
                        pe.wait_ge(lo_split, st.n + 1)
                        for q in range(2):
                            k = 2 * quarter + q
                            for b in range(TB):
                                tk = slice(P * b, P * b + P)
                                last = three_moving(bank[b][:, :], st, slice(512 * q, 512 * q + 512),
                                                    Hhi[:, k, tk], Hlo[:, k, tk], k == 0, k == C - 1)
                        last.then_inc(weights_used, 1)

            def na(layer, p):
                j = layer // 3
                last_layer = layer == DEPTH - 1
                per = p["qk_per"]
                qk0 = 2 * C * j
                a0 = 4

                def head_sum(k_static, k, tok):
                    pe.wait_ge(qk_squared, qk0 + k + 1)
                    t.matmul(bank[4 + k_static % 2][:, tok], one_head[:, :], na_sq[:, k_static % 2, tok],
                             start=True, stop=True).then_inc(qk_summed, 1)

                stride = per // 4
                for part, tok in ((0, XT if last_layer else ALL), (1, ALL)):
                    for i in bodies(pe, 2):
                        for m in range(4):
                            k = 8 * part + m + 4 * i
                            st = Step(p["mix"] + 2 * per * part + stride * m, per, i)
                            if layer == 0:
                                ada(st, m)
                                st = st.ahead(1)
                            tile(p["mix_tile"] + k, m, [(st, C)], Hhi, Hlo, tok,
                                 (h_ready, p["mix_ready"]) if m == 0 else None)
                            if m:
                                head_sum(m - 1, k - 1, tok)
                        if layer == 0:
                            ada_cols(a0 + 2 * part + i)
                        head_sum(3, 8 * part + 3 + 4 * i, tok)
                tokens_major(p["v"], 4, 2, p["mix_tile"] + 16, None)

                n_units = 4 if last_layer else 8
                u0 = 0 if layer == 0 else 8 * C
                blocks = (2, 3) if last_layer else (0, 1, 2, 3)
                units = [(par, b) for par in range(2) for b in blocks]
                pe.wait_ge(tile_free, FREE0 + p["mix_tile"] + 24)
                if layer == 0:
                    pe.wait_ge(mod_ready, 8)

                def scores(i, u):
                    par, b = units[u]
                    keys = CT if b < 2 else ALL
                    if b == blocks[0]:
                        pe.wait_ge(q_staged, 2 * C * j + par + 1 + 2 * i)
                    pe.wait_ge(exped, u0 + u + 1 + n_units * i)
                    t.matmul(bank[u % 4][:, keys], Qz[:, par, P * b:P * b + P], QK[:, 8 + i, keys],
                             start=True, stop=True).then_inc(scored, 1)

                def turn(i, u):
                    par, b = units[u]
                    pe.wait_ge(exped, u0 + 4 + u + 1 + n_units * i)
                    pe.wait_ge(p_copied, u0 + u + 1 + n_units * i)
                    for kb in range(2 if b < 2 else 4):
                        last = t.transpose(bank[4 + u % 2][:, P * kb:P * kb + P], prob[:, u % 2, P * kb:P * kb + P],
                                           ident[:, :])
                    last.then_inc(p_turned, 1)

                def attend(i, u):
                    par, b = units[u]
                    pe.wait_ge(p_copied, u0 + 2 + u + 1 + n_units * i)
                    pe.wait_ge(o_stored, u0 + 2 + u + 1 + n_units * i)
                    n_keys = 2 if b < 2 else 4
                    for kb in range(n_keys):
                        last = t.matmul(bank[6 + u % 2][:, 0:NA_HD], probT[:, u % 2, P * kb:P * kb + P],
                                        V[:, kb, bass.ts(2 * i + par, NA_HD)], start=kb == 0, stop=kb == n_keys - 1)
                    last.then_inc(attended, 1)

                def pair(i, first):
                    for s in range(n_units):
                        scores(i, s)
                        if s >= 2:
                            turn(i, s - 2)
                        elif not first:
                            turn(i - 1, s - 2 + n_units)
                        if s >= 3:
                            attend(i, s - 3)
                        elif not first:
                            attend(i - 1, s - 3 + n_units)

                pair(0, True)
                with pe.Fori(1, C) as i:
                    pair(i, False)
                for s in range(3):
                    if s < 2:
                        turn(C - 1, s - 2 + n_units)
                    attend(C - 1, s - 3 + n_units)
                out_blocks = blocks
                pe.wait_ge(o_stored, u0 + 4 + n_units * C)
                for c in range(C):
                    if c >= 4:
                        pe.wait_ge(h_ready, p["o_ready"] + c - 3)
                    for b in out_blocks:
                        last = t.transpose(bank[c % 4][:, P * b:P * b + P], O[:, b, P * c:P * c + P], ident[:, :])
                    last.then_inc(o_turned, 1)
                tok = XT if last_layer else ALL
                per = p["o_per"]
                pe.wait_ge(h_ready, p["o_ready"] + C)
                for i in bodies(pe, 2):
                    for m in range(4):
                        st = Step(p["o"] + per // 4 * m, per, i)
                        if layer == 0:
                            for q in range(2):
                                ada(st.ahead(q), 2 * (m % 2) + q)
                            st = st.ahead(2)
                        tile(p["mix_tile"] + 24 + m + 4 * i, m, [(st, C)], Hhi, Hlo, tok)
                        if layer == 0 and m % 2:
                            ada_cols(8 + m // 2 + 2 * i)

            def retention(p):
                for i in bodies(pe, 4):
                    for m in range(4):
                        tile(p["mix_tile"] + m + 4 * i, m, [(Step(p["mix"] + m, 4, i), C)], Hhi, Hlo, ALL,
                             (h_ready, p["mix_ready"]) if m == 0 else None)
                tokens_major(p["v"], 4, 4, p["mix_tile"] + 16, None)
                pe.wait_ge(tile_free, FREE0 + p["mix_tile"] + 32)
                pe.wait_ge(rope_step, 17)

                def scores(h):
                    if h:
                        pe.wait_ge(weighted, 3 * h)
                    for kb in range(TB):
                        dst = bank[kb][:, :] if kb < 2 else bank[2][:, CTX * (kb - 2):CTX * (kb - 1)]
                        for d in range(2):
                            last = t.matmul(dst, QKr[:, C + 2 * h + d, P * kb:P * kb + P],
                                            QKr[:, 2 * h + d, ALL if kb < 2 else XT], start=d == 0, stop=d == 1)
                    last.then_inc(ret_scored, 1)

                def mix_values(h):
                    pe.wait_ge(weighted, 3 * h + 3)
                    for b in range(TB):
                        if h:
                            pe.wait_ge(gn_done, TB * (h - 1) + b + 1)
                        n_keys = 2 if b < 2 else 4
                        for kb in range(n_keys):
                            a = A[kb][:, P * b:P * b + P] if kb < 2 else \
                                A[2][:, CTX * (kb - 2) + P * (b - 2):CTX * (kb - 2) + P * (b - 1)]
                            last = t.matmul(bank[4 + b][:, :], a, Vr[:, kb, RET_V * h:RET_V * (h + 1)],
                                            start=kb == 0, stop=kb == n_keys - 1)
                    last.then_inc(ret_out, 1)

                scores(0)
                for h in range(RET_HEADS):
                    if h + 1 < RET_HEADS:
                        scores(h + 1)
                    mix_values(h)
                pe.wait_ge(gn_done, TB * RET_HEADS)
                for c in range(RET_VC):
                    if c >= 4:
                        pe.wait_ge(ot_copied, c - 3)
                    for b in range(TB):
                        last = t.transpose(bank[c % 4][:, P * b:P * b + P], On[:, b, P * c:P * c + P], ident[:, :])
                    last.then_inc(gn_turned, 1)
                pe.wait_ge(ot_copied, RET_VC)
                for i in bodies(pe, 4):
                    for m in range(4):
                        tile(p["mix_tile"] + 32 + m + 4 * i, m, [(Step(p["g"] + m, 4, i), C)], Hhi, Hlo, ALL)
                pe.wait_ge(tile_free, FREE0 + p["mix_tile"] + 48)
                for i in bodies(pe, 2):
                    for m in range(4):
                        tile(p["mix_tile"] + 48 + m + 4 * i, m,
                             [(Step(p["o"] + 2 * m, 8, i), 8), (Step(p["o"] + 2 * m + 1, 8, i), 8)], Yhi, Ylo, ALL)

            def conv(p):
                for i in bodies(pe, 4):
                    for m in range(4):
                        tile(p["mix_tile"] + m + 4 * i, m, [(Step(p["mix"] + m, 4, i), C)], Hhi, Hlo, ALL,
                             (h_ready, p["mix_ready"]) if m == 0 else None)
                for c in range(C):
                    pe.wait_ge(tap_done, TAP_FREE + TAP_STEPS * (c + 1))
                    last = t.matmul(bank[4][:, :], one[:, :], Wc[:, c, :], start=c == 0, stop=c == C - 1)
                last.then_inc(ln_stat, 1)
                for c in range(C):
                    pe.wait_ge(ln_square, c + 1)
                    t.matmul(bank[5][:, :], one[:, :], square[:, c % 2, :], start=c == 0, stop=c == C - 1)\
                        .then_inc(ln_used, 1)
                for i in bodies(pe, 2):
                    for m in range(4):
                        tile(p["mix_tile"] + 16 + m + 4 * i, m, [(Step(p["o"] + m, 4, i), C)], Hhi, Hlo, ALL,
                             (h_ready, p["o_ready"]) if m == 0 else None)

            def ffn(layer, p):
                last_layer = layer == DEPTH - 1
                tok = XT if last_layer else ALL
                per = p["up_per"]
                r = 2 * layer + 1
                if last_layer:
                    norm_sum(r, tok)
                else:
                    for quarter in range(4):
                        ada(Step(p["ada"] + quarter), quarter)
                        if quarter == 1:
                            norm_sum(r, tok)
                    ada_cols(ADA_SLICES * (layer + 1))
                for i in bodies(pe, FC // 2):
                    for m in range(4):
                        s = p["up"] + (2 * m if per == 8 else m)
                        if per == 8:
                            ada(Step(s, per, i), m)
                            s += 1
                        tile(p["up_tile"] + m + 4 * i, m, [(Step(s, per, i), C)], Hhi, Hlo, tok,
                             (h_ready, p["ffn_ready"]) if m == 0 else None)
                    if per == 8:
                        ada_cols(ADA_SLICES * (layer + 1) + 1 + i)
                per = 4 * len(DOWN)
                for i in bodies(pe, 2, last_layer):
                    for m in range(4):
                        tile(p["down_tile"] + m + 4 * i, m,
                             [(Step(p["down"] + 3 * m + q, per, i), DOWN[q]) for q in range(3)], Ghi, Glo, tok,
                             (g_ready, 2 + FC * layer) if m == 0 else None)

            pe.wait_ge(c_ready, 2)
            for s in range(4):
                if s >= 2:
                    pe.wait_ge(rows_copied, s - 1)
                pe.wait_ge(ada_loaded[s], 64)
                for k in range(C):
                    last = t.matmul(bank[5 + s % 2][0:2, :], csilu[:, k, :],
                                    ada_raw[:, 4 * s + k // 2, 512 * (k % 2):512 * (k % 2) + 512],
                                    start=k == 0, stop=k == C - 1)
                last.then_inc(ada_rows_made, 1)
                if s:
                    ada_cols(s - 1, 2)
            ada_cols(3, 2)
            pe.wait_ge(const_loaded, CONSTS_IN)
            pe.wait_ge(c_ready, 4)
            for layer, p in enumerate(layers):
                norm_sum(2 * layer, ALL)
                if layer % 3 == 0:
                    na(layer, p)
                elif layer % 3 == 1:
                    retention(p)
                else:
                    conv(p)
                ffn(layer, p)

        @block.scalar
        def _(act):
            a = nc.scalar

            def split(st):
                st = st.ahead(LEAD)
                if isinstance(st.n, int) and st.n >= n_groups:
                    return
                act.wait_ge(raw_loaded[st.slot], 16 * (st.lap + 1))
                a.activation(Whi[:, st.slot, :], raw[:, st.slot, :], ACT.Copy).then_inc(hi_split, 1)

            def norm_apply(layer, part, between=()):
                tok = norm_tokens(layer, part)
                r = 2 * layer + part
                act.wait_ge(norm_summed, r + 1)
                a.activation(root[:, tok], bank[4][:, tok], ACT.Sqrt, bias=eps[:, :], scale=1.0 / D)\
                    .then_inc(norm_root, 1)
                if between:
                    act.wait_ge(weights_used, between[-1].n + 1)
                    a.activation(rows[:, :], bank[6][0:4, :], ACT.Copy).then_inc(rows_copied, 1)
                k0 = C * r
                for c in range(C):
                    act.wait_ge(norm_scaled, k0 + c + 1)
                    for half, hs in halves(tok):
                        last = a.activation(Hhi[:, c, hs], hb[:, c % 2, hs], ACT.Identity,
                                            bias=mod[:, layer % 2, 3 * C * part + c, half:half + 1])
                    last.then_inc(h_hi, 1)
                    if c < len(between):
                        split(between[c])

            def na(layer, p):
                j = layer // 3
                last_layer = layer == DEPTH - 1
                per = p["qk_per"]
                qk0 = 2 * C * j

                def root_of(k_static, k, tok):
                    act.wait_ge(qk_summed, qk0 + k + 1)
                    a.activation(na_root[:, k_static % 4, tok], bank[4 + k_static % 2][:, tok], ACT.Sqrt,
                                 bias=eps[:, :], scale=1.0 / NA_HD).then_inc(qk_root, 1)

                a.preload_act_table(ACT.Sqrt)
                for part, tok in ((0, XT if last_layer else ALL), (1, ALL)):
                    for i in bodies(act, 2):
                        stride = per // 4
                        for m in range(4):
                            k = 8 * part + m + 4 * i
                            st = Step(p["mix"] + 2 * per * part + stride * m, per, i)
                            if stride == 2:
                                split(st)
                                st = st.ahead(1)
                            act.wait_ge(weights_used, st.n + 1)
                            a.activation(na_sq[:, m % 2, tok], bank[m][:, tok], ACT.Square).then_inc(qk_squared, 1)
                            split(st)
                            if m:
                                root_of(m - 1, k - 1, tok)
                        root_of(3, 8 * part + 3 + 4 * i, tok)
                for i in bodies(act, 2):
                    for quarter in range(4):
                        split(Step(p["v"] + quarter, 4, i))

                n_units = 4 if last_layer else 8
                u0 = 0 if layer == 0 else 8 * C
                blocks = (2, 3) if last_layer else (0, 1, 2, 3)
                units = [(par, b) for par in range(2) for b in blocks]
                a.preload_act_table(ACT.Exp)

                def copy_turned(i, u):
                    par, b = units[u]
                    keys = CT if b < 2 else ALL
                    act.wait_ge(p_turned, u0 + 2 + u + 1 + n_units * i)
                    act.wait_ge(attended, u0 + u + 1 + n_units * i)
                    a.activation(probT[:, u % 2, keys], bank[4 + u % 2][:, keys], ACT.Copy).then_inc(p_copied, 1)

                def exponentials(i, u):
                    par, b = units[u]
                    keys = CT if b < 2 else ALL
                    act.wait_ge(peaked, u0 + u + 1 + n_units * i)
                    act.wait_ge(p_turned, u0 + u + 1 + n_units * i)
                    act.wait_ge(o_stored, u0 + u + 1 + n_units * i)
                    a.activation(prob[:, u % 2, keys], bank[u % 4][:, keys], ACT.Exp, bias=peak[:, u % 4:u % 4 + 1],
                                 accum_out=psum_p[:, u % 4:u % 4 + 1]).then_inc(exped, 1)

                def pair(i, first):
                    for s in range(n_units):
                        if s >= 2:
                            copy_turned(i, s - 2)
                        elif not first:
                            copy_turned(i - 1, s - 2 + n_units)
                        exponentials(i, s)

                pair(0, True)
                with act.Fori(1, C) as i:
                    pair(i, False)
                for s in range(2):
                    copy_turned(C - 1, s - 2 + n_units)
                a.preload_act_table(ACT.Sqrt)
                tok = XT if last_layer else ALL
                for c in range(C):
                    act.wait_ge(o_turned, C * j + c + 1)
                    a.activation(Hhi[:, c, tok], bank[c % 4][:, tok], ACT.Copy).then_inc(h_hi, 1)
                per = p["o_per"]
                for i in bodies(act, 2):
                    for m in range(per):
                        split(Step(p["o"] + m, per, i))

            def retention(p):
                for i in bodies(act, 4):
                    for m in range(4):
                        split(Step(p["mix"] + m, 4, i))
                for i in bodies(act, 4):
                    for m in range(4):
                        split(Step(p["v"] + m, 4, i))
                act.wait_ge(lg_step, 6)

                def decays(h):
                    act.wait_ge(dist_loaded, 16 * (h + 1))
                    for way in range(2):
                        lg = log_gamma[:, RET_HEADS * way + h:RET_HEADS * way + h + 1]
                        a.activation(decay_t[:, way, :], decay_t[:, way, :], ACT.Exp, scale=lg).then_inc(decayed, 1)

                decays(0)
                for h in range(RET_HEADS):
                    if h + 1 < RET_HEADS:
                        decays(h + 1)
                    act.wait_ge(gn_stat, 2 * TB * (h + 1))
                    a.activation(sd4[:, :], mv[:, :, 1], ACT.Sqrt, bias=eps[:, :]).then_inc(gn_root, 1)
                for c in range(RET_VC):
                    act.wait_ge(gn_turned, c + 1)
                    a.activation(OT[:, c, :], bank[c % 4][:, :], ACT.Copy).then_inc(ot_copied, 1)
                a.preload_act_table(ACT.Silu)
                for i in bodies(act, 4):
                    for m in range(4):
                        st = Step(p["g"] + m, 4, i)
                        act.wait_ge(weights_used, st.n + 1)
                        a.activation(gated[m], bank[m][:, :], ACT.Silu).then_inc(gate_silu, 1)
                        split(st)
                        act.wait_ge(y_made, m + 1 + 4 * i)
                        a.activation(Yhi[:, m + 4 * i, :], gated[m], ACT.Copy).then_inc(y_hi, 1)
                a.preload_act_table(ACT.Sqrt)
                for i in bodies(act, 2):
                    for m in range(8):
                        split(Step(p["o"] + m, 8, i))

            def conv(p):
                a.preload_act_table(ACT.Sigmoid)
                for i in bodies(act, 4):
                    for k in range(2):
                        split(Step(p["mix"] + 2 * k, 4, i))
                        st = Step(p["mix"] + 2 * k + 1, 4, i)
                        act.wait_ge(weights_used, st.n + 1)
                        a.activation(glu_s[:, k, :], bank[2 * k + 1][:, :], ACT.Sigmoid,
                                     bias=cvb[:, 1, bass.ds(2 * i + k, 1)]).then_inc(glu_sigmoid, 1)
                        split(st)
                        c = 2 * i + k
                        act.wait_ge(tile_free, FREE0 + p["mix_tile"] + 2 * k + 1 + 4 * i)
                        for n, tap in enumerate(pool_taps):
                            shift = tap - mid
                            lo, hi = max(0, -shift), min(CTX, CTX - shift)
                            ring = (POOL_TAPS * k + n) % 4
                            act.wait_ge(tap_pooled, POOL_TAPS * c + n + 1)
                            a.activation(prods[:, ring, :].rearrange("p (s n) -> p s n", s=2)[:, :, lo:hi],
                                         U[:, k, :].rearrange("p (s n) -> p s n", s=2)[:, :, lo + shift:hi + shift],
                                         ACT.Identity, scale=cvf[:, bass.ds(c, 1), tap]).then_inc(tap_made, 1)
                a.preload_act_table(ACT.Sqrt)
                for c in range(C):
                    act.wait_ge(ln_centred, c + 1)
                    if c >= 2:
                        act.wait_ge(ln_used, c - 1)
                    a.activation(square[:, c % 2, :], Wc[:, c, :], ACT.Square).then_inc(ln_square, 1)
                act.wait_ge(ln_used, C)
                a.activation(root[:, :], bank[5][:, :], ACT.Sqrt, bias=eps[:, :], scale=1.0 / D).then_inc(ln_mean, 1)
                a.preload_act_table(ACT.Silu)
                for c in range(C):
                    act.wait_ge(ln_scaled, c + 1)
                    a.activation(hb[:, c % 2, :], hb[:, c % 2, :], ACT.Silu, bias=cvb[:, 4, c:c + 1],
                                 scale=cvb[:, 3, c:c + 1]).then_inc(ln_silu, 1)
                    act.wait_ge(ln_silu, c + 1)
                    a.activation(Hhi[:, c, :], hb[:, c % 2, :], ACT.Copy).then_inc(h_hi, 1)
                a.preload_act_table(ACT.Sqrt)
                for i in bodies(act, 2):
                    for m in range(4):
                        split(Step(p["o"] + m, 4, i))

            def ffn(layer, p):
                last_layer = layer == DEPTH - 1
                tok = XT if last_layer else ALL
                per = p["up_per"]
                a.preload_act_table(ACT.Gelu_apprx_tanh)
                for i in bodies(act, FC // 2):
                    for m in range(4):
                        s = p["up"] + (2 * m if per == 8 else m)
                        if per == 8:
                            split(Step(s, per, i))
                            s += 1
                        split(Step(s, per, i))
                        k = m // 2
                        act.wait_ge(tile_free, FREE0 + p["up_tile"] + m + 1 + 4 * i)
                        if m % 2 == 0:
                            a.activation(cv[:, k, tok], cv[:, k, tok], ACT.Gelu_apprx_tanh).then_inc(gelu_done, 1)
                        else:
                            a.activation(Ghi[:, k + 2 * i, tok], cv[:, k, tok], ACT.Copy).then_inc(g_hi, 1)
                per = 4 * len(DOWN)
                if not last_layer:
                    a.preload_act_table(ACT.Sqrt)
                for i in bodies(act, 2, last_layer):
                    for m in range(per):
                        split(Step(p["down"] + m, per, i))

            act.dma_start(cfull[:, :, :], ada_in).then_inc(c_loaded, 16)
            for src, dst in CONSTS:
                full = dst[tuple(slice(None) for _ in dst.shape)]
                act.dma_start(full, src).then_inc(const_loaded, 16)
            act.dma_start(X[:, :, :], x).then_inc(x_loaded, 16)
            act.wait_ge(c_loaded, 16)
            a.activation(csilu[:, :, :], cfull[:, :, :], ACT.Silu).then_inc(c_ready, 1)
            act.wait_ge(c_ready, 2)
            a.activation(cparts[:, :, 0:2], csilu[:, :, :], ACT.Copy).then_inc(c_ready, 1)
            act.wait_ge(lg_step, 2)
            a.activation(small[:, 1, :], small[:, 0, :], ACT.Exp, scale=-1.0).then_inc(lg_step, 1)
            act.wait_ge(lg_step, 3)
            a.activation(small[:, 2, :], small[:, 1, :], ACT.Ln, bias=1.0).then_inc(lg_step, 1)
            for n in range(LEAD):
                split(Step(n - LEAD))
            for layer, p in enumerate(layers):
                norm_apply(layer, 0)
                if layer % 3 == 0:
                    na(layer, p)
                elif layer % 3 == 1:
                    retention(p)
                else:
                    conv(p)
                if layer < DEPTH - 1:
                    split(Step(p["ada"]))
                    norm_apply(layer, 1, [Step(p["ada"] + q) for q in (1, 2, 3)])
                else:
                    norm_apply(layer, 1)
                ffn(layer, p)

        @block.vector
        def _(dve):
            v = nc.vector

            def split(st):
                st = st.ahead(LEAD)
                if isinstance(st.n, int) and st.n >= n_groups:
                    return
                dve.wait_ge(hi_split, st.n + 1)
                v.tensor_tensor(Wlo[:, st.slot, :], raw[:, st.slot, :], Whi[:, st.slot, :].bitcast(F32), ALU.subtract)\
                    .then_inc(lo_split, 1)

            def ada_rows(st):
                dve.wait_ge(weights_used, st.n + 1)
                v.tensor_copy(rows[:, :], bank[6][0:4, :]).then_inc(rows_copied, 1)

            def ada_store(index, layer, s):
                dve.wait_ge(cols_made, index + 1)
                v.tensor_tensor(mod[:, layer % 2, bass.ts(s, 4), :],
                                bank[7][:, 0:8].rearrange("p (q s) -> p q s", s=2),
                                bias_ada[:, layer, bass.ts(s, 4)].unsqueeze(2).to_broadcast([P, 4, 2]), ALU.add)\
                    .then_inc(mod_ready, 1)

            def norm_apply(layer, part, between=()):
                tok = norm_tokens(layer, part)
                r = 2 * layer + part
                if layer == 0:
                    dve.wait_ge(mod_ready, 12 if part else 4)
                else:
                    dve.wait_ge(mod_ready, ADA_SLICES * (layer + 1))
                v.scalar_tensor_tensor(scale[:, part, :, :], mod[:, layer % 2, C * (3 * part + 1):C * (3 * part + 2), :],
                                       1.0, gains[:, layer, part, :].unsqueeze(2).to_broadcast([P, C, 2]),
                                       ALU.add, ALU.mult)
                dve.wait_ge(norm_root, r + 1)
                v.reciprocal(rstd[:, tok], root[:, tok]).then_inc(norm_rstd, 1)
                dve.wait_ge(norm_rstd, r + 1)
                ready = layers[layer]["ffn_ready" if part else "mix_ready"]

                def low(c):
                    dve.wait_ge(h_hi, ready + c + 1)
                    for half, hs in halves(tok):
                        last = v.scalar_tensor_tensor(Hlo[:, c, hs], hb[:, c % 2, hs],
                                                      mod[:, layer % 2, 3 * C * part + c, half:half + 1],
                                                      Hhi[:, c, hs].bitcast(F32), ALU.add, ALU.subtract)
                    last.then_inc(h_ready, 1)

                for c in range(C):
                    if c >= 2:
                        dve.wait_ge(h_ready, ready + c - 1)
                    for half, hs in halves(tok):
                        last = v.scalar_tensor_tensor(hb[:, c % 2, hs], X[:, c, hs], scale[:, part, c, half:half + 1],
                                                      rstd[:, hs], ALU.mult, ALU.mult)
                    last.then_inc(norm_scaled, 1)
                    if c:
                        low(c - 1)
                    if c < len(between):
                        between[c]()
                low(C - 1)

            def residual(layer, part, src, m, tok, bias=None):
                for half, hs in halves(tok):
                    gate = mod[:, layer % 2, bass.ds(C * (3 * part + 2) + m, 1), half]
                    last = v.scalar_tensor_tensor(X[:, m, hs], src[:, hs], gate, X[:, m, hs], ALU.mult, ALU.add)
                last.then_inc(tile_free, 1)

            def projected(layer, first, stride, per, tok, unroll=False):
                part = 1 if stride == 3 else 0
                for i in bodies(dve, 2, unroll):
                    for m in range(4):
                        st = Step(first + stride * m, per, i)
                        for q in range(stride - 1):
                            split(st.ahead(q))
                        dve.wait_ge(weights_used, st.ahead(stride - 1).n + 1)
                        residual(layer, part, bank[m], m + 4 * i, tok)
                        split(st.ahead(stride - 1))

            def tokens_major(first, count, dst):
                for i in bodies(dve, count):
                    for quarter in range(3):
                        split(Step(first + quarter, 4, i))
                    st = Step(first + 3, 4, i)
                    dve.wait_ge(weights_used, st.n + 1)
                    for b in range(TB):
                        v.tensor_copy(dst[:, b, bass.ts(i, 512)], bank[b][:, :]).then_inc(tile_free, 1)
                    split(st)

            def na(layer, p):
                j = layer // 3
                last_layer = layer == DEPTH - 1
                per = p["qk_per"]
                qk0 = 2 * C * j
                for part, tok in ((0, XT if last_layer else ALL), (1, ALL)):
                    def normed(m, k, tok):
                        dve.wait_ge(qk_root, qk0 + k + 1)
                        v.reciprocal(na_root[:, m, tok], na_root[:, m, tok]).then_inc(qk_rstd, 1)
                        dve.wait_ge(qk_rstd, qk0 + k + 1)
                        v.scalar_tensor_tensor(QK[:, k, tok], bank[m][:, tok], qk_gain[:, j, part:part + 1],
                                               na_root[:, m, tok], ALU.mult, ALU.mult).then_inc(tile_free, 1)

                    for i in bodies(dve, 2):
                        stride = per // 4
                        for m in range(4):
                            k = 8 * part + m + 4 * i
                            st = Step(p["mix"] + 2 * per * part + stride * m, per, i)
                            if stride == 2:
                                split(st)
                                if m == 3:
                                    ada_rows(st)
                                st = st.ahead(1)
                            split(st)
                            if m:
                                normed(m - 1, k - 1, tok)
                        if layer == 0:
                            s = 4 + 2 * part + i
                            ada_store(s, 0, s)
                        normed(3, 8 * part + 3 + 4 * i, tok)
                dve.wait_ge(rel_ready, j + 1)
                tokens_major(p["v"], 2, V)

                n_units = 4 if last_layer else 8
                u0 = 0 if layer == 0 else 8 * C
                blocks = (2, 3) if last_layer else (0, 1, 2, 3)
                units = [(par, b) for par in range(2) for b in blocks]
                x_units = sum(b >= 2 for _, b in units)
                b0 = 0 if layer == 0 else 4 * C

                def peaks(i, u):
                    par, b = units[u]
                    keys = CT if b < 2 else ALL
                    dve.wait_ge(scored, SCORED0 + u0 + u + 1 + n_units * i)
                    if b >= 2:
                        a0 = 2 if b == 2 else 0
                        sx = bank[u % 4][:, XT].rearrange("p (r k) -> p r k", k=GRID_W)
                        v.tensor_tensor(sx, sx, rel[:, 2 * i + par, a0:a0 + 4, :], ALU.add).then_inc(biased, 1)
                        dve.wait_ge(biased, b0 + 2 * par + b - 1 + x_units * i)
                    v.tensor_reduce(peak[:, u % 4:u % 4 + 1], bank[u % 4][:, keys], axis=AX, op=ALU.max,
                                    negate=True).then_inc(peaked, 1)

                def store(i, u):
                    par, b = units[u]
                    dve.wait_ge(attended, u0 + 2 + u + 1 + n_units * i)
                    v.reciprocal(rinv[:, u % 4:u % 4 + 1], psum_p[:, u % 4:u % 4 + 1]).then_inc(inverted, 1)
                    dve.wait_ge(inverted, u0 + u + 1 + n_units * i)
                    v.tensor_scalar(O[:, b, bass.ts(2 * i + par, NA_HD)], bank[6 + u % 2][:, 0:NA_HD],
                                    rinv[:, u % 4:u % 4 + 1], None, ALU.mult).then_inc(o_stored, 1)

                def pair(i, first):
                    for s in range(n_units):
                        peaks(i, s)
                        if s >= 3:
                            store(i, s - 3)
                        elif not first:
                            store(i - 1, s - 3 + n_units)

                pair(0, True)
                with dve.Fori(1, C) as i:
                    pair(i, False)
                for s in range(3):
                    store(C - 1, s - 3 + n_units)
                tok = XT if last_layer else ALL
                for c in range(C):
                    dve.wait_ge(h_hi, p["o_ready"] + c + 1)
                    v.tensor_tensor(Hlo[:, c, tok], bank[c % 4][:, tok], Hhi[:, c, tok].bitcast(F32), ALU.subtract)\
                        .then_inc(h_ready, 1)
                if layer:
                    projected(layer, p["o"], 1, 4, tok)
                else:
                    for i in bodies(dve, 2):
                        for m in range(4):
                            st = Step(p["o"] + 3 * m, 12, i)
                            split(st)
                            split(st.ahead(1))
                            if m % 2:
                                ada_rows(st.ahead(1))
                            dve.wait_ge(weights_used, st.ahead(2).n + 1)
                            residual(layer, 0, bank[m], m + 4 * i, ALL)
                            split(st.ahead(2))
                            if m % 2:
                                s = 8 + m // 2 + 2 * i
                                ada_store(s, 0, s)

            def retention(p):
                cos, sin = cos_sin[:, 0, :], cos_sin[:, 1, :]
                for i in bodies(dve, 4):
                    for k in range(2):
                        split(Step(p["mix"] + 2 * k, 4, i))
                        st = Step(p["mix"] + 2 * k + 1, 4, i)
                        dve.wait_ge(weights_used, st.n + 1)
                        first, second = bank[2 * k], bank[2 * k + 1]
                        j = 2 * k + 4 * i
                        dve.wait_ge(rope_step, 2 * k + 1 + 4 * i)
                        v.tensor_tensor(rope_t[:, 0, :], first[:, XT], cos, ALU.mult)
                        v.tensor_tensor(rope_t[:, 1, :], first[:, XT], sin, ALU.mult)
                        v.tensor_copy(QKr[:, j, CT], first[:, CT]).then_inc(tile_free, 1)
                        v.tensor_tensor(rope_t[:, 2, :], second[:, XT], sin, ALU.mult)
                        v.tensor_tensor(rope_t[:, 3, :], second[:, XT], cos, ALU.mult)
                        v.tensor_copy(QKr[:, j + 1, CT], second[:, CT]).then_inc(tile_free, 1)
                        dve.wait_ge(tile_free, FREE0 + p["mix_tile"] + 2 * k + 2 + 4 * i)
                        v.tensor_tensor(QKr[:, j, XT], rope_t[:, 0, :], rope_t[:, 2, :], ALU.subtract)\
                            .then_inc(rope_step, 1)
                        v.tensor_tensor(QKr[:, j + 1, XT], rope_t[:, 1, :], rope_t[:, 3, :], ALU.add)\
                            .then_inc(rope_step, 1)
                        split(st)
                tokens_major(p["v"], 4, Vr)
                for h in range(RET_HEADS):
                    dve.wait_ge(ret_scored, h + 1)
                    dve.wait_ge(mask_made, 6 * (h + 1))
                    for b in range(3):
                        v.scalar_tensor_tensor(A[b], bank[b][:, :], RET_QK ** -0.5, A[b],
                                               ALU.mult, ALU.mult).then_inc(weighted, 1)
                    dve.wait_ge(ret_out, h + 1)
                    for b in range(TB):
                        v.bn_stats(stats[:, b, :], bank[4 + b][:, :]).then_inc(gn_stat, 1)
                    dve.wait_ge(gn_stat, 2 * TB * h + TB)
                    for b in range(TB):
                        v.bn_aggr(mv[:, b, :], stats[:, b, :]).then_inc(gn_stat, 1)
                    dve.wait_ge(gn_root, h + 1)
                    v.reciprocal(sd4[:, :], sd4[:, :]).then_inc(gn_rstd, 1)
                    dve.wait_ge(gn_rstd, h + 1)
                    for b in range(TB):
                        v.tensor_scalar(On[:, b, RET_V * h:RET_V * (h + 1)], bank[4 + b][:, :], mv[:, b, 0:1],
                                        sd4[:, b:b + 1], ALU.subtract, ALU.mult).then_inc(gn_done, 1)
                for i in bodies(dve, 4):
                    for m in range(4):
                        dve.wait_ge(gate_silu, m + 1 + 4 * i)
                        v.scalar_tensor_tensor(gated[m], OT[:, m + 4 * i, :], gn[:, bass.ds(m + 4 * i, 1)],
                                               gated[m], ALU.mult, ALU.mult).then_inc(y_made, 1)
                        dve.wait_ge(y_made, m + 1 + 4 * i)
                        split(Step(p["g"] + m, 4, i))
                        dve.wait_ge(y_hi, m + 1 + 4 * i)
                        v.tensor_tensor(Ylo[:, m + 4 * i, :], gated[m], Yhi[:, m + 4 * i, :].bitcast(F32),
                                        ALU.subtract).then_inc(tile_free, 1)
                projected(1, p["o"], 2, 8, ALL)

            def conv(p):
                u3 = U[:, :, :].rearrange("p k (s n) -> p k s n", s=2)
                w4 = Wc[:, :, :].rearrange("p c (s n) -> p c s n", s=2)
                z4 = odd[:, :, :].rearrange("p k (s n) -> p k s n", s=2)
                for i in bodies(dve, 4):
                    for k in range(2):
                        split(Step(p["mix"] + 2 * k, 4, i))
                        st = Step(p["mix"] + 2 * k + 1, 4, i)
                        c = 2 * i + k
                        dve.wait_ge(glu_sigmoid, c + 1)
                        v.scalar_tensor_tensor(U[:, k, :], bank[2 * k][:, :], cvb[:, 0, bass.ds(c, 1)], glu_s[:, k, :],
                                               ALU.add, ALU.mult).then_inc(tile_free, 1)
                        dve.wait_ge(tile_free, FREE0 + p["mix_tile"] + 2 * k + 1 + 4 * i)
                        dve.sem_inc(tile_free, 1)
                        split(st)
                        done = TAP_FREE + TAP_STEPS * c
                        for n, tap in enumerate(taps):
                            w = cvf[:, bass.ds(c, 1), tap]
                            shift = tap - mid
                            lo, hi = max(0, -shift), min(CTX, CTX - shift)
                            acc = w4[:, c, :, :] if n % 2 == 0 else z4[:, k, :, :]
                            src = u3[:, k, :, lo + shift:hi + shift]
                            if n == 0:
                                v.tensor_scalar(acc, src, w, cvb[:, 2, bass.ds(c, 1)], ALU.mult, ALU.add)\
                                    .then_inc(tap_done, 1)
                            elif n == 1:
                                v.memset(z4[:, k, :, 0:lo], 0.0)
                                v.tensor_scalar(acc[:, :, lo:hi], src, w, None, ALU.mult).then_inc(tap_done, 1)
                            else:
                                dve.wait_ge(tap_done, done + n - 1)
                                v.scalar_tensor_tensor(acc[:, :, lo:hi], src, w, acc[:, :, lo:hi], ALU.mult, ALU.add)\
                                    .then_inc(tap_done, 1)
                        dve.wait_ge(tap_done, done + len(taps))
                        v.tensor_tensor(Wc[:, c, :], Wc[:, c, :], odd[:, k, :], ALU.add).then_inc(tap_done, 1)
                        dve.wait_ge(tap_pooled, 4 + POOL_TAPS * (c + 1))
                        dve.wait_ge(tap_done, done + len(taps) + 1)
                        v.tensor_tensor(Wc[:, c, :], Wc[:, c, :], pooled[:, k, :], ALU.add).then_inc(tap_done, 1)
                dve.wait_ge(ln_stat, 1)
                v.tensor_scalar(rstd[:, :], bank[4][:, :], 1.0 / D, None, ALU.mult).then_inc(ln_mean, 1)
                dve.wait_ge(ln_mean, 1)
                for c in range(C):
                    v.tensor_tensor(Wc[:, c, :], Wc[:, c, :], rstd[:, :], ALU.subtract).then_inc(ln_centred, 1)
                dve.wait_ge(ln_centred, C)
                dve.wait_ge(ln_mean, 2)
                v.reciprocal(rstd[:, :], root[:, :]).then_inc(ln_mean, 1)
                dve.wait_ge(ln_mean, 3)

                def low(c):
                    dve.wait_ge(h_hi, p["o_ready"] + c + 1)
                    v.tensor_tensor(Hlo[:, c, :], hb[:, c % 2, :], Hhi[:, c, :].bitcast(F32), ALU.subtract)\
                        .then_inc(h_ready, 1)

                for c in range(C):
                    if c >= 2:
                        dve.wait_ge(h_ready, p["o_ready"] + c - 1)
                    v.tensor_tensor(hb[:, c % 2, :], Wc[:, c, :], rstd[:, :], ALU.mult).then_inc(ln_scaled, 1)
                    if c:
                        low(c - 1)
                low(C - 1)
                for i in bodies(dve, 2):
                    for m in range(4):
                        st = Step(p["o"] + m, 4, i)
                        c = m + 4 * i
                        dve.wait_ge(weights_used, st.n + 1)
                        dve.wait_ge(tile_free, FREE0 + p["mix_tile"] + 16 + c - 1)
                        v.tensor_scalar(glu_s[:, m % 2, :], bank[m][:, :], cvb[:, 5, bass.ds(c, 1)], None, ALU.add)\
                            .then_inc(cv_y, 1)
                        dve.wait_ge(cv_y, c + 1)
                        residual(2, 0, glu_s[:, m % 2, :], c, ALL)
                        split(st)

            def ffn(layer, p):
                last_layer = layer == DEPTH - 1
                tok = XT if last_layer else ALL
                s0 = 1 if last_layer else 0
                per = p["up_per"]
                for i in bodies(dve, FC // 2):
                    for m in range(4):
                        s = p["up"] + (2 * m if per == 8 else m)
                        if per == 8:
                            split(Step(s, per, i))
                            if m == 3:
                                ada_rows(Step(s, per, i))
                            s += 1
                        st = Step(s, per, i)
                        k, j = m // 2, m // 2 + 2 * i
                        dve.wait_ge(weights_used, st.n + 1)
                        if m % 2 == 0:
                            u3 = bank[m][:, :].rearrange("p (s n) -> p s n", s=2)[:, s0:2, :]
                            c3 = cv[:, k, :].rearrange("p (s n) -> p s n", s=2)[:, s0:2, :]
                            f = fff[:, layer, bass.ds(j, 1), :]
                            dve.wait_ge(g_ready, FC * layer + k + 1 + 2 * i)
                            v.tensor_scalar(c3, u3, f[:, 0, 1:2], f[:, 0, 3:4], ALU.mult, ALU.add).then_inc(ffn_tap, 1)
                            dve.wait_ge(ffn_tap, 2 * FC * layer + 2 * k + 1 + 4 * i)
                            v.scalar_tensor_tensor(c3[:, :, 1:], u3[:, :, :-1], f[:, 0, 0:1], c3[:, :, 1:],
                                                   ALU.mult, ALU.add).then_inc(ffn_tap, 1)
                            dve.wait_ge(ffn_tap, 2 * FC * layer + 2 * k + 2 + 4 * i)
                            v.scalar_tensor_tensor(c3[:, :, :-1], u3[:, :, 1:], f[:, 0, 2:3], c3[:, :, :-1],
                                                   ALU.mult, ALU.add).then_inc(tile_free, 1)
                            split(st)
                        else:
                            dve.wait_ge(gelu_done, FC * layer + k + 1 + 2 * i)
                            v.tensor_tensor(cv[:, k, tok], cv[:, k, tok], bank[m][:, tok], ALU.mult)\
                                .then_inc(tile_free, 1)
                            split(st)
                            dve.wait_ge(g_hi, FC * layer + k + 1 + 2 * i)
                            v.tensor_tensor(Glo[:, j, tok], cv[:, k, tok], Ghi[:, j, tok].bitcast(F32), ALU.subtract)\
                                .then_inc(g_ready, 1)
                    if per == 8:
                        ada_store(ADA_SLICES * (layer + 1) + 1 + i, layer + 1, 1 + i)
                projected(layer, p["down"], 3, 12, tok, last_layer)

            dve.sem_inc(tile_free, FREE0)
            for s, n in ((g_ready, 2), (rope_step, 1), (scored, SCORED0), (tap_done, TAP_FREE), (tap_pooled, 4), (exped, 4), (p_copied, 2), (o_stored, 4), (p_turned, 2), (attended, 2)):
                dve.sem_inc(s, n)
            dve.wait_ge(const_loaded, CONSTS_IN)
            for s in range(4):
                dve.wait_ge(ada_rows_made, s + 1)
                v.tensor_copy(rows[0:2, :], bank[5 + s % 2][0:2, :]).then_inc(rows_copied, 1)
                ada_store(s, 0, s)
            dve.wait_ge(c_ready, 3)
            v.tensor_tensor(cparts[:, :, 2:4], csilu[:, :, :], cparts[:, :, 0:2].bitcast(F32), ALU.subtract)\
                .then_inc(c_ready, 1)
            v.tensor_scalar(small[:, 1, :], logit[:, :], -1.0, None, ALU.mult).then_inc(lg_step, 1)
            dve.wait_ge(lg_step, 1)
            v.tensor_tensor(small[:, 0, :], small[:, 1, :], logit[:, :], ALU.max).then_inc(lg_step, 1)
            v.tensor_scalar(qk_gain[:, :, 0:1], qk_gain[:, :, 0:1], NA_HD ** -0.5, None, ALU.mult)
            dve.wait_ge(lg_step, 4)
            v.scalar_tensor_tensor(log_gamma[:, :], logit[:, :], 0.0, small[:, 2, :], ALU.min, ALU.subtract)\
                .then_inc(lg_step, 1)
            dve.wait_ge(lg_step, 5)
            v.tensor_scalar(log_gamma[:, :], log_gamma[:, :], -1e-25, None, ALU.min).then_inc(lg_step, 1)
            for n in range(LEAD):
                split(Step(n - LEAD))
            for layer, p in enumerate(layers):
                norm_apply(layer, 0)
                if layer % 3 == 0:
                    na(layer, p)
                elif layer % 3 == 1:
                    retention(p)
                else:
                    conv(p)
                if layer < DEPTH - 1:
                    first = p["ada"]
                    split(Step(first))
                    norm_apply(layer, 1, [
                        lambda: split(Step(first + 1)), lambda: ada_store(ADA_SLICES * (layer + 1), layer + 1, 0),
                        lambda: split(Step(first + 2)), lambda: split(Step(first + 3))])
                else:
                    norm_apply(layer, 1)
                ffn(layer, p)


def _tile_groups(w, order=None):
    k, n = w.shape[0] // P, w.shape[1] // P
    tiles = w.reshape(k, P, n, P).transpose(2, 1, 0, 3)
    return tiles[order] if order is not None else tiles


def _whole(w, order=None):
    return _tile_groups(w, order).reshape(-1, P, GROUP)


def _slices(w):
    n = w.shape[1] // 512
    return w.reshape(4, 2, P, n, 512).transpose(3, 0, 2, 1, 4).reshape(n, 4, P, GROUP)


def _stream(a):
    ada = [_slices(a["ada_w"][layer]) for layer in range(DEPTH)]
    parts = []
    for layer in range(DEPTH):
        j = layer // 3
        if layer % 3 == 0:
            qkv = a["na_w_qkv"][j]
            qk = _whole(qkv[:, :2 * D])
            o = _whole(a["na_w_o"][j])
            if layer == 0:
                with_qk, with_o = ada[0][4:8].reshape(2 * C, 1, P, GROUP), ada[0][8:12].reshape(C, 2, P, GROUP)
                qk = np.concatenate([with_qk, qk[:, None]], axis=1).reshape(-1, P, GROUP)
                o = np.concatenate([with_o, o[:, None]], axis=1).reshape(-1, P, GROUP)
            parts += [qk, _slices(qkv[:, 2 * D:]).reshape(-1, P, GROUP), o]
        elif layer % 3 == 1:
            o = a["ret_w_o"][j].reshape(2, D, D)
            o = np.stack([_whole(o[0]), _whole(o[1])], axis=1).reshape(-1, P, GROUP)
            parts += [_whole(a["ret_w_q"][j]), _whole(a["ret_w_k"][j]),
                      _slices(a["ret_w_v"][j]).reshape(-1, P, GROUP), _whole(a["ret_w_g"][j]), o]
        else:
            pw = _whole(a["cv_w_pw1"][j]).reshape(2, C, P, GROUP).transpose(1, 0, 2, 3)
            parts += [pw.reshape(-1, P, GROUP), _whole(a["cv_w_pw2"][j])]
        up = _whole(a["ffn_w_up"][layer]).reshape(2, FC, P, GROUP).transpose(1, 0, 2, 3).reshape(-1, P, GROUP)
        if layer < DEPTH - 1:
            parts.append(ada[layer + 1][0])
            rest = ada[layer + 1][1:].reshape(-1, P, GROUP)
            up = np.stack([rest, up], axis=1).reshape(-1, P, GROUP)
        parts.append(up)
        down = _tile_groups(a["ffn_w_down"][layer])
        down = np.pad(down, ((0, 0), (0, 0), (0, 24 - FC), (0, 0)))
        parts.append(down.reshape(C, P, 3, GROUP).transpose(0, 2, 1, 3).reshape(-1, P, GROUP))
    return np.concatenate(parts)


def _per_feature(v):
    v = v.reshape(v.shape[:-1] + (-1, P))
    return np.moveaxis(v, -1, 0)


def _constants():
    col = np.arange(GRID_W)
    start = np.clip(col - NA_KW // 2, 0, GRID_W - NA_KW)
    inside = (col[None, :] >= start[:, None]) & (col[None, :] < start[:, None] + NA_KW)
    na_mask = np.tile(np.where(inside, 0.0, -FAR), (2, 1)).astype(np.float32)

    t = np.arange(SEQ)
    n_freq = RET_QK // 4
    inv = np.power(np.float32(10000.0), -np.arange(n_freq, dtype=np.float32) / np.float32(n_freq)).astype(np.float32)
    ang = np.concatenate([(t // GRID_W).astype(np.float32)[None, :] * inv[:, None],
                          (t % GRID_W).astype(np.float32)[None, :] * inv[:, None]])
    rope = np.stack([np.cos(ang), np.sin(ang)], axis=1).astype(np.float32)

    p, u = np.arange(P)[:, None], np.arange(DIST_W)[None, :]
    ahead, back = u - P - p, p + 3 * P - u
    dist = np.stack([np.where(ahead >= 0, ahead, FAR), np.where(back >= 0, back, FAR)], axis=1).astype(np.float32)

    head = np.arange(P) // NA_HD
    return {
        "na_mask": na_mask, "rope": rope, "dist": dist,
        "ones": np.ones((P, P), np.float32),
        "head_ones": (head[:, None] == head[None, :]).astype(np.float32),
        "identity": np.eye(P, dtype=np.float32),
        "pick": np.tile(np.eye(2, dtype=np.float32), (2, 1)),
    }


def kernel(**inputs):
    import concourse.bacc as bacc
    from concourse.bass_utils import run_bass_kernel_spmd

    a = {k: np.asarray(v) for k, v in inputs.items()}
    tokens = np.concatenate([a["ctx"][0], a["x"][0]])
    arrays = {
        "x": _per_feature(tokens).transpose(0, 2, 1),
        "ada_first": _slices(a["ada_w"][0][:, :2 * D]).reshape(-1, P, GROUP),
        "weights": _stream(a),
        "ada_in": _per_feature(np.stack([a["c_ctx"], a["c"][0]])).transpose(0, 2, 1),
        "ada_bias": _per_feature(a["ada_b"]),
        "gain": _per_feature(np.stack([a["norm_mix"], a["norm_ffn"]], axis=1)),
        "na_gain": np.tile(np.stack([a["na_q_gain"], a["na_k_gain"]], axis=1), (1, 1, 2)).transpose(2, 0, 1),
        "rpb": a["na_rpb"][..., ::-1],
        "decay": np.broadcast_to(a["ret_decay_logit"][0].reshape(1, -1), (P, 2 * RET_HEADS)),
        "gn_gain": _per_feature(a["ret_gn_gain"][0]),
        "cv_bias": _per_feature(np.stack([a["cv_b_pw1"][0, :D], a["cv_b_pw1"][0, D:], a["cv_b_dw"][0],
                                          a["cv_ln_g"][0], a["cv_ln_b"][0], a["cv_b_pw2"][0]])),
        "cv_filter": _per_feature(a["cv_w_dw"][0]).transpose(0, 2, 1),
        "ffn_filter": _per_feature(np.concatenate([a["ffn_w_dw"], a["ffn_b_dw"][:, None]], axis=1))
        .transpose(0, 1, 3, 2),
        **_constants(),
    }
    arrays = {k: np.ascontiguousarray(v) for k, v in arrays.items()}
    nc = bacc.Bacc("TRN2", target_bir_lowering=False, num_devices=1)
    aps = {k: nc.dram_tensor(f"in_{k}", v.shape, mybir.dt.from_np(v.dtype), kind="ExternalInput").ap()
           for k, v in arrays.items()}
    out = nc.dram_tensor("out_y", (P, C, SEQ), F32, kind="ExternalOutput").ap()
    build(nc, out=out, **aps)
    run = run_bass_kernel_spmd(nc, [{f"in_{k}": v for k, v in arrays.items()}], core_ids=[0])
    y = run.results[0]["out_y"]
    return np.ascontiguousarray(y.transpose(2, 1, 0)).reshape(1, SEQ, D)
```

```python
from contextlib import ExitStack

import numpy as np

import concourse.bass as bass
from concourse import mybir

F32 = mybir.dt.float32
F32R = mybir.dt.float32r
ALU = mybir.AluOpType
ACT = mybir.ActivationFunctionType
AX = mybir.AxisListType.X

P = 128
D = 1024
C = D // P
CTX = 256
SEQ = 256
T = CTX + SEQ
TB = T // P
DEPTH = 4
GRID_W = 64
EPS = 1e-6
ALL = slice(0, T)
CT = slice(0, CTX)
XT = slice(CTX, T)

NA_HEADS = 16
NA_HD = D // NA_HEADS
NA_KH = 8
NA_KW = 16
RPB_H = 2 * NA_KH - 1
RPB_W = 2 * NA_KW - 1
ROWS = SEQ // GRID_W

RET_HEADS = 4
RET_QK = D // RET_HEADS
RET_V = 2 * D // RET_HEADS
RET_VC = 2 * D // P
DIST_W = 5 * P

CONV_W = 31
POOL_TAPS = 12
FFN_H = 2816
FC = FFN_H // P
DOWN = (8, 8, 6)

SLOTS = 4
LEAD = 3
GROUP = 8 * P
ADA_SLICES = 6 * D // 512
TILE_AT, ADA_AT = (0, 2, 5, 7), (1, 3, 4, 6)
V_BANKS = (6, 7, 0, 1), (2, 3, 4, 5)
FAR = 1e30


class Step:

    def __init__(self, first, per=0, i=0):
        self.first, self.per, self.i = first, per, i
        self.slot = first % SLOTS
        self.n = first + per * i
        self.lap = first // SLOTS + (per // SLOTS) * i

    def ahead(self, k):
        return Step(self.first + k, self.per, self.i)


def plan():
    group, tile, ready = 0, 0, 0
    layers = []
    for layer in range(DEPTH):
        p = {"mix": group, "mix_tile": tile, "mix_ready": ready}
        ready += C
        if layer % 3 == 0:
            p["qk_per"], p["o_per"] = (8, 12) if layer == 0 else (4, 4)
            p["v"] = group + 4 * p["qk_per"]
            p["o"] = p["v"] + 8
            p["o_ready"] = ready
            ready += C
            group, tile = p["o"] + 2 * p["o_per"], tile + 32
        elif layer % 3 == 1:
            p["v"] = group + 16
            p["g"] = p["v"] + 16
            p["o"] = p["g"] + 16
            group, tile = p["o"] + 16, tile + 56
        else:
            p["first_ada"] = group
            p["mix"] = group + 4
            p["last_ada"] = p["mix"] + 6 * C
            p["o"] = p["last_ada"] + 8
            p["o_ready"] = ready
            ready += C
            group, tile = p["o"] + 8, tile + 24
        p["ffn_ready"] = ready
        ready += C
        p["ada"] = group if layer < DEPTH - 1 else None
        p["up"] = group + (4 if layer < DEPTH - 1 else 0)
        p["ada_index"] = ADA_SLICES * (layer + 1) + (ADA_SLICES - 1 if layer % 3 == 2 else 0)
        p["up_per"] = 8 if layer < DEPTH - 1 and layer % 3 < 2 else 4
        p["up_tile"] = tile
        p["down"] = p["up"] + FC // 2 * p["up_per"]
        p["down_tile"] = tile + 2 * FC
        group, tile = p["down"] + C * len(DOWN), tile + 2 * FC + C
        layers.append(p)
    return layers, group


def bodies(engine, count, unroll=False):
    if unroll:
        yield from range(count)
    else:
        with engine.Fori(0, count) as i:
            yield i


def peeled(engine, count):
    yield 0, True
    if count > 1:
        with engine.Fori(1, count) as i:
            yield i, False


def build(nc, x, ada_first, weights, ada_in, ada_bias, gain, na_gain, rpb, na_mask, rope, decay, dist, gn_gain,
          cv_bias, cv_filter, ffn_filter, ones, head_ones, identity, pick, out):
    layers, n_groups = plan()
    ctx = ExitStack()
    with ctx:
        def sb(name, shape, dt=F32):
            return ctx.enter_context(nc.sbuf_tensor(name, shape, dt))

        def sem(name):
            return ctx.enter_context(nc.semaphore(name))

        X = sb("X", [P, C, T])
        Hhi = sb("Hhi", [P, C, T], F32R)
        Hlo = sb("Hlo", [P, C, T], F32R)
        Whi = sb("Whi", [P, SLOTS, GROUP], F32R)
        with nc.sbuf_tensor("raw", [P, SLOTS, GROUP], F32) as raw:
            pass
        Wlo = sb("Wlo", [P, SLOTS, GROUP], F32R)
        hb = sb("hb", [P, 2, T])
        total = sb("total", [P, T])
        square = sb("square", [P, 2, T])
        root = sb("root", [P, T])
        last_square = root
        diagonal = root
        token_root = sb("token_root", [P, 2 * TB])
        rstd = sb("rstd", [P, T])
        rows = sb("rows", [4, 512])
        mod = sb("mod", [P, 2, 6 * C, 2])
        scale = sb("scale", [P, 2, C, 2])
        cfull = sb("cfull", [P, C, 2])
        csilu = sb("csilu", [P, C, 2])
        cparts = sb("cparts", [P, C, 4], F32R)
        bias_ada = sb("bias_ada", [P, DEPTH, 6 * C])
        gains = sb("gains", [P, DEPTH, 2, C])
        qk_gain = sb("qk_gain", [P, 2, 2])
        mask = sb("mask", [P, GRID_W])
        cos_sin = sb("cos_sin", [P, 2, SEQ])
        logit = sb("logit", [P, 2 * RET_HEADS])
        small = sb("small", [P, 3, 2 * RET_HEADS])
        log_gamma = sb("log_gamma", [P, 2 * RET_HEADS])
        gn = sb("gn", [P, RET_VC])
        cvb = sb("cvb", [P, 6, C])
        cvf = sb("cvf", [P, C, CONV_W])
        fff = sb("fff", [P, DEPTH, FC, 4])
        one = sb("one", [P, P])
        one_head = sb("one_head", [P, P])
        ident = sb("ident", [P, P])
        picker = sb("picker", [4, 2])
        eps = sb("eps", [P, 1])
        peak = sb("peak", [P, 4])
        psum_p = sb("psum_p", [P, 4])
        rinv = sb("rinv", [P, 4])
        stats = sb("stats", [P, TB, 6])
        mv = sb("mv", [P, TB, 2])
        sd4 = sb("sd4", [P, TB])

        def region(*tensors):
            with ExitStack() as stack:
                return [stack.enter_context(nc.sbuf_tensor(n, s, dt)) for n, s, dt in tensors]

        ada_raw, = region(("ada_raw", [P, 16, GROUP], F32))
        Ghi, Glo, cv = region(("Ghi", [P, FC, T], F32R), ("Glo", [P, FC, T], F32R), ("cv", [P, 2, T], F32))
        QK, V, O, rel, prob, probT, Qz = region(
            ("QK", [P, 2 * C, T], F32), ("V", [P, TB, D], F32), ("O", [P, TB, D], F32),
            ("rel", [P, NA_HEADS, 6, GRID_W], F32), ("prob", [P, 2, T], F32), ("probT", [P, 2, T], F32),
            ("Qz", [P, 2, T], F32))
        _, rel_in = region(("na_qk", [P, 2 * C * T], F32), ("rel_in", [P, NA_HEADS * 6, GRID_W], F32))
        _, na_sq, na_root = region(("na_skip", [P, 2 * C * T + 2 * TB * D + NA_HEADS * 6 * GRID_W], F32),
                                   ("na_sq", [P, 2, T], F32), ("na_root", [P, 4, T], F32))
        QKr, Vr, On, decay_t = region(
            ("QKr", [P, 2 * C, T], F32), ("Vr", [P, TB, 2 * D], F32), ("On", [P, TB, 2 * D], F32),
            ("decay_t", [P, 2, DIST_W], F32))
        OT, Yhi, Ylo = region(("OT", [P, RET_VC, T], F32), ("Yhi", [P, RET_VC, T], F32R),
                              ("Ylo", [P, RET_VC, T], F32R))
        _, rope_t = region(("ret_skip", [P, 2 * C * T + 2 * TB * 2 * D], F32), ("rope_t", [P, 4, SEQ], F32))
        A = [hb[:, 0, :], square[:, 0, :], square[:, 1, :]]
        ring = [hb[:, 0, :], hb[:, 1, :], square[:, 0, :], square[:, 1, :]]
        U, odd, pooled, prods, Wc, glu_s, zeros = region(
            ("U", [P, 2, T], F32), ("odd", [P, 2, T], F32), ("pooled", [P, 2, T], F32), ("prods", [P, 4, T], F32),
            ("Wc", [P, C, T], F32), ("glu_s", [P, 2, T], F32), ("zeros", [P, T], F32))
        bank = [ctx.enter_context(nc.psum_tensor(f"bank{b}", [P, 512], F32)) for b in range(8)]

        ada_loaded = [sem(f"ada_loaded{s}") for s in range(16)]
        raw_loaded = [sem(f"raw_loaded{s}") for s in range(SLOTS)]
        first_loaded = sem("first_loaded")
        const_loaded = sem("const_loaded")
        x_loaded = sem("x_loaded")
        hi_split = sem("hi_split")
        lo_split = sem("lo_split")
        weights_used = sem("weights_used")
        tile_free = sem("tile_free")
        c_loaded = sem("c_loaded")
        c_ready = sem("c_ready")
        lg_step = sem("lg_step")
        ada_rows_made = sem("ada_rows_made")
        rows_copied = sem("rows_copied")
        cols_made = sem("cols_made")
        mod_ready = sem("mod_ready")
        sum_step = sem("sum_step")
        last_squared = sem("last_squared")
        norm_summed = sem("norm_summed")
        norm_root = sem("norm_root")
        token_rstd = sem("token_rstd")
        norm_diagonal = sem("norm_diagonal")
        norm_rstd = sem("norm_rstd")
        scale_ready = sem("scale_ready")
        norm_scaled = sem("norm_scaled")
        h_hi = sem("h_hi")
        h_ready = sem("h_ready")
        qk_squared = sem("qk_squared")
        qk_summed = sem("qk_summed")
        qk_root = sem("qk_root")
        qk_rstd = sem("qk_rstd")
        rel_loaded = sem("rel_loaded")
        rel_ready = sem("rel_ready")
        qz_cleared = sem("qz_cleared")
        q_staged = sem("q_staged")
        scored = sem("scored")
        biased = sem("biased")
        peaked = sem("peaked")
        exped = sem("exped")
        p_turned = sem("p_turned")
        p_copied = sem("p_copied")
        attended = sem("attended")
        inverted = sem("inverted")
        o_stored = sem("o_stored")
        o_turned = sem("o_turned")
        rope_step = sem("rope_step")
        dist_loaded = sem("dist_loaded")
        decayed = sem("decayed")
        mask_made = sem("mask_made")
        ret_scored = sem("ret_scored")
        weighted = sem("weighted")
        ret_out = sem("ret_out")
        gn_stat = sem("gn_stat")
        gn_root = sem("gn_root")
        gn_rstd = sem("gn_rstd")
        gn_done = sem("gn_done")
        gn_turned = sem("gn_turned")
        ot_copied = sem("ot_copied")
        gate_silu = sem("gate_silu")
        y_made = sem("y_made")
        y_hi = sem("y_hi")
        glu_sigmoid = sem("glu_sigmoid")
        tap_done = sem("tap_done")
        tap_made = sem("tap_made")
        tap_cleared = sem("tap_cleared")
        tap_pooled = sem("tap_pooled")
        ln_used = sem("ln_used")
        ln_stat = sem("ln_stat")
        ln_mean = sem("ln_mean")
        ln_centred = sem("ln_centred")
        ln_square = sem("ln_square")
        ln_scaled = sem("ln_scaled")
        ln_silu = sem("ln_silu")
        cv_y = sem("cv_y")
        ffn_tap = sem("ffn_tap")
        gelu_done = sem("gelu_done")
        g_hi = sem("g_hi")
        g_ready = sem("g_ready")
        out_stored = sem("out_stored")

        FREE0 = 4
        SCORED0 = 8
        mid = CONV_W // 2
        order = [mid] + [k for k in range(CONV_W) if k != mid]
        taps, pool_taps = order[:CONV_W - POOL_TAPS], order[CONV_W - POOL_TAPS:]
        TAP_STEPS = len(taps) + 2
        SUM_STEPS = 1 + 2 * (C - 1)
        TAP_FREE = TAP_STEPS + 1

        def norm_tokens(layer, part):
            return XT if layer == DEPTH - 1 and part == 1 else ALL

        def residual_end(r):
            p = layers[r // 2]
            return p["up_tile"] if r % 2 else p["mix_tile"]

        def token_blocks(tok):
            return (2, 3) if tok == XT else (0, 1, 2, 3)

        def halves(tok):
            return ((1, XT),) if tok == XT else ((0, CT), (1, XT))

        FIRST_CONSTS = [(ada_bias, bias_ada), (pick, picker), (ones, one), (identity, ident)]
        CONSTS = [(gain, gains), (na_gain, qk_gain), (na_mask, mask),
                  (rope, cos_sin), (decay, logit), (gn_gain, gn), (cv_bias, cvb), (cv_filter, cvf),
                  (ffn_filter, fff), (head_ones, one_head)]
        CONSTS_IN = 16 * len(CONSTS)

        block = ctx.enter_context(nc.Block())

        @block.sync
        def _(sp):
            for src, dst in FIRST_CONSTS:
                full = dst[tuple(slice(None) for _ in dst.shape)]
                sp.dma_start(full, src).then_inc(first_loaded, 16)
            for q in range(16):
                sp.dma_start(ada_raw[:, q, :], ada_first[q, :, :]).then_inc(ada_loaded[q], 16)
            for s in range(SLOTS):
                sp.dma_start(raw[:, s, :], weights[s, :, :]).then_inc(raw_loaded[s], 16)
            with sp.Fori(1, n_groups // SLOTS) as lap:
                for s in range(SLOTS):
                    sp.wait_ge(weights_used, SLOTS * lap + (s - SLOTS + 1))
                    sp.dma_start(raw[:, s, :], weights[SLOTS * lap + s, :, :]).then_inc(raw_loaded[s], 16)
            last = layers[-1]
            sp.wait_ge(tile_free, FREE0 + last["down_tile"] + C)
            sp.dma_start(out, X[:, :, XT]).then_inc(out_stored, 16)
            sp.wait_ge(out_stored, 16)

        @block.gpsimd
        def _(pool):
            g = nc.gpsimd

            def clear_total(r, tok):
                if r:
                    pool.wait_ge(norm_summed, r)
                g.memset(total[:, tok], 0.0).then_inc(sum_step, 1)

            def add_square(r, c, c_static, tok):
                first = r * SUM_STEPS + 1
                g.tensor_tensor(square[:, c_static % 2, tok], X[:, c, tok], X[:, c, tok], ALU.mult)\
                    .then_inc(sum_step, 1)
                pool.wait_ge(sum_step, first + 2 * c + 1)
                g.tensor_tensor(total[:, tok], total[:, tok], square[:, c_static % 2, tok], ALU.add)\
                    .then_inc(sum_step, 1)

            def after_residual(r, tile0, tok):
                clear_total(r, tok)
                for c in range(C - 1):
                    pool.wait_ge(tile_free, FREE0 + tile0 + 1 + c)
                    add_square(r, c, c, tok)

            def pairs_staged(layer):
                j = layer // 3
                r = 2 * layer
                pool.wait_ge(norm_summed, r + 1)
                pool.wait_ge(ada_rows_made, 4)
                for par in range(2):
                    for a in range(6):
                        src = bass.AP(rpb.tensor, j * NA_HEADS * RPB_H * RPB_W + (a + 5 - par) * RPB_W - 48,
                                      [[1, GRID_W], [RPB_H * RPB_W, NA_HEADS], [1, GRID_W]])
                        dst = rel_in[:, :, :].rearrange("p (h a) k -> p h a k", a=6)
                        g.dma_start(dst[64 * par:64 * par + 64, :, a, :], src).then_inc(rel_loaded, 16)
                pool.wait_ge(rel_loaded, 16 * 12 * (j + 1))
                pool.wait_ge(const_loaded, CONSTS_IN)
                g.tensor_tensor(rel[:, :, :, :].rearrange("p h a k -> p (h a) k"),
                                rel_in[:, :, ::-1],
                                mask[:, None, :].to_broadcast([P, NA_HEADS * 6, GRID_W]), ALU.add)\
                    .then_inc(rel_ready, 1)
                pool.wait_ge(tile_free, FREE0 + layers[layer]["mix_tile"] + 2 * C)
                pool.wait_ge(rel_ready, j + 1)
                g.memset(Qz[64:128, 0, :], 0.0).then_inc(qz_cleared, 1)
                g.memset(Qz[0:64, 1, :], 0.0).then_inc(qz_cleared, 1)
                tok, n_units, u0 = (XT, 4, 8 * C) if layer == DEPTH - 1 else (ALL, 8, 0)
                for i in bodies(pool, C):
                    for par in range(2):
                        pool.wait_ge(scored, SCORED0 + u0 - n_units + n_units // 2 * (par + 1) + n_units * i)
                        half = slice(64 * par, 64 * par + 64)
                        g.tensor_copy(Qz[half, par, tok], QK[half, i, tok]).then_inc(q_staged, 1)
                pool.wait_ge(q_staged, 2 * C * (j + 1))

            g.memset(eps[:, :], EPS).then_inc(c_ready, 1)
            pool.wait_ge(x_loaded, 16)
            clear_total(0, ALL)
            for c in range(C - 1):
                add_square(0, c, c, ALL)

            for layer, p in enumerate(layers):
                r = 2 * layer
                if layer % 3 == 0:
                    pairs_staged(layer)
                    out_tile = p["mix_tile"] + 24
                elif layer % 3 == 1:
                    def add(dst, a0, b0):
                        return g.tensor_tensor(dst, decay_t[:, 0, a0:a0 + CTX], decay_t[:, 1, b0:b0 + CTX], ALU.add)

                    for h in range(RET_HEADS):
                        if h:
                            pool.wait_ge(mask_made, 6 * h)
                        else:
                            pool.wait_ge(rope_step, 17)
                        g.dma_start(decay_t[:, :, :], dist).then_inc(dist_loaded, 16)
                        pool.wait_ge(decayed, 2 * h + 2)
                        for b, (left, right) in enumerate((((P, 3 * P), (3 * P, P)), ((0, 2 * P), (2 * P, 0)),
                                                           ((P, 3 * P), (0, 2 * P)))):
                            if h:
                                pool.wait_ge(ret_out, 3 * (h - 1) + b + 1)
                            add(A[b][:, CT], *left).then_inc(mask_made, 1)
                            add(A[b][:, XT], *right).then_inc(mask_made, 1)
                    out_tile = p["mix_tile"] + 48
                else:
                    pool.wait_ge(norm_summed, r + 1)
                    g.memset(zeros[:, :], 0.0).then_inc(tap_cleared, 1)
                    pool.wait_ge(tap_cleared, 1)
                    for i in bodies(pool, 4):
                        for k in range(2):
                            c = 2 * i + k
                            pool.wait_ge(tap_done, TAP_STEPS * (c - 1) + TAP_FREE)
                            g.tensor_tensor(pooled[:, k, :], zeros[:, :], zeros[:, :], ALU.add).then_inc(tap_cleared, 1)
                            pool.wait_ge(tap_cleared, c + 2)
                            for n, tap in enumerate(pool_taps):
                                shift = tap - mid
                                lo, hi = max(0, -shift), min(CTX, CTX - shift)
                                place = (POOL_TAPS * k + n) % 4
                                acc = pooled[:, k, :].rearrange("p (s n) -> p s n", s=2)[:, :, lo:hi]
                                made = prods[:, place, :].rearrange("p (s n) -> p s n", s=2)[:, :, lo:hi]
                                pool.wait_ge(tap_made, POOL_TAPS * c + n + 1)
                                pool.wait_ge(tap_pooled, 4 + POOL_TAPS * c + n)
                                g.tensor_tensor(acc, acc, made, ALU.add).then_inc(tap_pooled, 1)
                    out_tile = p["mix_tile"] + 16
                after_residual(r + 1, out_tile, norm_tokens(layer, 1))
                if layer < DEPTH - 1:
                    after_residual(r + 2, p["down_tile"], ALL)

        @block.tensor
        def _(pe):
            t = nc.tensor

            def three(dst, st, w, hi, lo, start, stop):
                t.matmul(dst, Whi[:, st.slot, w], hi, start=start, stop=False)
                t.matmul(dst, Whi[:, st.slot, w], lo, start=False, stop=False)
                return t.matmul(dst, Wlo[:, st.slot, w], hi, start=False, stop=stop)

            def three_moving(dst, st, w, hi, lo, start, stop):
                t.matmul(dst, hi, Whi[:, st.slot, w], start=start, stop=False)
                t.matmul(dst, lo, Whi[:, st.slot, w], start=False, stop=False)
                return t.matmul(dst, hi, Wlo[:, st.slot, w], start=False, stop=stop)

            def tile(index, static, groups, hi, lo, tok, ready=None):
                pe.wait_ge(tile_free, index + 1)
                dst, k, count = bank[static % 4], 0, sum(n for _, n in groups)
                for st, n in groups:
                    pe.wait_ge(lo_split, st.n + 1)
                    for q in range(n):
                        if ready:
                            pe.wait_ge(ready[0], ready[1] + k + 1)
                        last = three(dst[:, tok], st, slice(P * q, P * q + P), hi[:, k, tok], lo[:, k, tok],
                                     k == 0, k == count - 1)
                        k += 1
                    last.then_inc(weights_used, 1)

            def two_tiles(index, steps, tok, ready, counts=(1, 1)):
                pe.wait_ge(tile_free, index + 2)
                pe.wait_ge(lo_split, steps[1].n + 1)
                for k in range(C):
                    pe.wait_ge(h_ready, ready + k + 1)
                    for m in range(2):
                        last = three(bank[m][:, tok], steps[m], slice(P * k, P * k + P), Hhi[:, k, tok],
                                     Hlo[:, k, tok], k == 0, k == C - 1)
                        if k == C - 1 and counts[m]:
                            last.then_inc(weights_used, counts[m])

            def ada(st, quarter, used=1):
                pe.wait_ge(lo_split, st.n + 1)
                for q in range(2):
                    k = 2 * quarter + q
                    w = slice(512 * q, 512 * q + 512)
                    t.matmul(bank[6][0:4, :], cparts[:, k, :], Whi[:, st.slot, w], start=k == 0, stop=False)
                    last = t.matmul(bank[6][0:4, :], cparts[:, k, :], Wlo[:, st.slot, w], start=False, stop=k == C - 1)
                last.then_inc(weights_used, used)

            def ada_raw_slice(first, per, i, b):
                for quarter in range(4):
                    st = Step(first + quarter, per, i)
                    pe.wait_ge(raw_loaded[st.slot], 16 * (st.lap + 1))
                    for q in range(2):
                        k = 2 * quarter + q
                        last = t.matmul(bank[b][0:2, :], csilu[:, k, :], raw[:, st.slot, 512 * q:512 * q + 512],
                                        start=k == 0, stop=k == C - 1)
                    last.then_inc(weights_used, 1)

            def ada_cols(index, n_rows=4):
                pe.wait_ge(rows_copied, index + 1)
                for q in range(4):
                    last = t.matmul(bank[7][:, 2 * q:2 * q + 2], rows[0:n_rows, P * q:P * q + P],
                                    picker[0:n_rows, :], start=True, stop=True)
                last.then_inc(cols_made, 1)

            def norm_sum(r, tok):
                pe.wait_ge(sum_step, (r + 1) * SUM_STEPS)
                for b in token_blocks(tok):
                    t.matmul(bank[4][:, 2 * b:2 * b + 2], total[:, P * b:P * b + P], one[:, 0:2],
                             start=b == token_blocks(tok)[0], stop=False)
                pe.wait_ge(last_squared, r + 1)
                for b in token_blocks(tok):
                    last = t.matmul(bank[4][:, 2 * b:2 * b + 2], last_square[:, P * b:P * b + P], one[:, 0:2],
                                    start=False, stop=b == TB - 1)
                last.then_inc(norm_summed, 1)

            def norm_spread(r, tok):
                pe.wait_ge(norm_diagonal, r + 1)
                t.matmul(bank[5][:, tok], one[:, :], diagonal[:, tok], start=True, stop=True).then_inc(norm_rstd, 1)

            def gap_slice(first, r, tok, index):
                for quarter in range(4):
                    ada(Step(first + quarter), quarter)
                    if quarter == 1:
                        norm_sum(r, tok)
                    if quarter == 2:
                        norm_spread(r, tok)
                ada_cols(index)

            def tokens_major(first, count, tile0):
                for i, peeled_off in peeled(pe, count // 2):
                    for y in range(2):
                        for b in range(TB):
                            if not peeled_off:
                                pe.wait_ge(tile_free, tile0 + b + 1 + TB * (y - 1) + 2 * TB * i)
                            elif V_BANKS[y][b] < 4:
                                pe.wait_ge(tile_free, tile0 + V_BANKS[y][b] + 1)
                        for quarter in range(4):
                            st = Step(first + 4 * y + quarter, 8, i)
                            pe.wait_ge(lo_split, st.n + 1)
                            for q in range(2):
                                k = 2 * quarter + q
                                for b in range(TB):
                                    tk = slice(P * b, P * b + P)
                                    last = three_moving(bank[V_BANKS[y][b]][:, :], st, slice(512 * q, 512 * q + 512),
                                                        Hhi[:, k, tk], Hlo[:, k, tk], k == 0, k == C - 1)
                            last.then_inc(weights_used, 1)

            def na(layer, p):
                j = layer // 3
                last_layer = layer == DEPTH - 1
                per = p["qk_per"]
                qk0 = 2 * C * j
                a0 = 4

                def head_sum(k_static, k, tok):
                    pe.wait_ge(qk_squared, qk0 + k + 1)
                    t.matmul(bank[4 + k_static % 2][:, tok], one_head[:, :], na_sq[:, k_static % 2, tok],
                             start=True, stop=True).then_inc(qk_summed, 1)

                for part, tok in ((0, XT if last_layer else ALL), (1, ALL)):
                    for i, first in peeled(pe, 2):
                        start = p["mix"] + 2 * per * part
                        steps = [Step(start + (TILE_AT[m] if per == 8 else m), per, i) for m in range(4)]
                        ada_steps = [Step(start + ADA_AT[m], per, i) for m in range(4)]
                        together = first and part == 0
                        if together:
                            two_tiles(p["mix_tile"], steps[:2], tok, p["mix_ready"], (1, 0 if per == 8 else 1))
                        for m in range(4):
                            k = 8 * part + m + 4 * i
                            if per == 8 and m >= 2:
                                ada(ada_steps[m], m)
                            if not (together and m < 2):
                                tile(p["mix_tile"] + k, m, [(steps[m], C)], Hhi, Hlo, tok)
                            if per == 8 and m < 2:
                                ada(ada_steps[m], m, 2 if together and m == 0 else 1)
                            if m:
                                head_sum(m - 1, k - 1, tok)
                        if layer == 0:
                            ada_cols(a0 + 2 * part + i)
                        head_sum(3, 8 * part + 3 + 4 * i, tok)
                if layer == 0:
                    pe.wait_ge(mod_ready, 8)
                tokens_major(p["v"], 2, p["mix_tile"] + 16)

                n_units = 4 if last_layer else 8
                u0 = 0 if layer == 0 else 8 * C
                blocks = (2, 3) if last_layer else (0, 1, 2, 3)
                units = [(par, b) for par in range(2) for b in blocks]

                def scores(i, u):
                    par, b = units[u]
                    keys = CT if b < 2 else ALL
                    if b == blocks[0]:
                        pe.wait_ge(q_staged, 2 * C * j + par + 1 + 2 * i)
                    pe.wait_ge(exped, u0 + u + 1 + n_units * i)
                    t.matmul(bank[u % 4][:, keys], Qz[:, par, P * b:P * b + P], QK[:, 8 + i, keys],
                             start=True, stop=True).then_inc(scored, 1)

                def turn(i, u):
                    par, b = units[u]
                    pe.wait_ge(exped, u0 + 4 + u + 1 + n_units * i)
                    pe.wait_ge(p_copied, u0 + u + 1 + n_units * i)
                    for kb in range(2 if b < 2 else 4):
                        last = t.transpose(bank[4 + u % 2][:, P * kb:P * kb + P], prob[:, u % 2, P * kb:P * kb + P],
                                           ident[:, :])
                    last.then_inc(p_turned, 1)

                def attend(i, u):
                    par, b = units[u]
                    pe.wait_ge(p_copied, u0 + 2 + u + 1 + n_units * i)
                    pe.wait_ge(o_stored, u0 + 2 + u + 1 + n_units * i)
                    n_keys = 2 if b < 2 else 4
                    for kb in range(n_keys):
                        last = t.matmul(bank[6 + u % 2][:, 0:NA_HD], probT[:, u % 2, P * kb:P * kb + P],
                                        V[:, kb, bass.ts(2 * i + par, NA_HD)], start=kb == 0, stop=kb == n_keys - 1)
                    last.then_inc(attended, 1)

                def pair(i, first):
                    for s in range(n_units):
                        if first and s == 0:
                            pe.wait_ge(tile_free, FREE0 + p["mix_tile"] + 2 * C + TB)
                        if first and s == 2:
                            pe.wait_ge(tile_free, FREE0 + p["mix_tile"] + 2 * C + 2 * TB)
                        scores(i, s)
                        if s >= 2:
                            turn(i, s - 2)
                        elif not first:
                            turn(i - 1, s - 2 + n_units)
                        if s >= 3:
                            attend(i, s - 3)
                        elif not first:
                            attend(i - 1, s - 3 + n_units)

                pair(0, True)
                with pe.Fori(1, C) as i:
                    pair(i, False)
                for s in range(3):
                    if s < 2:
                        turn(C - 1, s - 2 + n_units)
                    attend(C - 1, s - 3 + n_units)
                out_blocks = blocks
                pe.wait_ge(o_stored, u0 + 4 + n_units * C)
                for c in range(C):
                    if c >= 4:
                        pe.wait_ge(h_ready, p["o_ready"] + c - 3)
                    for b in out_blocks:
                        last = t.transpose(bank[c % 4][:, P * b:P * b + P], O[:, b, P * c:P * c + P], ident[:, :])
                    last.then_inc(o_turned, 1)
                tok = XT if last_layer else ALL
                per = p["o_per"]
                pe.wait_ge(h_ready, p["o_ready"] + C)
                for i in bodies(pe, 2):
                    for m in range(4):
                        st = Step(p["o"] + per // 4 * m, per, i)
                        if layer == 0:
                            for q in range(2):
                                ada(st.ahead(q), 2 * (m % 2) + q)
                            st = st.ahead(2)
                        tile(p["mix_tile"] + 24 + m + 4 * i, m, [(st, C)], Hhi, Hlo, tok)
                        if layer == 0 and m % 2:
                            ada_cols(8 + m // 2 + 2 * i)

            def retention(p):
                for i, first in peeled(pe, 4):
                    if first:
                        two_tiles(p["mix_tile"], [Step(p["mix"] + m) for m in range(2)], ALL, p["mix_ready"])
                    for m in range(2 if first else 0, 4):
                        tile(p["mix_tile"] + m + 4 * i, m, [(Step(p["mix"] + m, 4, i), C)], Hhi, Hlo, ALL)
                tokens_major(p["v"], 4, p["mix_tile"] + 16)
                pe.wait_ge(tile_free, FREE0 + p["mix_tile"] + 32)
                pe.wait_ge(rope_step, 17)

                def scores(h):
                    if h:
                        pe.wait_ge(weighted, 3 * h)
                    for kb in range(TB):
                        dst = bank[kb][:, :] if kb < 2 else bank[2][:, CTX * (kb - 2):CTX * (kb - 1)]
                        for d in range(2):
                            last = t.matmul(dst, QKr[:, C + 2 * h + d, P * kb:P * kb + P],
                                            QKr[:, 2 * h + d, ALL if kb < 2 else XT], start=d == 0, stop=d == 1)
                    last.then_inc(ret_scored, 1)

                def mix_values(h):
                    for kb in range(TB):
                        pe.wait_ge(weighted, 3 * h + min(kb, 2) + 1)
                        for b in range(0 if kb < 2 else 2, TB):
                            if h and kb == 0:
                                pe.wait_ge(gn_done, TB * (h - 1) + b + 1)
                            a = A[kb][:, P * b:P * b + P] if kb < 2 else \
                                A[2][:, CTX * (kb - 2) + P * (b - 2):CTX * (kb - 2) + P * (b - 1)]
                            last = t.matmul(bank[4 + b][:, :], a, Vr[:, kb, RET_V * h:RET_V * (h + 1)],
                                            start=kb == 0, stop=kb == (1 if b < 2 else 3))
                        if kb != 2:
                            last.then_inc(ret_out, 1)

                scores(0)
                for h in range(RET_HEADS):
                    if h + 1 < RET_HEADS:
                        scores(h + 1)
                    mix_values(h)

                for m in range(2):
                    tile(p["mix_tile"] + 32 + m, m, [(Step(p["g"] + m), C)], Hhi, Hlo, ALL)
                pe.wait_ge(gn_done, TB * RET_HEADS)
                for c in range(RET_VC):
                    if c >= 4:
                        pe.wait_ge(ot_copied, c - 3)
                    for b in range(TB):
                        last = t.transpose(bank[4 + c % 4][:, P * b:P * b + P], On[:, b, P * c:P * c + P], ident[:, :])
                    last.then_inc(gn_turned, 1)
                for i, first in peeled(pe, 4):
                    for m in range(2 if first else 0, 4):
                        tile(p["mix_tile"] + 32 + m + 4 * i, m, [(Step(p["g"] + m, 4, i), C)], Hhi, Hlo, ALL)
                pe.wait_ge(tile_free, FREE0 + p["mix_tile"] + 48)
                for i in bodies(pe, 2):
                    for m in range(4):
                        tile(p["mix_tile"] + 48 + m + 4 * i, m,
                             [(Step(p["o"] + 2 * m, 8, i), 8), (Step(p["o"] + 2 * m + 1, 8, i), 8)], Yhi, Ylo, ALL)

            def conv(p):
                index = ADA_SLICES * 3 + 1
                for i, first in peeled(pe, 4):
                    for k in range(2):
                        ada_raw_slice(p["mix"] + 6 * k, 12, i, 6)
                        steps = [Step(p["mix"] + 6 * k + 4 + m, 12, i) for m in range(2)]
                        if first and k == 0:
                            two_tiles(p["mix_tile"], steps, ALL, p["mix_ready"])
                        else:
                            for m in range(2):
                                tile(p["mix_tile"] + 2 * k + m + 4 * i, 2 * k + m, [(steps[m], C)], Hhi, Hlo, ALL)
                        ada_cols(index + k + 2 * i, 2)
                ada_raw_slice(p["last_ada"], 0, 0, 6)
                ada_raw_slice(p["last_ada"] + 4, 0, 0, 5)
                ada_cols(index + C, 2)
                for c in range(C):
                    pe.wait_ge(tap_done, TAP_FREE + TAP_STEPS * (c + 1))
                    last = t.matmul(bank[4][:, :], one[:, :], Wc[:, c, :], start=c == 0, stop=c == C - 1)
                last.then_inc(ln_stat, 1)
                ada_cols(index + C + 1, 2)
                for c in range(C):
                    pe.wait_ge(ln_square, c + 1)
                    t.matmul(bank[5][:, :], one[:, :], square[:, c % 2, :], start=c == 0, stop=c == C - 1)\
                        .then_inc(ln_used, 1)
                for i, first in peeled(pe, 2):
                    if first:
                        two_tiles(p["mix_tile"] + 16, [Step(p["o"] + m) for m in range(2)], ALL, p["o_ready"])
                    for m in range(2 if first else 0, 4):
                        tile(p["mix_tile"] + 16 + m + 4 * i, m, [(Step(p["o"] + m, 4, i), C)], Hhi, Hlo, ALL)

            def ffn(layer, p):
                last_layer = layer == DEPTH - 1
                tok = XT if last_layer else ALL
                per = p["up_per"]
                r = 2 * layer + 1
                if last_layer:
                    norm_sum(r, tok)
                    norm_spread(r, tok)
                else:
                    gap_slice(p["ada"], r, tok, p["ada_index"])
                for i, first in peeled(pe, FC // 2):
                    steps = [Step(p["up"] + (TILE_AT[m] if per == 8 else m), per, i) for m in range(4)]
                    ada_steps = [Step(p["up"] + ADA_AT[m], per, i) for m in range(4)]
                    if first:
                        two_tiles(p["up_tile"], steps[:2], tok, p["ffn_ready"], (1, 0 if per == 8 else 1))
                    for m in range(4):
                        if per == 8 and m >= 2:
                            ada(ada_steps[m], m)
                        if not (first and m < 2):
                            tile(p["up_tile"] + m + 4 * i, m, [(steps[m], C)], Hhi, Hlo, tok)
                        if per == 8 and m < 2:
                            ada(ada_steps[m], m, 2 if first and m == 0 else 1)
                    if per == 8:
                        ada_cols(ADA_SLICES * (layer + 1) + 1 + i)
                per = 4 * len(DOWN)
                for i in bodies(pe, 2, last_layer):
                    for m in range(4):
                        tile(p["down_tile"] + m + 4 * i, m,
                             [(Step(p["down"] + 3 * m + q, per, i), DOWN[q]) for q in range(3)], Ghi, Glo, tok,
                             (g_ready, 2 + FC * layer) if m == 0 else None)

            pe.wait_ge(c_ready, 2)
            for s in range(4):
                if s >= 2:
                    pe.wait_ge(rows_copied, s - 1)
                for k in range(C):
                    if k % 2 == 0:
                        pe.wait_ge(ada_loaded[4 * s + k // 2], 16)
                    last = t.matmul(bank[5 + s % 2][0:2, :], csilu[:, k, :],
                                    ada_raw[:, 4 * s + k // 2, 512 * (k % 2):512 * (k % 2) + 512],
                                    start=k == 0, stop=k == C - 1)
                last.then_inc(ada_rows_made, 1)
                if s == 0:
                    pe.wait_ge(first_loaded, 16 * len(FIRST_CONSTS))
                else:
                    ada_cols(s - 1, 2)
                if s == 2:
                    norm_sum(0, ALL)
            norm_spread(0, ALL)
            ada_cols(3, 2)
            pe.wait_ge(const_loaded, CONSTS_IN)
            pe.wait_ge(c_ready, 4)
            for layer, p in enumerate(layers):
                if layer % 3 == 2:
                    gap_slice(p["first_ada"], 2 * layer, ALL, ADA_SLICES * (layer + 1))
                elif layer:
                    norm_sum(2 * layer, ALL)
                    norm_spread(2 * layer, ALL)
                if layer % 3 == 0:
                    na(layer, p)
                elif layer % 3 == 1:
                    retention(p)
                else:
                    conv(p)
                ffn(layer, p)

        @block.scalar
        def _(act):
            a = nc.scalar

            def split_group(st):
                act.wait_ge(raw_loaded[st.slot], 16 * (st.lap + 1))
                a.activation(Whi[:, st.slot, :], raw[:, st.slot, :], ACT.Copy).then_inc(hi_split, 1)

            def split(st):
                st = st.ahead(LEAD)
                if not isinstance(st.n, int) or st.n < n_groups:
                    split_group(st)

            def square_last(r, tok):
                if r:
                    act.wait_ge(tile_free, FREE0 + residual_end(r))
                else:
                    act.wait_ge(x_loaded, 16)
                a.activation(last_square[:, tok], X[:, C - 1, tok], ACT.Square).then_inc(last_squared, 1)

            def root_of_norm(r, tok):
                square_last(r, tok)
                act.wait_ge(norm_summed, r + 1)
                cols = slice(2 * token_blocks(tok)[0], 2 * TB)
                a.activation(token_root[:, cols], bank[4][:, cols], ACT.Sqrt, bias=eps[:, :], scale=1.0 / D)\
                    .then_inc(norm_root, 1)

            def norm_apply(layer, part, gap=None, between={}):
                tok = norm_tokens(layer, part)
                r = 2 * layer + part
                if r:
                    root_of_norm(r, tok)
                if gap is not None:
                    act.wait_ge(weights_used, gap + 4)
                    a.activation(rows[:, :], bank[6][0:4, :], ACT.Copy).then_inc(rows_copied, 1)
                k0 = C * r
                for c in range(C):
                    act.wait_ge(norm_scaled, k0 + c + 1)
                    for half, hs in halves(tok):
                        last = a.activation(Hhi[:, c, hs], ring[c % 4][:, hs], ACT.Identity,
                                            bias=mod[:, layer % 2, 3 * C * part + c, half:half + 1])
                    last.then_inc(h_hi, 1)
                    if c in between:
                        between[c]()

            def na(layer, p):
                j = layer // 3
                last_layer = layer == DEPTH - 1
                per = p["qk_per"]
                qk0 = 2 * C * j

                def root_of(k_static, k, tok):
                    act.wait_ge(qk_summed, qk0 + k + 1)
                    a.activation(na_root[:, k_static % 4, tok], bank[4 + k_static % 2][:, tok], ACT.Sqrt,
                                 bias=eps[:, :], scale=1.0 / NA_HD).then_inc(qk_root, 1)

                a.preload_act_table(ACT.Sqrt)
                for part, tok in ((0, XT if last_layer else ALL), (1, ALL)):
                    for i in bodies(act, 2):
                        start = p["mix"] + 2 * per * part
                        for m in range(4):
                            k = 8 * part + m + 4 * i
                            if per == 8:
                                split(Step(start + 2 * m, per, i))
                            act.wait_ge(weights_used, Step(start + (TILE_AT[m] if per == 8 else m), per, i).n + 1)
                            a.activation(na_sq[:, m % 2, tok], bank[m][:, tok], ACT.Square).then_inc(qk_squared, 1)
                            split(Step(start + (2 * m + 1 if per == 8 else m), per, i))
                            if m:
                                root_of(m - 1, k - 1, tok)
                        root_of(3, 8 * part + 3 + 4 * i, tok)
                for i in bodies(act, 2):
                    for quarter in range(4):
                        split(Step(p["v"] + quarter, 4, i))

                n_units = 4 if last_layer else 8
                u0 = 0 if layer == 0 else 8 * C
                blocks = (2, 3) if last_layer else (0, 1, 2, 3)
                units = [(par, b) for par in range(2) for b in blocks]
                a.preload_act_table(ACT.Exp)

                def copy_turned(i, u):
                    par, b = units[u]
                    keys = CT if b < 2 else ALL
                    act.wait_ge(p_turned, u0 + 2 + u + 1 + n_units * i)
                    act.wait_ge(attended, u0 + u + 1 + n_units * i)
                    a.activation(probT[:, u % 2, keys], bank[4 + u % 2][:, keys], ACT.Copy).then_inc(p_copied, 1)

                def exponentials(i, u):
                    par, b = units[u]
                    keys = CT if b < 2 else ALL
                    act.wait_ge(peaked, u0 + u + 1 + n_units * i)
                    act.wait_ge(p_turned, u0 + u + 1 + n_units * i)
                    act.wait_ge(o_stored, u0 + u + 1 + n_units * i)
                    a.activation(prob[:, u % 2, keys], bank[u % 4][:, keys], ACT.Exp, bias=peak[:, u % 4:u % 4 + 1],
                                 accum_out=psum_p[:, u % 4:u % 4 + 1]).then_inc(exped, 1)

                def pair(i, first):
                    for s in range(n_units):
                        if s >= 2:
                            copy_turned(i, s - 2)
                        elif not first:
                            copy_turned(i - 1, s - 2 + n_units)
                        exponentials(i, s)

                pair(0, True)
                with act.Fori(1, C) as i:
                    pair(i, False)
                for s in range(2):
                    copy_turned(C - 1, s - 2 + n_units)
                a.preload_act_table(ACT.Sqrt)
                tok = XT if last_layer else ALL
                for c in range(C):
                    act.wait_ge(o_turned, C * j + c + 1)
                    a.activation(Hhi[:, c, tok], bank[c % 4][:, tok], ACT.Copy).then_inc(h_hi, 1)
                per = p["o_per"]
                for i in bodies(act, 2):
                    for m in range(per):
                        split(Step(p["o"] + m, per, i))

            def retention(p):
                act.wait_ge(lg_step, 2)
                a.activation(small[:, 1, :], small[:, 0, :], ACT.Exp, scale=-1.0).then_inc(lg_step, 1)
                act.wait_ge(lg_step, 3)
                a.activation(small[:, 2, :], small[:, 1, :], ACT.Ln, bias=1.0).then_inc(lg_step, 1)
                for i in bodies(act, 4):
                    for m in range(4):
                        split(Step(p["mix"] + m, 4, i))
                for i in bodies(act, 4):
                    for m in range(4):
                        split(Step(p["v"] + m, 4, i))
                act.wait_ge(lg_step, 6)

                def decays(h):
                    act.wait_ge(dist_loaded, 16 * (h + 1))
                    for way in range(2):
                        lg = log_gamma[:, RET_HEADS * way + h:RET_HEADS * way + h + 1]
                        a.activation(decay_t[:, way, :], decay_t[:, way, :], ACT.Exp, scale=lg).then_inc(decayed, 1)

                decays(0)
                for h in range(RET_HEADS):
                    if h + 1 < RET_HEADS:
                        decays(h + 1)
                    a.preload_act_table(ACT.Sqrt)
                    act.wait_ge(gn_stat, 2 * TB * (h + 1))
                    a.activation(sd4[:, :], mv[:, :, 1], ACT.Sqrt, bias=eps[:, :]).then_inc(gn_root, 1)
                for c in range(RET_VC):
                    act.wait_ge(gn_turned, c + 1)
                    a.activation(OT[:, c, :], bank[4 + c % 4][:, :], ACT.Copy).then_inc(ot_copied, 1)
                a.preload_act_table(ACT.Silu)
                for i in bodies(act, 4):
                    for m in range(4):
                        st = Step(p["g"] + m, 4, i)
                        act.wait_ge(weights_used, st.n + 1)
                        a.activation(ring[m], bank[m][:, :], ACT.Silu).then_inc(gate_silu, 1)
                        split(st)
                        act.wait_ge(y_made, m + 1 + 4 * i)
                        a.activation(Yhi[:, m + 4 * i, :], ring[m], ACT.Copy).then_inc(y_hi, 1)
                a.preload_act_table(ACT.Sqrt)
                for i in bodies(act, 2):
                    for m in range(8):
                        split(Step(p["o"] + m, 8, i))

            def conv(p):
                def chunk(i, k, last):
                    nxt = Step(p["mix"] + 6 * k + 6, 12, i)
                    act.wait_ge(weights_used, nxt.n)
                    a.activation(glu_s[:, k, :], bank[2 * k + 1][:, :], ACT.Sigmoid,
                                 bias=cvb[:, 1, bass.ds(2 * i + k, 1)]).then_inc(glu_sigmoid, 1)
                    act.sem_inc(hi_split, 8 if last else 4)
                    c = 2 * i + k
                    act.wait_ge(tile_free, FREE0 + p["mix_tile"] + 2 * k + 1 + 4 * i)
                    for n, tap in enumerate(pool_taps):
                        shift = tap - mid
                        lo, hi = max(0, -shift), min(CTX, CTX - shift)
                        place = (POOL_TAPS * k + n) % 4
                        act.wait_ge(tap_pooled, POOL_TAPS * c + n + 1)
                        a.activation(prods[:, place, :].rearrange("p (s n) -> p s n", s=2)[:, :, lo:hi],
                                     U[:, k, :].rearrange("p (s n) -> p s n", s=2)[:, :, lo + shift:hi + shift],
                                     ACT.Identity, scale=cvf[:, bass.ds(c, 1), tap]).then_inc(tap_made, 1)
                        if not last and n in (4, 7):
                            split_group(nxt.ahead(4 if n == 4 else 5))

                a.preload_act_table(ACT.Sigmoid)
                with act.Fori(0, 3) as i:
                    for k in range(2):
                        chunk(i, k, False)
                chunk(3, 0, False)
                chunk(3, 1, True)
                for m in range(LEAD):
                    split_group(Step(p["o"] + m))
                a.preload_act_table(ACT.Sqrt)
                for c in range(C):
                    act.wait_ge(ln_centred, c + 1)
                    if c >= 2:
                        act.wait_ge(ln_used, c - 1)
                    a.activation(square[:, c % 2, :], Wc[:, c, :], ACT.Square).then_inc(ln_square, 1)
                act.wait_ge(ln_used, C)
                a.activation(root[:, :], bank[5][:, :], ACT.Sqrt, bias=eps[:, :], scale=1.0 / D).then_inc(ln_mean, 1)
                a.preload_act_table(ACT.Silu)
                for c in range(C):
                    act.wait_ge(ln_scaled, c + 1)
                    a.activation(hb[:, c % 2, :], hb[:, c % 2, :], ACT.Silu, bias=cvb[:, 4, c:c + 1],
                                 scale=cvb[:, 3, c:c + 1]).then_inc(ln_silu, 1)
                    act.wait_ge(ln_silu, c + 1)
                    a.activation(Hhi[:, c, :], hb[:, c % 2, :], ACT.Copy).then_inc(h_hi, 1)
                a.preload_act_table(ACT.Sqrt)
                for i in bodies(act, 2):
                    for m in range(4):
                        split(Step(p["o"] + m, 4, i))

            def ffn(layer, p):
                last_layer = layer == DEPTH - 1
                tok = XT if last_layer else ALL
                per = p["up_per"]
                a.preload_act_table(ACT.Gelu_apprx_tanh)
                for i in bodies(act, FC // 2):
                    for m in range(4):
                        s = p["up"] + (2 * m if per == 8 else m)
                        if per == 8:
                            split(Step(s, per, i))
                            s += 1
                        split(Step(s, per, i))
                        k = m // 2
                        act.wait_ge(tile_free, FREE0 + p["up_tile"] + m + 1 + 4 * i)
                        if m % 2 == 0:
                            a.activation(cv[:, k, tok], cv[:, k, tok], ACT.Gelu_apprx_tanh).then_inc(gelu_done, 1)
                        else:
                            a.activation(Ghi[:, k + 2 * i, tok], cv[:, k, tok], ACT.Copy).then_inc(g_hi, 1)
                per = 4 * len(DOWN)
                if not last_layer:
                    a.preload_act_table(ACT.Sqrt)
                for i in bodies(act, 2, last_layer):
                    for m in range(per):
                        split(Step(p["down"] + m, per, i))

            act.dma_start(cfull[:, :, :], ada_in).then_inc(c_loaded, 16)
            act.wait_ge(c_loaded, 16)
            a.activation(csilu[:, :, :], cfull[:, :, :], ACT.Silu).then_inc(c_ready, 1)
            act.wait_ge(c_ready, 2)
            a.activation(cparts[:, :, 0:2], csilu[:, :, :], ACT.Copy).then_inc(c_ready, 1)
            act.dma_start(X[:, :, :], x).then_inc(x_loaded, 16)
            for src, dst in CONSTS:
                full = dst[tuple(slice(None) for _ in dst.shape)]
                act.dma_start(full, src).then_inc(const_loaded, 16)
            root_of_norm(0, ALL)
            for n in range(LEAD):
                split(Step(n - LEAD))
            for layer, p in enumerate(layers):
                if layer % 3 == 2:
                    first = p["first_ada"]
                    split_group(Step(first + 3))
                    norm_apply(layer, 0, first, {
                        0: lambda: act.sem_inc(hi_split, 4),
                        3: lambda: split_group(Step(first + 8)), 5: lambda: split_group(Step(first + 9))})
                else:
                    norm_apply(layer, 0)
                if layer % 3 == 0:
                    na(layer, p)
                elif layer % 3 == 1:
                    retention(p)
                else:
                    conv(p)
                if layer < DEPTH - 1:
                    first = p["ada"]
                    split(Step(first))
                    norm_apply(layer, 1, first, {
                        c: lambda c=c: split(Step(first + 1 + c)) for c in range(3)})
                else:
                    norm_apply(layer, 1)
                ffn(layer, p)

        @block.vector
        def _(dve):
            v = nc.vector

            def split_group(st):
                dve.wait_ge(hi_split, st.n + 1)
                v.tensor_tensor(Wlo[:, st.slot, :], raw[:, st.slot, :], Whi[:, st.slot, :].bitcast(F32), ALU.subtract)\
                    .then_inc(lo_split, 1)

            def split(st):
                st = st.ahead(LEAD)
                if not isinstance(st.n, int) or st.n < n_groups:
                    split_group(st)

            def ada_rows(st, b=6, n_rows=4):
                dve.wait_ge(weights_used, st.n + 1)
                v.tensor_copy(rows[0:n_rows, :], bank[b][0:n_rows, :]).then_inc(rows_copied, 1)

            def ada_store(index, layer, s):
                dve.wait_ge(cols_made, index + 1)
                v.tensor_tensor(mod[:, layer % 2, bass.ts(s, 4), :],
                                bank[7][:, 0:8].rearrange("p (q s) -> p q s", s=2),
                                bias_ada[:, layer, bass.ts(s, 4)].unsqueeze(2).to_broadcast([P, 4, 2]), ALU.add)\
                    .then_inc(mod_ready, 1)

            def invert_root(r, tok):
                b0 = token_blocks(tok)[0]
                dve.wait_ge(norm_root, r + 1)
                v.reciprocal(token_root[:, 2 * b0:2 * TB], token_root[:, 2 * b0:2 * TB]).then_inc(token_rstd, 1)
                dve.wait_ge(token_rstd, r + 1)
                v.tensor_tensor(diagonal[:, tok].rearrange("p (b n) -> p b n", n=P),
                                ident[:, None, :].to_broadcast([P, TB - b0, P]),
                                token_root[:, 2 * b0:2 * TB:2].unsqueeze(2).to_broadcast([P, TB - b0, P]), ALU.mult)\
                    .then_inc(norm_diagonal, 1)

            def norm_apply(layer, part, between={}):
                tok = norm_tokens(layer, part)
                r = 2 * layer + part
                if layer == 0:
                    dve.wait_ge(mod_ready, 12 if part else 4)
                else:
                    dve.wait_ge(mod_ready, ADA_SLICES * (layer + 1))
                v.scalar_tensor_tensor(scale[:, part, :, :],
                                       mod[:, layer % 2, C * (3 * part + 1):C * (3 * part + 2), :],
                                       1.0, gains[:, layer, part, :].unsqueeze(2).to_broadcast([P, C, 2]),
                                       ALU.add, ALU.mult).then_inc(scale_ready, 1)
                if r:
                    invert_root(r, tok)
                dve.wait_ge(scale_ready, r + 1)
                dve.wait_ge(norm_rstd, r + 1)
                ready = layers[layer]["ffn_ready" if part else "mix_ready"]
                def low(c):
                    dve.wait_ge(h_hi, ready + c + 1)
                    for half, hs in halves(tok):
                        last = v.scalar_tensor_tensor(Hlo[:, c, hs], ring[c % 4][:, hs],
                                                      mod[:, layer % 2, 3 * C * part + c, half:half + 1],
                                                      Hhi[:, c, hs].bitcast(F32), ALU.add, ALU.subtract)
                    last.then_inc(h_ready, 1)

                for c in range(C):
                    if c >= 4:
                        dve.wait_ge(h_ready, ready + c - 3)
                    for half, hs in halves(tok):
                        last = v.scalar_tensor_tensor(ring[c % 4][:, hs], X[:, c, hs], scale[:, part, c, half:half + 1],
                                                      bank[5][:, hs], ALU.mult, ALU.mult)
                    last.then_inc(norm_scaled, 1)
                    if c:
                        low(c - 1)
                    if c in between:
                        between[c]()
                low(C - 1)

            def residual(layer, part, src, m, tok, bias=None):
                for half, hs in halves(tok):
                    gate = mod[:, layer % 2, bass.ds(C * (3 * part + 2) + m, 1), half]
                    last = v.scalar_tensor_tensor(X[:, m, hs], src[:, hs], gate, X[:, m, hs], ALU.mult, ALU.add)
                last.then_inc(tile_free, 1)

            def projected(layer, first, stride, per, tok, unroll=False):
                part = 1 if stride == 3 else 0
                for i in bodies(dve, 2, unroll):
                    for m in range(4):
                        st = Step(first + stride * m, per, i)
                        for q in range(stride - 1):
                            split(st.ahead(q))
                        dve.wait_ge(weights_used, st.ahead(stride - 1).n + 1)
                        residual(layer, part, bank[m], m + 4 * i, tok)
                        split(st.ahead(stride - 1))

            def tokens_major(first, count, dst):
                for i in bodies(dve, count // 2):
                    for y in range(2):
                        for quarter in range(4):
                            split(Step(first + 4 * y + quarter, 8, i))
                        dve.wait_ge(weights_used, Step(first + 4 * y + 3, 8, i).n + 1)
                        for b in range(TB):
                            v.tensor_copy(dst[:, b, bass.ts(2 * i + y, 512)], bank[V_BANKS[y][b]][:, :])\
                                .then_inc(tile_free, 1)

            def na(layer, p):
                j = layer // 3
                last_layer = layer == DEPTH - 1
                per = p["qk_per"]
                qk0 = 2 * C * j
                for part, tok in ((0, XT if last_layer else ALL), (1, ALL)):
                    def normed(m, k, tok):
                        dve.wait_ge(qk_root, qk0 + k + 1)
                        v.reciprocal(na_root[:, m, tok], na_root[:, m, tok]).then_inc(qk_rstd, 1)
                        dve.wait_ge(qk_rstd, qk0 + k + 1)
                        v.scalar_tensor_tensor(QK[:, k, tok], bank[m][:, tok], qk_gain[:, j, part:part + 1],
                                               na_root[:, m, tok], ALU.mult, ALU.mult).then_inc(tile_free, 1)

                    for i in bodies(dve, 2):
                        start = p["mix"] + 2 * per * part
                        for m in range(4):
                            k = 8 * part + m + 4 * i
                            if per == 8:
                                if m == 3:
                                    ada_rows(Step(start + ADA_AT[3], per, i))
                                split(Step(start + 2 * m, per, i))
                            split(Step(start + (2 * m + 1 if per == 8 else m), per, i))
                            if m:
                                normed(m - 1, k - 1, tok)
                        if layer == 0:
                            s = 4 + 2 * part + i
                            ada_store(s, 0, s)
                        normed(3, 8 * part + 3 + 4 * i, tok)
                dve.wait_ge(rel_ready, j + 1)
                tokens_major(p["v"], 2, V)

                n_units = 4 if last_layer else 8
                u0 = 0 if layer == 0 else 8 * C
                blocks = (2, 3) if last_layer else (0, 1, 2, 3)
                units = [(par, b) for par in range(2) for b in blocks]
                x_units = sum(b >= 2 for _, b in units)
                b0 = 0 if layer == 0 else 4 * C

                def peaks(i, u):
                    par, b = units[u]
                    keys = CT if b < 2 else ALL
                    dve.wait_ge(scored, SCORED0 + u0 + u + 1 + n_units * i)
                    if b >= 2:
                        a0 = 2 if b == 2 else 0
                        sx = bank[u % 4][:, XT].rearrange("p (r k) -> p r k", k=GRID_W)
                        v.tensor_tensor(sx, sx, rel[:, 2 * i + par, a0:a0 + 4, :], ALU.add).then_inc(biased, 1)
                        dve.wait_ge(biased, b0 + 2 * par + b - 1 + x_units * i)
                    v.tensor_reduce(peak[:, u % 4:u % 4 + 1], bank[u % 4][:, keys], axis=AX, op=ALU.max,
                                    negate=True).then_inc(peaked, 1)

                def store(i, u):
                    par, b = units[u]
                    dve.wait_ge(attended, u0 + 2 + u + 1 + n_units * i)
                    v.reciprocal(rinv[:, u % 4:u % 4 + 1], psum_p[:, u % 4:u % 4 + 1]).then_inc(inverted, 1)
                    dve.wait_ge(inverted, u0 + u + 1 + n_units * i)
                    v.tensor_scalar(O[:, b, bass.ts(2 * i + par, NA_HD)], bank[6 + u % 2][:, 0:NA_HD],
                                    rinv[:, u % 4:u % 4 + 1], None, ALU.mult).then_inc(o_stored, 1)

                def pair(i, first):
                    for s in range(n_units):
                        peaks(i, s)
                        if s >= 3:
                            store(i, s - 3)
                        elif not first:
                            store(i - 1, s - 3 + n_units)

                pair(0, True)
                with dve.Fori(1, C) as i:
                    pair(i, False)
                for s in range(3):
                    store(C - 1, s - 3 + n_units)
                tok = XT if last_layer else ALL
                for c in range(C):
                    dve.wait_ge(h_hi, p["o_ready"] + c + 1)
                    v.tensor_tensor(Hlo[:, c, tok], bank[c % 4][:, tok], Hhi[:, c, tok].bitcast(F32), ALU.subtract)\
                        .then_inc(h_ready, 1)
                if layer:
                    projected(layer, p["o"], 1, 4, tok)
                else:
                    for i in bodies(dve, 2):
                        for m in range(4):
                            st = Step(p["o"] + 3 * m, 12, i)
                            split(st)
                            if m % 2:
                                ada_rows(st.ahead(1))
                            split(st.ahead(1))
                            dve.wait_ge(weights_used, st.ahead(2).n + 1)
                            residual(layer, 0, bank[m], m + 4 * i, ALL)
                            split(st.ahead(2))
                            if m % 2:
                                s = 8 + m // 2 + 2 * i
                                ada_store(s, 0, s)

            def retention(p):
                cos, sin = cos_sin[:, 0, :], cos_sin[:, 1, :]
                v.tensor_scalar(small[:, 1, :], logit[:, :], -1.0, None, ALU.mult).then_inc(lg_step, 1)
                dve.wait_ge(lg_step, 1)
                v.tensor_tensor(small[:, 0, :], small[:, 1, :], logit[:, :], ALU.max).then_inc(lg_step, 1)
                dve.wait_ge(lg_step, 4)
                v.scalar_tensor_tensor(log_gamma[:, :], logit[:, :], 0.0, small[:, 2, :], ALU.min, ALU.subtract)\
                    .then_inc(lg_step, 1)
                dve.wait_ge(lg_step, 5)
                v.tensor_scalar(log_gamma[:, :], log_gamma[:, :], -1e-25, None, ALU.min).then_inc(lg_step, 1)
                for i in bodies(dve, 4):
                    for k in range(2):
                        split(Step(p["mix"] + 2 * k, 4, i))
                        st = Step(p["mix"] + 2 * k + 1, 4, i)
                        dve.wait_ge(weights_used, st.n + 1)
                        first, second = bank[2 * k], bank[2 * k + 1]
                        j = 2 * k + 4 * i
                        dve.wait_ge(rope_step, 2 * k + 1 + 4 * i)
                        v.tensor_tensor(rope_t[:, 0, :], first[:, XT], cos, ALU.mult)
                        v.tensor_tensor(rope_t[:, 1, :], first[:, XT], sin, ALU.mult)
                        v.tensor_copy(QKr[:, j, CT], first[:, CT]).then_inc(tile_free, 1)
                        v.tensor_tensor(rope_t[:, 2, :], second[:, XT], sin, ALU.mult)
                        v.tensor_tensor(rope_t[:, 3, :], second[:, XT], cos, ALU.mult)
                        v.tensor_copy(QKr[:, j + 1, CT], second[:, CT]).then_inc(tile_free, 1)
                        dve.wait_ge(tile_free, FREE0 + p["mix_tile"] + 2 * k + 2 + 4 * i)
                        v.tensor_tensor(QKr[:, j, XT], rope_t[:, 0, :], rope_t[:, 2, :], ALU.subtract)\
                            .then_inc(rope_step, 1)
                        v.tensor_tensor(QKr[:, j + 1, XT], rope_t[:, 1, :], rope_t[:, 3, :], ALU.add)\
                            .then_inc(rope_step, 1)
                        split(st)
                tokens_major(p["v"], 4, Vr)
                def weighted_scores(h):
                    dve.wait_ge(ret_scored, h + 1)
                    for b in range(3):
                        dve.wait_ge(mask_made, 6 * h + 2 * b + 2)
                        v.scalar_tensor_tensor(A[b], bank[b][:, :], RET_QK ** -0.5, A[b],
                                               ALU.mult, ALU.mult).then_inc(weighted, 1)

                weighted_scores(0)
                for h in range(RET_HEADS):
                    if h + 1 < RET_HEADS:
                        weighted_scores(h + 1)
                    dve.wait_ge(ret_out, 3 * h + 3)
                    for b in range(TB):
                        v.bn_stats(stats[:, b, :], bank[4 + b][:, :]).then_inc(gn_stat, 1)
                    dve.wait_ge(gn_stat, 2 * TB * h + TB)
                    for b in range(TB):
                        v.bn_aggr(mv[:, b, :], stats[:, b, :]).then_inc(gn_stat, 1)
                    dve.wait_ge(gn_root, h + 1)
                    v.reciprocal(sd4[:, :], sd4[:, :]).then_inc(gn_rstd, 1)
                    dve.wait_ge(gn_rstd, h + 1)
                    for b in range(TB):
                        v.tensor_scalar(On[:, b, RET_V * h:RET_V * (h + 1)], bank[4 + b][:, :], mv[:, b, 0:1],
                                        sd4[:, b:b + 1], ALU.subtract, ALU.mult).then_inc(gn_done, 1)
                for i in bodies(dve, 4):
                    for m in range(4):
                        dve.wait_ge(gate_silu, m + 1 + 4 * i)
                        v.scalar_tensor_tensor(ring[m], OT[:, m + 4 * i, :], gn[:, bass.ds(m + 4 * i, 1)],
                                               ring[m], ALU.mult, ALU.mult).then_inc(y_made, 1)
                        dve.wait_ge(y_made, m + 1 + 4 * i)
                        split(Step(p["g"] + m, 4, i))
                        dve.wait_ge(y_hi, m + 1 + 4 * i)
                        v.tensor_tensor(Ylo[:, m + 4 * i, :], ring[m], Yhi[:, m + 4 * i, :].bitcast(F32),
                                        ALU.subtract).then_inc(tile_free, 1)
                projected(1, p["o"], 2, 8, ALL)

            def conv(p):
                u3 = U[:, :, :].rearrange("p k (s n) -> p k s n", s=2)
                w4 = Wc[:, :, :].rearrange("p c (s n) -> p c s n", s=2)
                z4 = odd[:, :, :].rearrange("p k (s n) -> p k s n", s=2)
                index = ADA_SLICES * 3 + 1

                def chunk(i, k, last):
                    nxt = Step(p["mix"] + 6 * k + 6, 12, i)
                    c = 2 * i + k
                    dve.wait_ge(glu_sigmoid, c + 1)
                    v.scalar_tensor_tensor(U[:, k, :], bank[2 * k][:, :], cvb[:, 0, bass.ds(c, 1)], glu_s[:, k, :],
                                           ALU.add, ALU.mult).then_inc(tile_free, 1)
                    dve.wait_ge(tile_free, FREE0 + p["mix_tile"] + 2 * k + 1 + 4 * i)
                    dve.sem_inc(tile_free, 1)
                    ada_store(index + c, 3, 2 + c)
                    dve.sem_inc(lo_split, 8 if last else 4)
                    done = TAP_FREE + TAP_STEPS * c
                    for n, tap in enumerate(taps):
                        w = cvf[:, bass.ds(c, 1), tap]
                        shift = tap - mid
                        lo, hi = max(0, -shift), min(CTX, CTX - shift)
                        acc = w4[:, c, :, :] if n % 2 == 0 else z4[:, k, :, :]
                        src = u3[:, k, :, lo + shift:hi + shift]
                        if n == 0:
                            v.tensor_scalar(acc, src, w, cvb[:, 2, bass.ds(c, 1)], ALU.mult, ALU.add)\
                                .then_inc(tap_done, 1)
                        elif n == 1:
                            v.memset(z4[:, k, :, 0:lo], 0.0)
                            v.tensor_scalar(acc[:, :, lo:hi], src, w, None, ALU.mult).then_inc(tap_done, 1)
                        else:
                            dve.wait_ge(tap_done, done + n - 1)
                            v.scalar_tensor_tensor(acc[:, :, lo:hi], src, w, acc[:, :, lo:hi], ALU.mult, ALU.add)\
                                .then_inc(tap_done, 1)
                        if n == 13:
                            ada_rows(nxt.ahead(3), 6, 2)
                        elif n in (5, 8) and not last:
                            split_group(nxt.ahead(4 if n == 5 else 5))
                    dve.wait_ge(tap_done, done + len(taps))
                    v.tensor_tensor(Wc[:, c, :], Wc[:, c, :], odd[:, k, :], ALU.add).then_inc(tap_done, 1)
                    dve.wait_ge(tap_pooled, 4 + POOL_TAPS * (c + 1))
                    dve.wait_ge(tap_done, done + len(taps) + 1)
                    v.tensor_tensor(Wc[:, c, :], Wc[:, c, :], pooled[:, k, :], ALU.add).then_inc(tap_done, 1)

                ada_rows(Step(p["mix"] + 3), 6, 2)
                with dve.Fori(0, 3) as i:
                    for k in range(2):
                        chunk(i, k, False)
                chunk(3, 0, False)
                chunk(3, 1, True)
                ada_store(index + C, 3, 2 + C)
                ada_rows(Step(p["last_ada"] + 7), 5, 2)
                dve.wait_ge(ln_stat, 1)
                v.tensor_scalar(rstd[:, :], bank[4][:, :], 1.0 / D, None, ALU.mult).then_inc(ln_mean, 1)
                dve.wait_ge(ln_mean, 1)
                for c in range(C):
                    v.tensor_tensor(Wc[:, c, :], Wc[:, c, :], rstd[:, :], ALU.subtract).then_inc(ln_centred, 1)
                ada_store(index + C + 1, 3, 3 + C)
                for m in range(LEAD):
                    split_group(Step(p["o"] + m))
                dve.wait_ge(ln_centred, C)
                dve.wait_ge(ln_mean, 2)
                v.reciprocal(rstd[:, :], root[:, :]).then_inc(ln_mean, 1)
                dve.wait_ge(ln_mean, 3)

                def low(c):
                    dve.wait_ge(h_hi, p["o_ready"] + c + 1)
                    v.tensor_tensor(Hlo[:, c, :], hb[:, c % 2, :], Hhi[:, c, :].bitcast(F32), ALU.subtract)\
                        .then_inc(h_ready, 1)

                for c in range(C):
                    if c >= 2:
                        dve.wait_ge(h_ready, p["o_ready"] + c - 1)
                    v.tensor_tensor(hb[:, c % 2, :], Wc[:, c, :], rstd[:, :], ALU.mult).then_inc(ln_scaled, 1)
                    if c:
                        low(c - 1)
                low(C - 1)
                for i in bodies(dve, 2):
                    for m in range(4):
                        st = Step(p["o"] + m, 4, i)
                        c = m + 4 * i
                        dve.wait_ge(weights_used, st.n + 1)
                        dve.wait_ge(tile_free, FREE0 + p["mix_tile"] + 16 + c - 1)
                        v.tensor_scalar(glu_s[:, m % 2, :], bank[m][:, :], cvb[:, 5, bass.ds(c, 1)], None, ALU.add)\
                            .then_inc(cv_y, 1)
                        dve.wait_ge(cv_y, c + 1)
                        residual(2, 0, glu_s[:, m % 2, :], c, ALL)
                        split(st)

            def ffn(layer, p):
                last_layer = layer == DEPTH - 1
                tok = XT if last_layer else ALL
                s0 = 1 if last_layer else 0
                per = p["up_per"]
                for i in bodies(dve, FC // 2):
                    for m in range(4):
                        s = p["up"] + (2 * m if per == 8 else m)
                        if per == 8:
                            if m == 3:
                                ada_rows(Step(p["up"] + ADA_AT[3], per, i))
                            split(Step(s, per, i))
                            s += 1
                        st = Step(s, per, i)
                        k, j = m // 2, m // 2 + 2 * i
                        dve.wait_ge(weights_used, Step(p["up"] + (TILE_AT[m] if per == 8 else m), per, i).n + 1)
                        if m % 2 == 0:
                            u3 = bank[m][:, :].rearrange("p (s n) -> p s n", s=2)[:, s0:2, :]
                            c3 = cv[:, k, :].rearrange("p (s n) -> p s n", s=2)[:, s0:2, :]
                            f = fff[:, layer, bass.ds(j, 1), :]
                            dve.wait_ge(g_ready, FC * layer + k + 1 + 2 * i)
                            v.tensor_scalar(c3, u3, f[:, 0, 1:2], f[:, 0, 3:4], ALU.mult, ALU.add).then_inc(ffn_tap, 1)
                            dve.wait_ge(ffn_tap, 2 * FC * layer + 2 * k + 1 + 4 * i)
                            v.scalar_tensor_tensor(c3[:, :, 1:], u3[:, :, :-1], f[:, 0, 0:1], c3[:, :, 1:],
                                                   ALU.mult, ALU.add).then_inc(ffn_tap, 1)
                            dve.wait_ge(ffn_tap, 2 * FC * layer + 2 * k + 2 + 4 * i)
                            v.scalar_tensor_tensor(c3[:, :, :-1], u3[:, :, 1:], f[:, 0, 2:3], c3[:, :, :-1],
                                                   ALU.mult, ALU.add).then_inc(tile_free, 1)
                            split(st)
                        else:
                            dve.wait_ge(gelu_done, FC * layer + k + 1 + 2 * i)
                            v.tensor_tensor(cv[:, k, tok], cv[:, k, tok], bank[m][:, tok], ALU.mult)\
                                .then_inc(tile_free, 1)
                            split(st)
                            dve.wait_ge(g_hi, FC * layer + k + 1 + 2 * i)
                            v.tensor_tensor(Glo[:, j, tok], cv[:, k, tok], Ghi[:, j, tok].bitcast(F32), ALU.subtract)\
                                .then_inc(g_ready, 1)
                    if per == 8:
                        ada_store(ADA_SLICES * (layer + 1) + 1 + i, layer + 1, 1 + i)
                projected(layer, p["down"], 3, 12, tok, last_layer)

            dve.sem_inc(tile_free, FREE0)
            for s, n in ((g_ready, 2), (rope_step, 1), (scored, SCORED0), (tap_done, TAP_FREE), (tap_pooled, 4),
                         (exped, 4), (p_copied, 2), (o_stored, 4), (p_turned, 2), (attended, 2)):
                dve.sem_inc(s, n)
            dve.wait_ge(c_ready, 3)
            v.tensor_tensor(cparts[:, :, 2:4], csilu[:, :, :], cparts[:, :, 0:2].bitcast(F32), ALU.subtract)\
                .then_inc(c_ready, 1)
            dve.wait_ge(first_loaded, 16 * len(FIRST_CONSTS))
            for s in range(4):
                dve.wait_ge(ada_rows_made, s + 1)
                v.tensor_copy(rows[0:2, :], bank[5 + s % 2][0:2, :]).then_inc(rows_copied, 1)
                ada_store(s, 0, s)
                if s == 2:
                    invert_root(0, ALL)
            dve.wait_ge(const_loaded, CONSTS_IN)
            v.tensor_scalar(qk_gain[:, :, 0:1], qk_gain[:, :, 0:1], NA_HD ** -0.5, None, ALU.mult)
            for n in range(LEAD):
                split(Step(n - LEAD))
            for layer, p in enumerate(layers):
                if layer % 3 == 2:
                    first = p["first_ada"]
                    split_group(Step(first + 3))
                    norm_apply(layer, 0, {
                        0: lambda: dve.sem_inc(lo_split, 4),
                        1: lambda: ada_store(ADA_SLICES * (layer + 1), layer + 1, 1),
                        4: lambda: split_group(Step(first + 8)), 6: lambda: split_group(Step(first + 9))})
                else:
                    norm_apply(layer, 0)
                if layer % 3 == 0:
                    na(layer, p)
                elif layer % 3 == 1:
                    retention(p)
                else:
                    conv(p)
                if layer < DEPTH - 1:
                    first = p["ada"]
                    split(Step(first))
                    norm_apply(layer, 1, {
                        0: lambda: split(Step(first + 1)), 1: lambda: ada_store(p["ada_index"], layer + 1, 0),
                        2: lambda: split(Step(first + 2)), 3: lambda: split(Step(first + 3))})
                else:
                    norm_apply(layer, 1)
                ffn(layer, p)


def _tile_groups(w):
    k, n = w.shape[0] // P, w.shape[1] // P
    return w.reshape(k, P, n, P).transpose(2, 1, 0, 3)


def _whole(w):
    return _tile_groups(w).reshape(-1, P, GROUP)


def _slices(w):
    n = w.shape[1] // 512
    return w.reshape(4, 2, P, n, 512).transpose(3, 0, 2, 1, 4).reshape(n, 4, P, GROUP)


def _with_slices(tiles, slices):
    out = np.empty((len(slices), 8, P, GROUP), tiles.dtype)
    out[:, list(TILE_AT)] = tiles.reshape(-1, 4, P, GROUP)
    out[:, list(ADA_AT)] = slices
    return out.reshape(-1, P, GROUP)


def _stream(a):
    ada = [_slices(a["ada_w"][layer]) for layer in range(DEPTH)]
    parts = []
    for layer in range(DEPTH):
        j = layer // 3
        if layer % 3 == 0:
            qkv = a["na_w_qkv"][j]
            qk = _whole(qkv[:, :2 * D])
            o = _whole(a["na_w_o"][j])
            if layer == 0:
                with_o = ada[0][8:12].reshape(C, 2, P, GROUP)
                qk = _with_slices(qk, ada[0][4:8])
                o = np.concatenate([with_o, o[:, None]], axis=1).reshape(-1, P, GROUP)
            parts += [qk, _slices(qkv[:, 2 * D:]).reshape(-1, P, GROUP), o]
        elif layer % 3 == 1:
            o = a["ret_w_o"][j].reshape(2, D, D)
            o = np.stack([_whole(o[0]), _whole(o[1])], axis=1).reshape(-1, P, GROUP)
            parts += [_whole(a["ret_w_q"][j]), _whole(a["ret_w_k"][j]),
                      _slices(a["ret_w_v"][j]).reshape(-1, P, GROUP), _whole(a["ret_w_g"][j]), o]
        else:
            pw = _whole(a["cv_w_pw1"][j]).reshape(2, C, P, GROUP).transpose(1, 0, 2, 3)
            pw = np.concatenate([ada[layer + 1][2:2 + C], pw], axis=1)
            parts += [ada[layer + 1][1], pw.reshape(-1, P, GROUP),
                      ada[layer + 1][2 + C:].reshape(-1, P, GROUP), _whole(a["cv_w_pw2"][j])]
        up = _whole(a["ffn_w_up"][layer]).reshape(2, FC, P, GROUP).transpose(1, 0, 2, 3).reshape(-1, P, GROUP)
        if layer < DEPTH - 1:
            parts.append(ada[layer + 1][0])
            if layer % 3 < 2:
                up = _with_slices(up, ada[layer + 1][1:])
        parts.append(up)
        down = _tile_groups(a["ffn_w_down"][layer])
        down = np.pad(down, ((0, 0), (0, 0), (0, 24 - FC), (0, 0)))
        parts.append(down.reshape(C, P, 3, GROUP).transpose(0, 2, 1, 3).reshape(-1, P, GROUP))
    return np.concatenate(parts)


def _per_feature(v):
    v = v.reshape(v.shape[:-1] + (-1, P))
    return np.moveaxis(v, -1, 0)


def _constants():
    col = np.arange(GRID_W)
    start = np.clip(col - NA_KW // 2, 0, GRID_W - NA_KW)
    inside = (col[None, :] >= start[:, None]) & (col[None, :] < start[:, None] + NA_KW)
    na_mask = np.tile(np.where(inside, 0.0, -FAR), (2, 1)).astype(np.float32)

    t = np.arange(SEQ)
    n_freq = RET_QK // 4
    inv = np.power(np.float32(10000.0), -np.arange(n_freq, dtype=np.float32) / np.float32(n_freq)).astype(np.float32)
    ang = np.concatenate([(t // GRID_W).astype(np.float32)[None, :] * inv[:, None],
                          (t % GRID_W).astype(np.float32)[None, :] * inv[:, None]])
    rope = np.stack([np.cos(ang), np.sin(ang)], axis=1).astype(np.float32)

    p, u = np.arange(P)[:, None], np.arange(DIST_W)[None, :]
    ahead, back = u - P - p, p + 3 * P - u
    dist = np.stack([np.where(ahead >= 0, ahead, FAR), np.where(back >= 0, back, FAR)], axis=1).astype(np.float32)

    head = np.arange(P) // NA_HD
    return {
        "na_mask": na_mask, "rope": rope, "dist": dist,
        "ones": np.ones((P, P), np.float32),
        "head_ones": (head[:, None] == head[None, :]).astype(np.float32),
        "identity": np.eye(P, dtype=np.float32),
        "pick": np.tile(np.eye(2, dtype=np.float32), (2, 1)),
    }


def kernel(**inputs):
    import concourse.bacc as bacc
    from concourse.bass_utils import run_bass_kernel_spmd

    a = {k: np.asarray(v) for k, v in inputs.items()}
    tokens = np.concatenate([a["ctx"][0], a["x"][0]])
    arrays = {
        "x": _per_feature(tokens).transpose(0, 2, 1),
        "ada_first": _slices(a["ada_w"][0][:, :2 * D]).reshape(-1, P, GROUP),
        "weights": _stream(a),
        "ada_in": _per_feature(np.stack([a["c_ctx"], a["c"][0]])).transpose(0, 2, 1),
        "ada_bias": _per_feature(a["ada_b"]),
        "gain": _per_feature(np.stack([a["norm_mix"], a["norm_ffn"]], axis=1)),
        "na_gain": np.tile(np.stack([a["na_q_gain"], a["na_k_gain"]], axis=1), (1, 1, 2)).transpose(2, 0, 1),
        "rpb": a["na_rpb"][..., ::-1],
        "decay": np.broadcast_to(a["ret_decay_logit"][0].reshape(1, -1), (P, 2 * RET_HEADS)),
        "gn_gain": _per_feature(a["ret_gn_gain"][0]),
        "cv_bias": _per_feature(np.stack([a["cv_b_pw1"][0, :D], a["cv_b_pw1"][0, D:], a["cv_b_dw"][0],
                                          a["cv_ln_g"][0], a["cv_ln_b"][0], a["cv_b_pw2"][0]])),
        "cv_filter": _per_feature(a["cv_w_dw"][0]).transpose(0, 2, 1),
        "ffn_filter": _per_feature(np.concatenate([a["ffn_w_dw"], a["ffn_b_dw"][:, None]], axis=1))
        .transpose(0, 1, 3, 2),
        **_constants(),
    }
    arrays = {k: np.ascontiguousarray(v) for k, v in arrays.items()}
    nc = bacc.Bacc("TRN2", target_bir_lowering=False, num_devices=1)
    aps = {k: nc.dram_tensor(f"in_{k}", v.shape, mybir.dt.from_np(v.dtype), kind="ExternalInput").ap()
           for k, v in arrays.items()}
    out = nc.dram_tensor("out_y", (P, C, SEQ), F32, kind="ExternalOutput").ap()
    build(nc, out=out, **aps)
    run = run_bass_kernel_spmd(nc, [{f"in_{k}": v for k, v in arrays.items()}], core_ids=[0])
    y = run.results[0]["out_y"]
    return np.ascontiguousarray(y.transpose(2, 1, 0)).reshape(1, SEQ, D)
```
